# Optimizing a Trainium2 kernel written in Bass

```python
import math
import jax, jax.numpy as jnp
from jax import lax
import numpy as np
import jax
import jax.numpy as jnp

D_MODEL = 1024
BATCH = 1
SEQ = 256
DEPTH = 2

GRID_W = 64
CTX_LEN = 256
N_MIXERS = 3
N_MOD = 9
D_FF = 2816
MACARON_W = 0.5
NORM_EPS = 1e-6
NEG_INF = -1e9

DA_HEADS = 8
DA_HEAD_DIM = 64
DA_Q_BLOCK = 128
ROPE_BASE = 10000.0
ROPE_PAIRS = DA_HEAD_DIM // 4

NA_HEADS = 16
NA_HEAD_DIM = D_MODEL // NA_HEADS
NA_ROWS = 8
NA_COLS = 16

RW_HEAD = 64
RW_HEADS = D_MODEL // RW_HEAD
RW_DECAY_LORA = 64
RW_AAA_LORA = 64
RW_GATE_LORA = 160
RW_LN_EPS = 64e-5


def _rmsnorm(h, g):
    hf = h.astype(jnp.float32)
    hf = hf * lax.rsqrt(jnp.mean(hf * hf, axis=-1, keepdims=True) + NORM_EPS)
    return hf.astype(h.dtype) * g

def _modulate(h, shift, scale):
    return h * (1 + scale) + shift

def _ffn_sublayer(h, mod, g_pre, g_post, w_in, w_out):
    shift, scale, gate = mod
    u = _modulate(_rmsnorm(h, g_pre), shift, scale)
    a, b = jnp.split(u @ w_in, 2, axis=-1)
    y = (jax.nn.silu(a) * b) @ w_out
    return h + MACARON_W * gate * _rmsnorm(y, g_post)

def _axial_rope_tables(seq_len):
    t = jnp.arange(seq_len)
    pos = jnp.stack([t // GRID_W, t % GRID_W], axis=-1).astype(jnp.float32)
    freq = ROPE_BASE ** (-jnp.arange(ROPE_PAIRS, dtype=jnp.float32) / ROPE_PAIRS)
    ang = pos[:, :, None] * freq
    return jnp.cos(ang), jnp.sin(ang)

def _axial_rope(x, cos, sin):
    d = x.shape[-1]
    xr = x.reshape(x.shape[:-1] + (2, 2, d // 4))
    x1, x2 = xr[..., 0, :], xr[..., 1, :]
    bshape = (cos.shape[0],) + (1,) * (x.ndim - 3) + (2, d // 4)
    c = cos.reshape(bshape).astype(x.dtype)
    s = sin.reshape(bshape).astype(x.dtype)
    return jnp.stack([x1 * c - x2 * s, x2 * c + x1 * s], axis=-2).reshape(x.shape)

def _attend(q, k, v):
    s = jnp.einsum('bthd,bkhd->bhtk', q, k).astype(jnp.float32)
    p = jax.nn.softmax(s, axis=-1).astype(v.dtype)
    return jnp.einsum('bhtk,bkhd->bthd', p, v)

def _diff_attend(q, k, v, lam):
    s = jnp.einsum('bthjd,bkhjd->bhjtk', q, k).astype(jnp.float32)
    p = jax.nn.softmax(s, axis=-1)
    p = p[:, :, 0] - lam.astype(jnp.float32) * p[:, :, 1]
    return jnp.einsum('bhtk,bkhe->bthe', p.astype(v.dtype), v)

def _diff_attention(uc, ux, w_in, w_out, lam_vec, subln_g, lam_init, cos, sin, need_ctx):
    B, S, D = ux.shape
    H, d = DA_HEADS, DA_HEAD_DIM

    def proj(u):
        L = u.shape[1]
        q, k, v = jnp.split(u @ w_in, 3, axis=-1)
        return (q.reshape(B, L, H, 2, d) * d ** -0.5, k.reshape(B, L, H, 2, d), v.reshape(B, L, H, 2 * d))

    qc, kc, vc = proj(uc)
    qx, kx, vx = proj(ux)
    qx = _axial_rope(qx, cos, sin)
    kx = _axial_rope(kx, cos, sin)
    lam = (jnp.exp(jnp.sum(lam_vec[0] * lam_vec[1])) - jnp.exp(jnp.sum(lam_vec[2] * lam_vec[3]))
           + lam_init)
    k_all = jnp.concatenate([kc, kx], axis=1)
    v_all = jnp.concatenate([vc, vx], axis=1)
    nb = S // DA_Q_BLOCK
    qb = jnp.moveaxis(qx.reshape(B, nb, DA_Q_BLOCK, H, 2, d), 1, 0)
    ox = lax.map(lambda q: _diff_attend(q, k_all, v_all, lam), qb)
    ox = jnp.moveaxis(ox, 0, 1).reshape(B, S, H, 2 * d)

    def out(o):
        o = _rmsnorm(o, subln_g) * (1 - lam_init)
        return o.reshape(o.shape[0], o.shape[1], H * 2 * d) @ w_out

    yx = out(ox)
    yc = out(_diff_attend(qc, kc, vc, lam)) if need_ctx else None
    return yc, yx

def _neighbourhood_attention(uc, ux, w_in, w_out, rpb, need_ctx):
    B, S, D = ux.shape
    C = uc.shape[1]
    H, d = NA_HEADS, NA_HEAD_DIM
    rows = S // GRID_W
    kr = min(NA_ROWS, rows)

    def proj(u):
        L = u.shape[1]
        q, k, v = jnp.split(u @ w_in, 3, axis=-1)
        return q.reshape(B, L, H, d) * d ** -0.5, k.reshape(B, L, H, d), v.reshape(B, L, H, d)

    qc, kc, vc = proj(uc)
    qx, kx, vx = proj(ux)
    q_grid = qx.reshape(B, rows, GRID_W, H, d)
    k_grid = kx.reshape(B, rows, GRID_W, H, d)
    v_grid = vx.reshape(B, rows, GRID_W, H, d)
    col = jnp.arange(GRID_W)
    col_start = jnp.clip(col - NA_COLS // 2, 0, GRID_W - NA_COLS)
    col_in = (col[None, :] >= col_start[:, None]) & (col[None, :] < col_start[:, None] + NA_COLS)
    col_off = jnp.clip(col[None, :] - col[:, None] + NA_COLS - 1, 0, 2 * NA_COLS - 2)
    col_bias = jnp.where(col_in, rpb[:, :, col_off].astype(jnp.float32), NEG_INF)

    def row_block(r):
        rs = jnp.clip(r - kr // 2, 0, rows - kr)
        q = lax.dynamic_index_in_dim(q_grid, r, axis=1, keepdims=False)
        kb = lax.dynamic_slice_in_dim(k_grid, rs, kr, axis=1)
        vb = lax.dynamic_slice_in_dim(v_grid, rs, kr, axis=1)
        bias = jnp.swapaxes(col_bias[:, rs + jnp.arange(kr) - r + NA_ROWS - 1], 1, 2)
        s_lat = jnp.einsum('bqhd,brkhd->bhqrk', q, kb).astype(jnp.float32) + bias
        s_ctx = jnp.einsum('bqhd,bchd->bhqc', q, kc).astype(jnp.float32)
        s = jnp.concatenate([s_ctx, s_lat.reshape(B, H, GRID_W, kr * GRID_W)], axis=-1)
        p = jax.nn.softmax(s, axis=-1).astype(vx.dtype)
        p_ctx = p[..., :C]
        p_lat = p[..., C:].reshape(B, H, GRID_W, kr, GRID_W)
        return (jnp.einsum('bhqc,bchd->bqhd', p_ctx, vc)
                + jnp.einsum('bhqrk,brkhd->bqhd', p_lat, vb))

    ox = lax.map(row_block, jnp.arange(rows))
    yx = jnp.moveaxis(ox, 0, 1).reshape(B, S, D) @ w_out
    yc = _attend(qc, kc, vc).reshape(B, C, D) @ w_out if need_ctx else None
    return yc, yx

def _rwkv7_prep(u, mu, w_in, w0, w1, w2, a0, a1, a2, g1, g2, k_k, k_a):
    B, L, D = u.shape
    H, N = RW_HEADS, RW_HEAD
    f32 = jnp.float32
    zero = jnp.zeros_like(u[:, :1])
    xx = 0.5 * (jnp.concatenate([zero, u[:, :-1]], axis=1) + jnp.concatenate([u[:, 1:], zero], axis=1)) - u
    xr, xw, xk, xv, xa, xg = [u + xx * mu[j] for j in range(6)]
    w_r, w_k, w_v = jnp.split(w_in, 3, axis=1)
    r = xr @ w_r
    k = xk @ w_k
    v = xv @ w_v
    lora_w = jnp.einsum('zblr,zrd->zbld', jnp.tanh(jnp.einsum('bld,zdr->zblr', xw, w1)), w2)
    w_log = -jax.nn.softplus(-(w0[:, None, None, :] + lora_w).astype(f32)) - 0.5
    decay = jnp.exp(-jnp.exp(w_log))
    a = jax.nn.sigmoid(a0[:, None, None, :]
                       + jnp.einsum('zblr,zrd->zbld', jnp.einsum('bld,zdr->zblr', xa, a1), a2))
    g = jax.nn.sigmoid(xg @ g1) @ g2
    kk = (k * k_k).reshape(B, L, H, N).astype(f32)
    kk = kk / jnp.maximum(jnp.linalg.norm(kk, axis=-1, keepdims=True), 1e-12)
    kd = k[None] * (1 + (a - 1) * k_a)

    def heads(t):
        return t.reshape(t.shape[:-1] + (H, N)).astype(f32)

    def two(t):
        return jnp.broadcast_to(t, (2,) + t.shape)

    def orient(t):
        t = jnp.stack([t[0], jnp.flip(t[1], axis=1)])
        return jnp.moveaxis(t, 2, 0)

    scan_in = (orient(two(heads(r))), orient(heads(decay)), orient(heads(kd)),
               orient(two(heads(v))), orient(two(-kk)), orient(kk[None] * heads(a)))
    return scan_in, (r, kd, v, g)

def _wkv7_scan(state0, r, w, k, v, a, b):
    def step(S, inp):
        rt, wt, kt, vt, at, bt = inp
        sa = jnp.einsum('zbhvk,zbhk->zbhv', S, at)
        S = S * wt[..., None, :] + sa[..., :, None] * bt[..., None, :] + vt[..., :, None] * kt[..., None, :]
        return S, jnp.einsum('zbhvk,zbhk->zbhv', S, rt)
    return lax.scan(step, state0, (r, w, k, v, a, b))

def _rwkv7_readout(y, r, kd, v, g, r_k, ln_g, ln_b, w_out):
    B, L, D = r.shape
    H, N = RW_HEADS, RW_HEAD
    y = jnp.moveaxis(y, 0, 2)
    y = y[0] + jnp.flip(y[1], axis=1)
    mean = jnp.mean(y, axis=-1, keepdims=True)
    var = jnp.mean(jnp.square(y - mean), axis=-1, keepdims=True)
    y = ((y - mean) * lax.rsqrt(var + RW_LN_EPS)).reshape(B, L, D).astype(r.dtype) * ln_g + ln_b
    rh = r.reshape(B, L, H, N)
    kh = (kd[0] + kd[1]).reshape(B, L, H, N)
    bonus = jnp.sum(rh * kh * r_k, axis=-1, keepdims=True) * v.reshape(B, L, H, N)
    return ((y + bonus.reshape(B, L, D)) * g) @ w_out

def _rwkv7_mixer(uc, ux, mu, w_in, w_out, w0, w1, w2, a0, a1, a2, g1, g2, k_k, k_a, r_k,
                 ln_g, ln_b, need_ctx):
    B = ux.shape[0]
    in_c, aux_c = _rwkv7_prep(uc, mu, w_in, w0, w1, w2, a0, a1, a2, g1, g2, k_k, k_a)
    in_x, aux_x = _rwkv7_prep(ux, mu, w_in, w0, w1, w2, a0, a1, a2, g1, g2, k_k, k_a)
    s0 = jnp.zeros((2, B, RW_HEADS, RW_HEAD, RW_HEAD), jnp.float32)
    s_ctx, y_c = _wkv7_scan(s0, *in_c)
    _, y_x = _wkv7_scan(s_ctx, *in_x)
    yx = _rwkv7_readout(y_x, *aux_x, r_k, ln_g, ln_b, w_out)
    yc = _rwkv7_readout(y_c, *aux_c, r_k, ln_g, ln_b, w_out) if need_ctx else None
    return yc, yx

def first_inputs(seed: int = 0) -> dict:
    key = jax.random.key(seed)
    ks = iter(jax.random.split(key, 48))
    f32 = jnp.float32
    D, F = D_MODEL, D_FF
    n_a, n_b, n_c = [len(range(m, DEPTH, N_MIXERS)) for m in range(N_MIXERS)]

    def nrm(shape, scale):
        return jax.random.normal(next(ks), shape, f32) * scale

    def gain(shape):
        return 1.0 + nrm(shape, 0.05)

    return {
        'x': nrm((BATCH, SEQ, D), 1.0),
        'c': nrm((BATCH, D), 1.0),
        'ctx': nrm((BATCH, CTX_LEN, D), 1.0),
        'c_ctx': nrm((D,), 1.0),
        'ada_w': nrm((DEPTH, D, N_MOD * D), 0.5 * D ** -0.5),
        'ada_b': nrm((DEPTH, N_MOD * D), 0.02),
        'norm_g': gain((DEPTH, 6, D)),
        'ffn_w_in': nrm((DEPTH, 2, D, 2 * F), D ** -0.5),
        'ffn_w_out': nrm((DEPTH, 2, F, D), F ** -0.5),
        'da_w_in': nrm((n_a, D, 3 * D), D ** -0.5),
        'da_w_out': nrm((n_a, D, D), D ** -0.5),
        'da_lambda': nrm((n_a, 4, DA_HEAD_DIM), 0.1),
        'da_subln_g': gain((n_a, 2 * DA_HEAD_DIM)),
        'na_w_in': nrm((n_b, D, 3 * D), D ** -0.5),
        'na_w_out': nrm((n_b, D, D), D ** -0.5),
        'na_rpb': nrm((n_b, NA_HEADS, 2 * NA_ROWS - 1, 2 * NA_COLS - 1), 0.2),
        'rw_mu': jax.random.uniform(next(ks), (n_c, 6, D), f32),
        'rw_w_in': nrm((n_c, D, 3 * D), D ** -0.5),
        'rw_w_out': nrm((n_c, D, D), D ** -0.5),
        'rw_w0': jax.random.uniform(next(ks), (n_c, 2, D), f32, -6.0, -1.0),
        'rw_w1': nrm((n_c, 2, D, RW_DECAY_LORA), D ** -0.5),
        'rw_w2': nrm((n_c, 2, RW_DECAY_LORA, D), 0.1 * RW_DECAY_LORA ** -0.5),
        'rw_a0': nrm((n_c, 2, D), 0.1),
        'rw_a1': nrm((n_c, 2, D, RW_AAA_LORA), D ** -0.5),
        'rw_a2': nrm((n_c, 2, RW_AAA_LORA, D), RW_AAA_LORA ** -0.5),
        'rw_g1': nrm((n_c, D, RW_GATE_LORA), D ** -0.5),
        'rw_g2': nrm((n_c, RW_GATE_LORA, D), RW_GATE_LORA ** -0.5),
        'rw_k_k': 0.85 + nrm((n_c, D), 0.05),
        'rw_k_a': gain((n_c, D)),
        'rw_r_k': nrm((n_c, RW_HEADS, RW_HEAD), 0.1),
        'rw_ln_g': gain((n_c, D)),
        'rw_ln_b': nrm((n_c, D), 0.02),
    }

def first_block(x, c, ctx, c_ctx, ada_w, ada_b, norm_g, ffn_w_in, ffn_w_out,
              da_w_in, da_w_out, da_lambda, da_subln_g,
              na_w_in, na_w_out, na_rpb,
              rw_mu, rw_w_in, rw_w_out, rw_w0, rw_w1, rw_w2, rw_a0, rw_a1, rw_a2,
              rw_g1, rw_g2, rw_k_k, rw_k_a, rw_r_k, rw_ln_g, rw_ln_b):
    B, S, D = x.shape
    cos, sin = _axial_rope_tables(S)
    hx, hc = x, ctx
    silu_c, silu_cc = jax.nn.silu(c), jax.nn.silu(c_ctx)
    for i in range(DEPTH):
        last = i == DEPTH - 1
        kind, slot = i % N_MIXERS, i // N_MIXERS
        g = norm_g[i]
        mx = (silu_c @ ada_w[i] + ada_b[i]).reshape(B, N_MOD, 1, D)
        mc = (silu_cc @ ada_w[i] + ada_b[i]).reshape(N_MOD, D)

        hx = _ffn_sublayer(hx, (mx[:, 0], mx[:, 1], mx[:, 2]), g[0], g[1], ffn_w_in[i, 0], ffn_w_out[i, 0])
        hc = _ffn_sublayer(hc, (mc[0], mc[1], mc[2]), g[0], g[1], ffn_w_in[i, 0], ffn_w_out[i, 0])

        ux = _modulate(_rmsnorm(hx, g[2]), mx[:, 3], mx[:, 4])
        uc = _modulate(_rmsnorm(hc, g[2]), mc[3], mc[4])
        if kind == 0:
            lam_init = 0.8 - 0.6 * math.exp(-0.3 * i)
            yc, yx = _diff_attention(uc, ux, da_w_in[slot], da_w_out[slot], da_lambda[slot],
                                     da_subln_g[slot], lam_init, cos, sin, not last)
        elif kind == 1:
            yc, yx = _neighbourhood_attention(uc, ux, na_w_in[slot], na_w_out[slot], na_rpb[slot], not last)
        else:
            yc, yx = _rwkv7_mixer(uc, ux, rw_mu[slot], rw_w_in[slot], rw_w_out[slot],
                                  rw_w0[slot], rw_w1[slot], rw_w2[slot],
                                  rw_a0[slot], rw_a1[slot], rw_a2[slot],
                                  rw_g1[slot], rw_g2[slot], rw_k_k[slot], rw_k_a[slot],
                                  rw_r_k[slot], rw_ln_g[slot], rw_ln_b[slot], not last)
        hx = hx + mx[:, 5] * _rmsnorm(yx, g[3])

        hx = _ffn_sublayer(hx, (mx[:, 6], mx[:, 7], mx[:, 8]), g[4], g[5], ffn_w_in[i, 1], ffn_w_out[i, 1])
        if not last:
            hc = hc + mc[5] * _rmsnorm(yc, g[3])
            hc = _ffn_sublayer(hc, (mc[6], mc[7], mc[8]), g[4], g[5], ffn_w_in[i, 1], ffn_w_out[i, 1])
    return hx


HEAD_DIM = 64
N_EVEN = (DEPTH + 1) // 2
N_ODD = DEPTH // 2
D_FF_2 = ((8 * D_MODEL // 3 + 255) // 256) * 256

POOL_WINDOWS = (2, 4, 8, 16)
POOL_GROUPS = len(POOL_WINDOWS)
POOL_WIDTH = D_MODEL // 4
POOL_GC = POOL_WIDTH // POOL_GROUPS

ATTN_Q_HEADS = (3 * D_MODEL // 4) // HEAD_DIM
ATTN_KV_HEADS = ATTN_Q_HEADS // 3
GQA_GROUP = ATTN_Q_HEADS // ATTN_KV_HEADS
WINDOW = 128
ATTN_BLOCK = 128
ROPE_THETA = 10000.0
EVEN_IN = POOL_WIDTH + (ATTN_Q_HEADS + 2 * ATTN_KV_HEADS) * HEAD_DIM
EVEN_MIX = POOL_WIDTH + ATTN_Q_HEADS * HEAD_DIM

CONV_CH = D_MODEL // 2
CONV_K = 31

SSM_INNER = D_MODEL
SSM_HEAD_DIM = 64
SSM_HEADS = SSM_INNER // SSM_HEAD_DIM
SSM_GROUPS = 4
SSM_STATE = 128
SSM_CONV = 4
SSM_CHUNK = 128
SSM_XBC = SSM_INNER + 2 * SSM_GROUPS * SSM_STATE
ODD_IN = 2 * CONV_CH + SSM_INNER + SSM_XBC + 2 * SSM_HEADS
ODD_MIX = CONV_CH + SSM_INNER


def rms_norm(x, w):
    xf = x.astype(jnp.float32)
    y = xf * lax.rsqrt(jnp.mean(xf * xf, axis=-1, keepdims=True) + NORM_EPS)
    return (y * w.astype(jnp.float32)).astype(x.dtype)

def layer_norm(x, g, b):
    xf = x.astype(jnp.float32)
    mu = jnp.mean(xf, axis=-1, keepdims=True)
    xc = xf - mu
    y = xc * lax.rsqrt(jnp.mean(xc * xc, axis=-1, keepdims=True) + NORM_EPS)
    return (y * g.astype(jnp.float32) + b.astype(jnp.float32)).astype(x.dtype)

def swiglu(h, w_gate, w_up, w_down):
    return (jax.nn.silu(h @ w_gate) * (h @ w_up)) @ w_down

def depthwise_conv(x, w, b, pad_left, pad_right):
    y = lax.conv_general_dilated(
        x, w[:, None, :].astype(x.dtype), window_strides=(1,),
        padding=[(pad_left, pad_right)],
        dimension_numbers=('NWC', 'WIO', 'NWC'),
        feature_group_count=x.shape[-1])
    return y + b.astype(x.dtype)

def rope_tables(seq_len):
    inv = 1.0 / (ROPE_THETA ** (jnp.arange(0, HEAD_DIM, 2, dtype=jnp.float32) / HEAD_DIM))
    ang = jnp.arange(seq_len, dtype=jnp.float32)[:, None] * inv[None, :]
    return jnp.cos(ang), jnp.sin(ang)

def apply_rope(t, cos, sin):
    tf = t.astype(jnp.float32)
    t1, t2 = tf[..., :HEAD_DIM // 2], tf[..., HEAD_DIM // 2:]
    c, s = cos[None, :, None, :], sin[None, :, None, :]
    return jnp.concatenate([t1 * c - t2 * s, t2 * c + t1 * s], axis=-1).astype(t.dtype)

def multiscale_pool(u, w_grp, scale):
    b, S, C = u.shape
    uf = u.astype(jnp.float32)
    cs = jnp.concatenate([jnp.zeros((b, 1, C), jnp.float32), jnp.cumsum(uf, axis=1)], axis=1)
    t = jnp.arange(S)
    outs = []
    for g, w in enumerate(POOL_WINDOWS):
        lo = jnp.clip(t - w // 2, 0, S)
        hi = jnp.clip(t + w - w // 2, 0, S)
        csg = cs[..., g * POOL_GC:(g + 1) * POOL_GC]
        cnt = (hi - lo).astype(jnp.float32)[None, :, None]
        mean = (jnp.take(csg, hi, axis=1) - jnp.take(csg, lo, axis=1)) / cnt
        outs.append(mean - uf[..., g * POOL_GC:(g + 1) * POOL_GC])
    p = jnp.stack(outs, axis=2).astype(u.dtype)
    y = jnp.einsum('bsgc,gcd->bsgd', p, w_grp).reshape(b, S, C)
    return y * scale

def windowed_gqa(q, k, v, sink):
    b, S = q.shape[0], q.shape[1]
    nb = S // ATTN_BLOCK
    qb = q.reshape(b, nb, ATTN_BLOCK, ATTN_KV_HEADS, GQA_GROUP, HEAD_DIM)

    def band(t):
        tp = jnp.pad(t, ((0, 0), (ATTN_BLOCK, ATTN_BLOCK), (0, 0), (0, 0)))
        tp = tp.reshape(b, nb + 2, ATTN_BLOCK, ATTN_KV_HEADS, HEAD_DIM)
        return jnp.concatenate([tp[:, :-2], tp[:, 1:-1], tp[:, 2:]], axis=2)

    kw, vw = band(k), band(v)
    s = jnp.einsum('bnqhgd,bnkhd->bnhgqk', qb, kw).astype(jnp.float32) * (HEAD_DIM ** -0.5)
    blk = jnp.arange(nb)[:, None, None] * ATTN_BLOCK
    qpos = blk + jnp.arange(ATTN_BLOCK)[None, :, None]
    kpos = blk - ATTN_BLOCK + jnp.arange(3 * ATTN_BLOCK)[None, None, :]
    valid = (jnp.abs(qpos - kpos) <= WINDOW) & (kpos >= 0) & (kpos < S)
    s = jnp.where(valid[None, :, None, None], s, -jnp.inf)
    sk = sink.astype(jnp.float32).reshape(ATTN_KV_HEADS, GQA_GROUP)[None, None, :, :, None, None]
    m = jnp.maximum(jnp.max(s, axis=-1, keepdims=True), sk)
    p = jnp.exp(s - m)
    denom = jnp.sum(p, axis=-1, keepdims=True) + jnp.exp(sk - m)
    o = jnp.einsum('bnhgqk,bnkhd->bnqhgd', (p / denom).astype(v.dtype), vw)
    return o.reshape(b, S, ATTN_Q_HEADS * HEAD_DIM)

def ssd_scan(x, dt, A, Bm, Cm):
    b, L, H, P = x.shape
    G, N = Bm.shape[2], Bm.shape[3]
    Hg = H // G
    c = L // SSM_CHUNK
    X = (x * dt[..., None]).reshape(b, c, SSM_CHUNK, G, Hg, P)
    a = jnp.moveaxis((dt * A).reshape(b, c, SSM_CHUNK, G, Hg), 2, -1)
    a_cs = jnp.cumsum(a, axis=-1)
    Bc = Bm.reshape(b, c, SSM_CHUNK, G, N)
    Cc = Cm.reshape(b, c, SSM_CHUNK, G, N)
    lower = jnp.tril(jnp.ones((SSM_CHUNK, SSM_CHUNK), bool))
    seg = a_cs[..., :, None] - a_cs[..., None, :]
    Lmat = jnp.exp(jnp.where(lower, seg, -jnp.inf))
    CB = jnp.einsum('bclgn,bcsgn->bcgls', Cc, Bc)
    y_diag = jnp.einsum('bcghls,bcsghp->bclghp', CB[:, :, :, None] * Lmat, X)
    decay_s = jnp.exp(a_cs[..., -1:] - a_cs)
    states = jnp.einsum('bclgn,bcghl,bclghp->bcghpn', Bc, decay_s, X)
    chunk_decay = jnp.exp(a_cs[..., -1])

    def step(h, inp):
        st, d = inp
        return h * d[..., None, None] + st, h

    h0 = jnp.zeros((b, G, Hg, P, N), jnp.float32)
    _, prev = lax.scan(step, h0, (jnp.moveaxis(states, 1, 0), jnp.moveaxis(chunk_decay, 1, 0)))
    prev = jnp.moveaxis(prev, 0, 1)
    y_off = jnp.einsum('bclgn,bcghpn,bcghl->bclghp', Cc, prev, jnp.exp(a_cs))
    return (y_diag + y_off).reshape(b, L, H, P)

def even_mixer(h, w_in, pool_w, pool_scale, sink, w_out, cos, sin):
    b, S, _ = h.shape
    proj = h @ w_in
    qw, kw = ATTN_Q_HEADS * HEAD_DIM, ATTN_KV_HEADS * HEAD_DIM
    o = POOL_WIDTH
    u = proj[..., :o]
    q = proj[..., o:o + qw].reshape(b, S, ATTN_Q_HEADS, HEAD_DIM)
    k = proj[..., o + qw:o + qw + kw].reshape(b, S, ATTN_KV_HEADS, HEAD_DIM)
    v = proj[..., o + qw + kw:o + qw + 2 * kw].reshape(b, S, ATTN_KV_HEADS, HEAD_DIM)
    q = apply_rope(q, cos, sin)
    k = apply_rope(k, cos, sin)
    pool_out = multiscale_pool(u, pool_w, pool_scale)
    attn_out = windowed_gqa(q, k, v, sink)
    return jnp.concatenate([pool_out, attn_out], axis=-1) @ w_out

def odd_mixer(h, w_in, dw_w, dw_b, ln_g, ln_b, conv_w, conv_b, A_log, dt_bias, D_skip, norm_w, w_out):
    b, S, _ = h.shape
    proj = h @ w_in
    glu_a = proj[..., :CONV_CH]
    glu_b = proj[..., CONV_CH:2 * CONV_CH]
    o = 2 * CONV_CH
    z = proj[..., o:o + SSM_INNER]
    o += SSM_INNER
    xbc = proj[..., o:o + SSM_XBC]
    o += SSM_XBC
    dt_raw = proj[..., o:o + 2 * SSM_HEADS].reshape(b, S, 2, SSM_HEADS)
    g = glu_a * jax.nn.sigmoid(glu_b)
    g = depthwise_conv(g, dw_w, dw_b, CONV_K // 2, CONV_K // 2)
    g = jax.nn.silu(layer_norm(g, ln_g, ln_b))
    xbc = jax.nn.silu(depthwise_conv(xbc, conv_w, conv_b, SSM_CONV // 2, SSM_CONV - 1 - SSM_CONV // 2))
    gn = SSM_GROUPS * SSM_STATE
    xs = xbc[..., :SSM_INNER].reshape(b, S, SSM_HEADS, SSM_HEAD_DIM).astype(jnp.float32)
    Bm = xbc[..., SSM_INNER:SSM_INNER + gn].reshape(b, S, SSM_GROUPS, SSM_STATE).astype(jnp.float32)
    Cm = xbc[..., SSM_INNER + gn:].reshape(b, S, SSM_GROUPS, SSM_STATE).astype(jnp.float32)
    dt = jax.nn.softplus(dt_raw.astype(jnp.float32) + dt_bias.astype(jnp.float32))
    A = -jnp.exp(A_log.astype(jnp.float32))
    flip = lambda t: jnp.flip(t, axis=1)
    y_f = ssd_scan(xs, dt[:, :, 0], A[0], Bm, Cm)
    y_b = flip(ssd_scan(flip(xs), flip(dt[:, :, 1]), A[1], flip(Bm), flip(Cm)))
    y = (y_f + y_b + xs * D_skip.astype(jnp.float32)[:, None]).reshape(b, S, SSM_INNER)
    y = rms_norm(y * jax.nn.silu(z.astype(jnp.float32)), norm_w).astype(h.dtype)
    return jnp.concatenate([g, y], axis=-1) @ w_out

def second_inputs(seed: int = 0) -> dict:
    key = jax.random.key(seed)
    ks = jax.random.split(key, 24)
    f32 = jnp.float32

    def nrm(k, shape, fan_in):
        return jax.random.normal(k, shape, f32) * (fan_in ** -0.5)

    def near_one(k, shape, s):
        return 1.0 + s * jax.random.normal(k, shape, f32)

    dt0 = jnp.exp(jax.random.uniform(ks[20], (N_ODD, 2, SSM_HEADS), f32,
                                     minval=math.log(1e-3), maxval=math.log(1e-1)))
    return {
        'x': jax.random.normal(ks[0], (BATCH, SEQ, D_MODEL), f32),
        'norm_w': near_one(ks[1], (DEPTH, 6, D_MODEL), 0.05),
        'ffn_w_gate': nrm(ks[2], (DEPTH, 2, D_MODEL, D_FF_2), D_MODEL),
        'ffn_w_up': nrm(ks[3], (DEPTH, 2, D_MODEL, D_FF_2), D_MODEL),
        'ffn_w_down': nrm(ks[4], (DEPTH, 2, D_FF_2, D_MODEL), D_FF_2),
        'ev_w_in': nrm(ks[5], (N_EVEN, D_MODEL, EVEN_IN), D_MODEL),
        'ev_pool_w': nrm(ks[6], (N_EVEN, POOL_GROUPS, POOL_GC, POOL_GC), POOL_GC),
        'ev_pool_scale': near_one(ks[7], (N_EVEN, POOL_WIDTH), 0.1),
        'ev_sink': 0.5 * jax.random.normal(ks[8], (N_EVEN, ATTN_Q_HEADS), f32),
        'ev_w_out': nrm(ks[9], (N_EVEN, EVEN_MIX, D_MODEL), EVEN_MIX),
        'od_w_in': nrm(ks[10], (N_ODD, D_MODEL, ODD_IN), D_MODEL),
        'cv_dw_w': nrm(ks[11], (N_ODD, CONV_K, CONV_CH), CONV_K),
        'cv_dw_b': 0.02 * jax.random.normal(ks[12], (N_ODD, CONV_CH), f32),
        'cv_ln_g': near_one(ks[13], (N_ODD, CONV_CH), 0.05),
        'cv_ln_b': 0.02 * jax.random.normal(ks[14], (N_ODD, CONV_CH), f32),
        'ssm_conv_w': nrm(ks[15], (N_ODD, SSM_CONV, SSM_XBC), SSM_CONV),
        'ssm_conv_b': 0.02 * jax.random.normal(ks[16], (N_ODD, SSM_XBC), f32),
        'ssm_A_log': jnp.log(jax.random.uniform(ks[17], (N_ODD, 2, SSM_HEADS), f32, minval=1.0, maxval=16.0)),
        'ssm_dt_bias': dt0 + jnp.log(-jnp.expm1(-dt0)),
        'ssm_D': near_one(ks[18], (N_ODD, SSM_HEADS), 0.1),
        'ssm_norm_w': near_one(ks[19], (N_ODD, SSM_INNER), 0.05),
        'od_w_out': nrm(ks[21], (N_ODD, ODD_MIX, D_MODEL), ODD_MIX),
    }

def second_block(x, norm_w, ffn_w_gate, ffn_w_up, ffn_w_down,
              ev_w_in, ev_pool_w, ev_pool_scale, ev_sink, ev_w_out,
              od_w_in, cv_dw_w, cv_dw_b, cv_ln_g, cv_ln_b,
              ssm_conv_w, ssm_conv_b, ssm_A_log, ssm_dt_bias, ssm_D, ssm_norm_w, od_w_out):
    cos, sin = rope_tables(x.shape[1])
    for l in range(DEPTH):
        nw = norm_w[l]
        x = x + 0.5 * rms_norm(swiglu(rms_norm(x, nw[0]), ffn_w_gate[l, 0], ffn_w_up[l, 0], ffn_w_down[l, 0]), nw[1])
        hn = rms_norm(x, nw[2])
        i = l // 2
        if l % 2 == 0:
            m = even_mixer(hn, ev_w_in[i], ev_pool_w[i], ev_pool_scale[i], ev_sink[i], ev_w_out[i], cos, sin)
        else:
            m = odd_mixer(hn, od_w_in[i], cv_dw_w[i], cv_dw_b[i], cv_ln_g[i], cv_ln_b[i],
                          ssm_conv_w[i], ssm_conv_b[i], ssm_A_log[i], ssm_dt_bias[i], ssm_D[i],
                          ssm_norm_w[i], od_w_out[i])
        x = x + rms_norm(m, nw[3])
        x = x + 0.5 * rms_norm(swiglu(rms_norm(x, nw[4]), ffn_w_gate[l, 1], ffn_w_up[l, 1], ffn_w_down[l, 1]), nw[5])
    return x


def setup_inputs(seed=0):
    out = dict(first_inputs(seed))
    for name, value in second_inputs(seed + 1).items():
        if name != "x":
            out[name + "_2"] = value
    return out


def reference(
    x, c, ctx, c_ctx, ada_w, ada_b, norm_g, ffn_w_in, ffn_w_out, da_w_in, da_w_out, da_lambda,
    da_subln_g, na_w_in, na_w_out, na_rpb, rw_mu, rw_w_in, rw_w_out, rw_w0, rw_w1, rw_w2, rw_a0,
    rw_a1, rw_a2, rw_g1, rw_g2, rw_k_k, rw_k_a, rw_r_k, rw_ln_g, rw_ln_b, norm_w_2,
    ffn_w_gate_2, ffn_w_up_2, ffn_w_down_2, ev_w_in_2, ev_pool_w_2, ev_pool_scale_2, ev_sink_2,
    ev_w_out_2, od_w_in_2, cv_dw_w_2, cv_dw_b_2, cv_ln_g_2, cv_ln_b_2, ssm_conv_w_2,
    ssm_conv_b_2, ssm_A_log_2, ssm_dt_bias_2, ssm_D_2, ssm_norm_w_2, od_w_out_2,
):
    x = first_block(
        x, c, ctx, c_ctx, ada_w, ada_b, norm_g, ffn_w_in, ffn_w_out, da_w_in, da_w_out,
        da_lambda, da_subln_g, na_w_in, na_w_out, na_rpb, rw_mu, rw_w_in, rw_w_out, rw_w0,
        rw_w1, rw_w2, rw_a0, rw_a1, rw_a2, rw_g1, rw_g2, rw_k_k, rw_k_a, rw_r_k, rw_ln_g,
        rw_ln_b,
    )
    return second_block(
        x, norm_w_2, ffn_w_gate_2, ffn_w_up_2, ffn_w_down_2, ev_w_in_2, ev_pool_w_2,
        ev_pool_scale_2, ev_sink_2, ev_w_out_2, od_w_in_2, cv_dw_w_2, cv_dw_b_2, cv_ln_g_2,
        cv_ln_b_2, ssm_conv_w_2, ssm_conv_b_2, ssm_A_log_2, ssm_dt_bias_2, ssm_D_2,
        ssm_norm_w_2, od_w_out_2,
    )


_drawn_inputs = setup_inputs


def setup_inputs(seed=0):
    import zlib

    import numpy as np

    out = dict(_drawn_inputs(seed))
    spreads = {}
    factors = {'na_rpb': 4.749,
     'ev_sink_2': 8.0,
     'cv_dw_b_2': 7.066,
     'cv_ln_g_2': 4.908,
     'cv_ln_b_2': 28.35,
     'ssm_conv_b_2': 3.985,
     'ssm_D_2': 6.189,
     'ssm_norm_w_2': 5.143}
    for name, (base, spread) in spreads.items():
        noise = np.random.default_rng([zlib.crc32(name.encode()), seed]).standard_normal(out[name].shape)
        drawn = base * np.exp(spread * noise) if base else spread * noise
        out[name] = jnp.asarray(drawn.astype(out[name].dtype))
    for name, factor in factors.items():
        out[name] = (out[name] * factor).astype(out[name].dtype)
    return out
```

```python
from contextlib import ExitStack

import numpy as np

import concourse.bass as bass
from concourse import mybir

F32 = mybir.dt.float32
F32R = mybir.dt.float32r
ACT = mybir.ActivationFunctionType
ALU = mybir.AluOpType
AX_X = mybir.AxisListType.X

P = 128
D = 1024
KT = D // P
SEQ = 256
CTX = 256
BOTH = SEQ + CTX
DFF = 2816
FT = DFF // P
HALF_FT = FT // 2
EPS = 1e-6
HD = 64
CHUNK = 2 * P
CHUNK_COLS = KT * CHUNK
OUT_COLS = HALF_FT * P
N_MOD = 9
GRID_W = 64
NA_H, NA_WIN = 16, 16
EV_QH = 12
CONV_K = 31
SSM_H, SSM_G = 16, 4
XBC = 2048
NEG = -1e9
FAR = -1e30
RAW_RING, PART_RING = 4, 2
DVE_ADDS = [2, 5, 7]
EV_HEADS = [0, 3, 1, 4, 2, 5, 6, 9, 7, 10, 8, 11]


def param_columns():
    sizes = [("silu_in", KT * 2), ("gain", 12 * KT * 2), ("gain2", 12 * KT), ("ada_b", 2 * N_MOD * KT * 2),
             ("lam", 4 * HD), ("subln", 1), ("sink", EV_QH), ("pool_scale", 2), ("dw_w", 4 * CONV_K),
             ("dw_b", 4), ("ln_g", 4), ("ln_b", 4), ("cw", 16 * 4), ("cb", 16), ("a_log", 2 * SSM_H),
             ("dt_bias", 2 * SSM_H), ("skip", KT), ("ssm_norm", KT)]
    at, out = 0, {}
    for name, n in sizes:
        out[name] = (at, n)
        at += n
    return out, at


def weight_plan():
    plan = []

    def ada(layer, m):
        plan.append((f"ada{layer}_{m}", "w_ada", (layer * N_MOD + m) * 4, 4, CHUNK_COLS))

    def ffn(s):
        n = s // 3 * 2 + (s % 3 == 2)
        plan.append((f"in{s}", "w_ffn_in", n * FT, FT, CHUNK_COLS))
        plan.append((f"out{s}", "w_ffn_out", n * 2 * KT, 2 * KT, OUT_COLS))

    for m in (0, 1, 2):
        ada(0, m)
    ffn(0)
    for m in (3, 4):
        ada(0, m)
    plan.append(("in1", "w_mix", 0, 12, CHUNK_COLS))
    for m in (5, 6, 7, 8):
        ada(0, m)
    plan.append(("out1", "w_mix", 12, 4, CHUNK_COLS))
    for m in (0, 1):
        ada(1, m)
    ffn(2)
    for m in (2, 3):
        ada(1, m)
    ffn(3)
    for m in (4, 5):
        ada(1, m)
    plan.append(("in4", "w_mix", 16, 12, CHUNK_COLS))
    for m in (6, 7, 8):
        ada(1, m)
    plan.append(("out4", "w_mix", 28, 4, CHUNK_COLS))
    ffn(5)
    ffn(6)
    plan.append(("in7", "w_mix", 32, 6, CHUNK_COLS))
    plan.append(("out7", "w_mix", 38, 4, CHUNK_COLS))
    ffn(8)
    ffn(9)
    plan.append(("in10", "w_mix", 42, 4, CHUNK_COLS))
    plan.append(("dt10", "w_dt", 0, 1, KT * 2 * SSM_H))
    plan.append(("in10b", "w_mix", 46, 12, CHUNK_COLS))
    plan.append(("out10", "w_od_out", 0, KT, 12 * P))
    ffn(11)
    return plan


def at(base, step, i):
    return base if i is None else i * step + base


def build_program(nc, t, out):
    plan = weight_plan()
    chunk_cols, first_chunk = [], {}
    for name, _, _, n, cols in plan:
        first_chunk[name] = len(chunk_cols)
        chunk_cols += [cols] * n
    parted = [g for name, _, _, n, _ in plan if not name.startswith("ada")
              for g in range(first_chunk[name], first_chunk[name] + n)]
    part_of = {g: q for q, g in enumerate(parted)}
    columns, n_columns = param_columns()
    subs = list(range(12))

    with ExitStack() as ctx:
        top = [(nc.sbuf_base + 31) // 32 * 32]

        def place(name, shape, dt, offset=None):
            size = (int(np.prod(shape[1:])) * 4 + 31) // 32 * 32
            where = top[0] if offset is None else offset
            if offset is None:
                top[0] += size
            assert where + size <= nc.sbuf_usable_end, (name, where + size, nc.sbuf_usable_end)
            return nc.alloc_sbuf_tensor_at(name, shape, dt, offset=where)

        def sem(name):
            return ctx.enter_context(nc.semaphore(name))

        raw = place("w_raw", [P, RAW_RING, CHUNK_COLS], F32)
        whi = place("w_high", [P, PART_RING, CHUNK_COLS], F32R)
        wlo = place("w_rest", [P, PART_RING, CHUNK_COLS], F32R)
        h = place("residual", [P, KT, BOTH], F32)
        u_at = top[0]
        uhi = place("u_high", [P, KT, BOTH], F32R)
        ulo = place("u_rest", [P, KT, BOTH], F32R)
        y = place("sublayer_out", [P, KT, BOTH], F32, offset=u_at)
        mix_at = top[0]
        ghi = place("gated_high", [P, FT, BOTH], F32R)
        glo = place("gated_rest", [P, FT, BOTH], F32R)
        mix_end = top[0]
        sq = place("squares", [P, 2, BOTH], F32)
        ta = place("work_a", [P, 2, BOTH], F32)
        tb = place("work_b", [P, 2, BOTH], F32)
        sd, rinv = tb[:, 0], tb[:, 1]
        par = place("params", [P, n_columns], F32)
        A = place("pre_scale", [P, 6, KT, 2], F32)
        B = place("pre_shift", [P, 6, KT, 2], F32)
        G = place("post_scale", [P, 12, KT, 2], F32)
        cond4 = place("cond_silu", [P, 2, KT, 4], F32)
        mod_rows = place("mod_rows", [P, 4 * P], F32)[0:4, :]
        msum = place("mod_sum", [P, KT, 2], F32)
        ones = place("ones", [P, P], F32)
        small = place("small", [P, 16], F32)

        def pcol(name, a=0, b=None):
            o, n = columns[name]
            return par[:, o + a:o + (n if b is None else b)]

        bank = [ctx.enter_context(nc.psum_tensor(f"bank{n}", [P, 512], F32)) for n in range(8)]
        stat, mod = bank[4], bank[5]

        in_landed = sem("in_landed")
        par_landed = sem("par_landed")
        raw_landed = [sem(f"raw_landed{n}") for n in range(RAW_RING)]
        w_hi_ready = sem("w_hi_ready")
        w_lo_ready = sem("w_lo_ready")
        w_used = sem("w_used")
        const_ready = sem("const_ready")
        cond_ready = sem("cond_ready")
        mod_copied = sem("mod_copied")
        mod_turned = sem("mod_turned")
        mod_read = sem("mod_read")
        dve_step = sem("dve_step")
        act_step = sem("act_step")
        silu_done = sem("silu_done")
        gate_done = sem("gate_done")
        ghi_done = sem("ghi_done")
        glo_done = sem("glo_done")
        sq_ready = sem("sq_ready")
        sq_used = sem("sq_used")
        sd_ready = sem("sd_ready")
        rinv_ready = sem("rinv_ready")
        y_ready = sem("y_ready")
        post_ready = sem("post_ready")
        h_ready_pool = sem("h_ready_pool")
        h_ready_dve = sem("h_ready_dve")
        pre_ready = sem("pre_ready")
        uhi_ready = sem("uhi_ready")
        ulo_ready = sem("ulo_ready")
        out_done = sem("out_done")

        chain = {"dve": 0, "act": 0}

        def link(eng, ins):
            which, s = ("dve", dve_step) if eng is nc.vector else ("act", act_step)
            chain[which] += 1
            ins.then_inc(s, 1)
            eng.wait_ge(s, chain[which])

        def width(s):
            return BOTH if s <= 3 else SEQ

        def width_in(s):
            return BOTH if s <= 4 else SEQ

        def halves(n):
            return [(0, slice(0, SEQ)), (1, slice(SEQ, BOTH))][:n // SEQ]

        def round_y(s):
            return 2 * s + 1

        def round_h(s):
            return 2 * s + 2

        ada_index = {}
        for name, *_ in plan:
            if name.startswith("ada"):
                ada_index[name] = len(ada_index)

        def behind(s):
            if s == subs[-1]:
                return []
            return {0: [(0, 3), (0, 4)], 1: [(1, 0), (1, 1)], 2: [(1, 2), (1, 3)], 3: [(1, 4), (1, 5)]}.get(s, [])

        def await_mod(eng, s, m):
            eng.wait_ge(mod_read, ada_index[f"ada{s // 3}_{3 * (s % 3) + m}"] + 1)

        def ring_loop(eng, n, body, peel=RAW_RING):
            for j in range(min(n, peel)):
                body(j, None)
            turns = (n - 1 - peel) // RAW_RING
            if turns > 0:
                with eng.Fori(0, turns) as i:
                    for j in range(peel, peel + RAW_RING):
                        body(j, i)
            for j in range(peel + RAW_RING * max(turns, 0), n):
                body(j, None)

        def load_chunk(sp, name, src, row, g0, j, i):
            g = g0 + j
            if g >= RAW_RING:
                old = g - RAW_RING
                if old in part_of:
                    sp.wait_ge(w_lo_ready, part_of[old] + 1)
                else:
                    sp.wait_ge(w_used, old + 1)
            n = chunk_cols[g]
            sp.dma_start(raw[:, g % RAW_RING, 0:n], t[src][row + j]).then_inc(raw_landed[g % RAW_RING], 16)

        def make_high(g, i=None):
            if g not in part_of:
                return
            q = part_of[g]
            nc.scalar.wait_ge(raw_landed[g % RAW_RING], at(16 * (g // RAW_RING + 1), 16, i))
            if q >= PART_RING:
                nc.scalar.wait_ge(w_used, at(parted[q - PART_RING] + 1, RAW_RING, i))
            n = chunk_cols[g]
            nc.scalar.activation(whi[:, q % PART_RING, 0:n], raw[:, g % RAW_RING, 0:n], ACT.Copy)\
                .then_inc(w_hi_ready, 1)

        def make_rest(g, i=None):
            if g not in part_of:
                return
            q = part_of[g]
            nc.vector.wait_ge(w_hi_ready, at(q + 1, RAW_RING, i))
            n = chunk_cols[g]
            nc.vector.tensor_tensor(wlo[:, q % PART_RING, 0:n], raw[:, g % RAW_RING, 0:n],
                                    whi[:, q % PART_RING, 0:n].bitcast(F32), ALU.subtract)\
                .then_inc(w_lo_ready, 1)

        def await_parts(g, i=None):
            nc.tensor.wait_ge(w_lo_ready, at(part_of[g] + 1, RAW_RING, i))

        def block_of(part, g, kt, m, cols=CHUNK):
            return part[:, part_of[g] % PART_RING, kt * cols + m * P:kt * cols + (m + 1) * P]

        def products(ps, g, kts, weights, acts_hi, acts_lo, first=True, last=True):
            pe = nc.tensor
            kts = list(kts)
            for n, kt in enumerate(kts):
                hi, lo = weights(whi, kt), weights(wlo, kt)
                a, b = acts_hi(kt), acts_lo(kt)
                pe.matmul(ps, hi, a, start=first and n == 0, stop=False)
                pe.matmul(ps, hi, b, start=False, stop=False)
                ins = pe.matmul(ps, lo, a, start=False, stop=last and n == len(kts) - 1)
            return ins

        def mod_products(layer, m, steps=range(4)):
            pe = nc.tensor
            g0, q = first_chunk[f"ada{layer}_{m}"], ada_index[f"ada{layer}_{m}"]
            for j in steps:
                g = g0 + j
                pe.wait_ge(raw_landed[g % RAW_RING], 16 * (g // RAW_RING + 1))
                if j == 0 and q:
                    pe.wait_ge(mod_read, q)
                c = CHUNK * (j % 2)
                for kt in range(KT):
                    ins = pe.matmul(mod[0:4, c:c + CHUNK], cond4[:, j // 2, kt, :],
                                    raw[:, g % RAW_RING, kt * CHUNK:(kt + 1) * CHUNK],
                                    start=j == 0 and kt == 0, stop=j == 3 and kt == KT - 1)
                ins.then_inc(w_used, 1)

        def mod_copy(layer, m):
            nc.scalar.wait_ge(w_used, first_chunk[f"ada{layer}_{m}"] + 4)
            nc.scalar.activation(mod_rows, mod[0:4, :], ACT.Copy).then_inc(mod_copied, 1)

        def mod_turn(layer, m):
            nc.tensor.wait_ge(mod_copied, ada_index[f"ada{layer}_{m}"] + 1)
            for k in range(KT // 2):
                ins = nc.tensor.transpose(mod[:, 4 * k:4 * k + 4], mod_rows[:, k * P:(k + 1) * P], ident[0:4, 0:4])
            ins.then_inc(mod_turned, 1)

        def take_mod(layer, m):
            dve = nc.vector
            dve.wait_ge(mod_turned, ada_index[f"ada{layer}_{m}"] + 1)
            ps = mod[:, 0:2 * KT].rearrange("p (k h c) -> p h k c", h=2, c=2)

            def split(ap):
                return ap.rearrange("p (h k) c -> p h k c", h=2)

            bias = pcol("ada_b", (layer * N_MOD + m) * 2 * KT, (layer * N_MOD + m + 1) * 2 * KT)\
                .rearrange("p (k c) -> p k c", c=2)
            s = 3 * layer + m // 3
            if m % 3 == 0:
                dve.tensor_tensor(split(B[:, s]), ps, split(bias), ALU.add).then_inc(mod_read, 1)
                return
            gain = pcol("gain", (2 * s + (m % 3 == 2)) * 2 * KT, (2 * s + 1 + (m % 3 == 2)) * 2 * KT)\
                .rearrange("p (k c) -> p k c", c=2)
            link(dve, dve.tensor_tensor(split(msum[:]), ps, split(bias), ALU.add))
            if m % 3 == 1:
                dve.scalar_tensor_tensor(A[:, s], msum[:], 1.0, gain, ALU.add, ALU.mult).then_inc(mod_read, 1)
            else:
                dve.scalar_tensor_tensor(G[:, s], msum[:], 0.5 if s % 3 != 1 else 1.0, gain, ALU.mult,
                                         ALU.mult).then_inc(mod_read, 1)

        def square(q, kt, src, n, i=None, step=0):
            k = 8 * q + kt
            if k >= 2 or i is not None:
                nc.scalar.wait_ge(sq_used, at(k - 1, step, i))
            dst = sq[:, kt % 2, 0:n] if i is None else sq[:, kt % 2:kt % 2 + 1, 0:n]
            nc.scalar.activation(dst, src, ACT.Square).then_inc(sq_ready, 1)

        def sum_squares(q, kt, n):
            pe = nc.tensor
            pe.wait_ge(sq_ready, 8 * q + kt + 1)
            if kt == 0 and q:
                pe.wait_ge(sd_ready, q)
            pe.matmul(stat[:, 0:n], ones[:], sq[:, kt % 2, 0:n], start=kt == 0, stop=kt == KT - 1)\
                .then_inc(sq_used, 1)

        def root(q, n):
            nc.scalar.wait_ge(sq_used, 8 * q + 8)
            nc.scalar.activation(sd[:, 0:n], stat[:, 0:n], ACT.Sqrt, scale=1.0 / D, bias=eps_col)\
                .then_inc(sd_ready, 1)

        def invert(q, n):
            nc.vector.wait_ge(sd_ready, q + 1)
            nc.vector.reciprocal(rinv[:, 0:n], sd[:, 0:n]).then_inc(rinv_ready, 1)
            nc.vector.wait_ge(rinv_ready, q + 1)

        eps_col = small[:, 0:1]

        def pre_pe(q, n):
            for kt in range(KT):
                sum_squares(q, kt, n)

        def norm_act(s, q, n):
            for kt in range(KT):
                if s:
                    await_h(nc.scalar, s - 1, kt)
                square(q, kt, h[:, kt, 0:n], n)
            root(q, n)

        def pre_act(s, n):
            act = nc.scalar
            for kt in range(KT):
                act.wait_ge(pre_ready, 8 * s + kt + 1)
                for c, sl in halves(n):
                    if s < 6:
                        ins = act.activation(uhi[:, kt, sl], ta[:, kt % 2, sl], ACT.Identity,
                                             bias=B[:, s, kt, c:c + 1])
                    else:
                        ins = act.activation(uhi[:, kt, sl], ta[:, kt % 2, sl], ACT.Copy)
                ins.then_inc(uhi_ready, 1)

        def pre_dve(s, n):
            dve = nc.vector

            def rest(kt):
                dve.wait_ge(uhi_ready, 8 * s + kt + 1)
                for c, sl in halves(n):
                    if s < 6:
                        ins = dve.scalar_tensor_tensor(ulo[:, kt, sl], ta[:, kt % 2, sl], B[:, s, kt, c:c + 1],
                                                       uhi[:, kt, sl].bitcast(F32), ALU.add, ALU.subtract)
                    else:
                        ins = dve.tensor_tensor(ulo[:, kt, sl], ta[:, kt % 2, sl], uhi[:, kt, sl].bitcast(F32),
                                                ALU.subtract)
                ins.then_inc(ulo_ready, 1)

            for kt in range(KT):
                if kt >= 2:
                    dve.wait_ge(ulo_ready, 8 * s + kt - 1)
                for c, sl in halves(n):
                    a = A[:, s, kt, c:c + 1] if s < 6 else pcol("gain2", (2 * (s - 6)) * KT + kt,
                                                               (2 * (s - 6)) * KT + kt + 1)
                    ins = dve.scalar_tensor_tensor(ta[:, kt % 2, sl], h[:, kt, sl], a, rinv[:, sl],
                                                   ALU.mult, ALU.mult)
                ins.then_inc(pre_ready, 1)
                if kt:
                    rest(kt - 1)
            rest(KT - 1)

        def post_dve(s):
            dve = nc.vector
            n = width(s)
            invert(round_y(s), n)

            def add(kt):
                if kt in DVE_ADDS:
                    dve.wait_ge(post_ready, 8 * s + kt + 1)
                    dve.tensor_tensor(h[:, kt, 0:n], h[:, kt, 0:n], y[:, kt, 0:n], ALU.add).then_inc(h_ready_dve, 1)

            for kt in range(KT):
                for c, sl in halves(n):
                    ins = dve.scalar_tensor_tensor(y[:, kt, sl], y[:, kt, sl], G[:, s, kt, c:c + 1],
                                                   rinv[:, sl], ALU.mult, ALU.mult)
                ins.then_inc(post_ready, 1)
                add(kt - 1)
            add(KT - 1)

        def post_pool(s):
            pool = nc.gpsimd
            n = width(s)
            for kt in range(KT):
                if kt not in DVE_ADDS:
                    pool.wait_ge(post_ready, 8 * s + kt + 1)
                    pool.tensor_tensor(h[:, kt, 0:n], h[:, kt, 0:n], y[:, kt, 0:n], ALU.add).then_inc(h_ready_pool, 1)

        def await_h(eng, s, kt):
            if kt in DVE_ADDS:
                eng.wait_ge(h_ready_dve, len(DVE_ADDS) * s + DVE_ADDS.index(kt) + 1)
            else:
                eng.wait_ge(h_ready_pool, (KT - len(DVE_ADDS)) * s + kt - sum(d < kt for d in DVE_ADDS) + 1)

        def ffn_in_pe(s):
            pe = nc.tensor
            g0, n, f = first_chunk[f"in{s}"], width_in(s), FT * (s // 3 * 2 + (s % 3 == 2))

            def body(j, i):
                g = g0 + j
                await_parts(g, i)
                if j >= 2:
                    pe.wait_ge(gate_done, at(f + j - 1, RAW_RING, i))
                if j == 0:
                    for kt in range(KT):
                        pe.wait_ge(ulo_ready, 8 * s + kt + 1)
                        for m in range(2):
                            ins = products(bank[2 * m][:, 0:n], g, [kt], lambda w, k: block_of(w, g, k, m),
                                           lambda k: uhi[:, k, 0:n], lambda k: ulo[:, k, 0:n],
                                           first=kt == 0, last=kt == KT - 1)
                else:
                    for m in range(2):
                        ins = products(bank[2 * m + j % 2][:, 0:n], g, range(KT), lambda w, k: block_of(w, g, k, m),
                                       lambda k: uhi[:, k, 0:n], lambda k: ulo[:, k, 0:n])
                ins.then_inc(w_used, 1)

            ring_loop(pe, FT, body)

        def ffn_in_act(s):
            act = nc.scalar
            g0, n, f = first_chunk[f"in{s}"], width_in(s), FT * (s // 3 * 2 + (s % 3 == 2))

            def high(j, i):
                act.wait_ge(gate_done, at(f + j + 1, RAW_RING, i))
                dst = ghi[:, j, 0:n] if i is None else ghi[:, bass.ds(at(j, RAW_RING, i), 1), 0:n]
                src = tb[:, j % 2, 0:n] if i is None else tb[:, j % 2:j % 2 + 1, 0:n]
                act.activation(dst, src, ACT.Copy).then_inc(ghi_done, 1)

            def body(j, i):
                make_high(g0 + j + 1, i)
                if j:
                    high(j - 1, i)
                act.wait_ge(w_used, at(g0 + j + 1, RAW_RING, i))
                act.activation(ta[:, j % 2, 0:n], bank[j % 2][:, 0:n], ACT.Silu).then_inc(silu_done, 1)

            ring_loop(act, FT, body)
            high(FT - 1, None)

        def ffn_in_dve(s):
            dve = nc.vector
            g0, n, f = first_chunk[f"in{s}"], width_in(s), FT * (s // 3 * 2 + (s % 3 == 2))

            def rest(j, i):
                dve.wait_ge(ghi_done, at(f + j + 1, RAW_RING, i))
                if i is None:
                    dst, hi, src = glo[:, j, 0:n], ghi[:, j, 0:n], tb[:, j % 2, 0:n]
                else:
                    w = bass.ds(at(j, RAW_RING, i), 1)
                    dst, hi, src = glo[:, w, 0:n], ghi[:, w, 0:n], tb[:, j % 2:j % 2 + 1, 0:n]
                dve.tensor_tensor(dst, src, hi.bitcast(F32), ALU.subtract).then_inc(glo_done, 1)

            def body(j, i):
                make_rest(g0 + j + 1, i)
                if j:
                    rest(j - 1, i)
                dve.wait_ge(silu_done, at(f + j + 1, RAW_RING, i))
                if j >= 2:
                    dve.wait_ge(glo_done, at(f + j - 1, RAW_RING, i))
                dve.tensor_tensor(tb[:, j % 2, 0:n], ta[:, j % 2, 0:n], bank[2 + j % 2][:, 0:n], ALU.mult)\
                    .then_inc(gate_done, 1)

            ring_loop(dve, FT, body)
            rest(FT - 1, None)

        def out_shape(s):
            return (2 * KT, -2, HALF_FT) if s % 3 != 1 else (KT, 1, 12) if s == 10 else (4, 2, KT)

        def tiles_of(s, j):
            _, per, _ = out_shape(s)
            return [j // 2] if per == -2 and j % 2 else [] if per == -2 else list(range(per * j, per * (j + 1)))

        def out_pe(s, acts_hi, acts_lo, ready):
            pe = nc.tensor
            chunks, per, nk = out_shape(s)
            g0, n, q = first_chunk[f"out{s}"], width(s), round_y(s)

            def body(j, i):
                g = g0 + j
                await_parts(g, i)
                if j == 0:
                    ready()
                tiles = [j // 2] if per == -2 else tiles_of(s, j)
                for d in tiles:
                    if d >= 2 and (per != -2 or j % 2 == 0):
                        pe.wait_ge(y_ready, at(8 * s + d - 1, 2, i))
                    k0 = nk * (j % 2) if per == -2 else 0
                    m = d % 2 if per == 2 else 0
                    cols = CHUNK if per == 2 else P
                    ins = products(bank[d % 2][:, 0:n], g, range(nk), lambda w, k: block_of(w, g, k, m, cols),
                                   lambda k: acts_hi(k0 + k, n), lambda k: acts_lo(k0 + k, n),
                                   first=k0 == 0, last=k0 + nk >= (FT if per == -2 else nk))
                ins.then_inc(w_used, 1)
            ring_loop(pe, chunks, body)
            pe.wait_ge(sq_used, 8 * q + pool_sums(s))
            pe.wait_ge(sd_ready, q)
            pe.matmul(stat[:, 0:n], ones[:], ta[:, 0, 0:n], start=True, stop=False)
            for d in range(pool_sums(s), KT):
                pe.wait_ge(sq_ready, 8 * q + d + 1)
                pe.matmul(stat[:, 0:n], ones[:], sq[:, d % 2, 0:n], start=False, stop=d == KT - 1)\
                    .then_inc(sq_used, 1)

        def pool_sums(s):
            return tiles_of(s, out_shape(s)[0] - 1)[0]

        def out_pool(s):
            pool = nc.gpsimd
            n, q = width(s), round_y(s)
            for d in range(1, pool_sums(s)):
                pool.wait_ge(sq_ready, 8 * q + d + 1)
                if d == 1:
                    pool.tensor_tensor(ta[:, 0, 0:n], sq[:, 0, 0:n], sq[:, 1, 0:n], ALU.add).then_inc(sq_used, 2)
                else:
                    pool.wait_ge(sq_used, 8 * q + d)
                    pool.tensor_tensor(ta[:, 0, 0:n], ta[:, 0, 0:n], sq[:, d % 2, 0:n], ALU.add)\
                        .then_inc(sq_used, 1)

        def out_done_count(s, d):
            _, per, _ = out_shape(s)
            return 2 * d + 2 if per == -2 else d // per + 1

        def out_act(s):
            act = nc.scalar
            chunks, per, nk = out_shape(s)
            g0, n, q = first_chunk[f"out{s}"], width(s), round_y(s)

            def body(j, i):
                make_high(g0 + j + 1, i)
                for d in tiles_of(s, j):
                    act.wait_ge(y_ready, at(8 * s + d + 1, 2, i))
                    square(q, d, y[:, d, 0:n] if i is None else y[:, bass.ds(at(d, 2, i), 1), 0:n], n, i, 2)

            ring_loop(act, chunks, body)
            root(q, n)

        def out_dve(s):
            dve = nc.vector
            chunks, per, nk = out_shape(s)
            g0, n = first_chunk[f"out{s}"], width(s)

            def body(j, i):
                make_rest(g0 + j + 1, i)
                for d in tiles_of(s, j):
                    dve.wait_ge(w_used, at(g0 + out_done_count(s, d), RAW_RING, i))
                    if i is None:
                        dve.tensor_copy(y[:, d, 0:n], bank[d % 2][:, 0:n]).then_inc(y_ready, 1)
                    else:
                        dve.tensor_copy(y[:, bass.ds(at(d, 2, i), 1), 0:n],
                                        bank[d % 2][:, 0:n].rearrange("p (a n) -> p a n", a=1)).then_inc(y_ready, 1)

            ring_loop(dve, chunks, body)

        def ffn_out_pe(s):
            f = FT * (s // 3 * 2 + (s % 3 == 2)) + FT

            def ready():
                nc.tensor.wait_ge(glo_done, f)

            out_pe(s, lambda k, n: ghi[:, k, 0:n], lambda k, n: glo[:, k, 0:n], ready)

        proj_taken = sem("proj_taken")
        const_landed = sem("const_landed")
        rot_ready = sem("rot_ready")
        rope_done = sem("rope_done")
        att_scored = sem("att_scored")
        att_biased = sem("att_biased")
        att_max = sem("att_max")
        att_exp = sem("att_exp")
        att_sum = sem("att_sum")
        att_p = sem("att_p")
        att_turned = sem("att_turned")
        att_pt = sem("att_pt")
        att_pv = sem("att_pv")
        att_o = sem("att_o")
        att_olo = sem("att_olo")
        total = {"taken": 0, "rope": 0, "map": 0, "item": 0, "biased": 0, "olo": 0, "sum": 0, "const": 0}

        def region():
            where = [mix_at]

            def put(name, shape, dt=F32):
                size = (int(np.prod(shape[1:])) * 4 + 31) // 32 * 32
                where[0] += size
                assert where[0] <= mix_end, (name, where[0], mix_end)
                return place(name, shape, dt, offset=where[0] - size)

            return put

        attn_e = place("attn_exp", [P, 4, BOTH], F32, offset=u_at)
        attn_p = place("attn_probs", [P, 2, BOTH], F32, offset=u_at + 4 * BOTH * 4)
        attn_pt = place("attn_probs_turned", [P, 2, 4, P], F32, offset=u_at + 6 * BOTH * 4)
        over_ulo = u_at + KT * BOTH * 4
        attn_cols = place("attn_columns", [P, 3, 64], F32)

        class Projection:

            def __init__(self, s, seg, kinds, widths):
                self.s, self.g0, self.kinds, self.widths = s, first_chunk.get(seg), kinds, widths
                self.base = total["taken"]
                self.release = None
                self.first = []
                e = 0
                for kind, n in zip(kinds, widths):
                    self.first.append(e)
                    e += 2 if kind == "f" else n // P
                self.n = e
                total["taken"] += e

            def count(self, c):
                return 2 if self.kinds[c] == "f" else self.widths[c] // P

            def pe_chunk(self, c, wait_input=False):
                pe = nc.tensor
                g, n = self.g0 + c, self.widths[c]
                await_parts(g)
                if wait_input:
                    pe.wait_ge(ulo_ready, 8 * self.s + 8)
                for m in range(self.count(c)):
                    e = self.first[c] + m
                    if e >= 4:
                        s_, count = self.release(e - 4) if self.release else (proj_taken, self.base + e - 3)
                        pe.wait_ge(s_, count)
                    if self.kinds[c] == "f":
                        ins = products(bank[e % 4][:, 0:n], g, range(KT), lambda w, k: block_of(w, g, k, m),
                                       lambda k: uhi[:, k, 0:n], lambda k: ulo[:, k, 0:n])
                    else:
                        wide = CHUNK if self.kinds[c] == "t" else 2 * SSM_H
                        ps, tok = bank[e % 4][:, 0:wide], slice(m * P, (m + 1) * P)
                        w_hi = lambda k: whi[:, part_of[g] % PART_RING, k * wide:(k + 1) * wide]
                        w_lo = lambda k: wlo[:, part_of[g] % PART_RING, k * wide:(k + 1) * wide]
                        for k in range(KT):
                            pe.matmul(ps, uhi[:, k, tok], w_hi(k), start=k == 0, stop=False)
                            pe.matmul(ps, uhi[:, k, tok], w_lo(k), start=False, stop=False)
                            ins = pe.matmul(ps, ulo[:, k, tok], w_hi(k), start=False, stop=k == KT - 1)
                ins.then_inc(w_used, 1)

        class Attention:

            def __init__(self, items, n_maps, extra, fillers, kind):
                self.items, self.n_maps, self.kind, self.fillers = items, n_maps, kind, fillers
                self.m0, self.i0, self.b0, self.o0, self.s0 = (total["map"], total["item"], total["biased"],
                                                               total["olo"], total["sum"])
                total["map"] += len(items) * n_maps
                total["item"] += len(items)
                if kind != "da":
                    total["biased"] += len(items)
                    total["olo"] += len(items)
                if kind == "ev":
                    total["sum"] += len(items)
                self.extra = extra

            def filler(self, i):
                return self.fillers[i // 8] if i // 8 < len(self.fillers) else None

            def fill_pe(self, i):
                group, step = self.filler(i), {0: 0, 1: 1, 2: 2, 4: 3}.get(i % 8)
                if group and step is not None:
                    mod_products(*group, [step])
                if group and i % 8 == 6:
                    mod_turn(*group)

            def fill_act(self, i):
                group = self.filler(i)
                if group and i % 8 == 5:
                    mod_copy(*group)
                if group and group == self.fillers[-1] and i % 8 == 5:
                    make_high(first_chunk[f"ada{group[0]}_{group[1]}"] + 4)

            def fill_dve(self, i):
                group = self.filler(i)
                if group and i % 8 == 6:
                    if group == self.fillers[-1]:
                        make_rest(first_chunk[f"ada{group[0]}_{group[1]}"] + 4)
                    take_mod(*group)

            def pe(self):
                pe = nc.tensor
                n = len(self.items)
                for i in range(n + 3):
                    if i < n:
                        it = self.items[i]
                        for j, (q, k) in enumerate(it["maps"]):
                            m = i * self.n_maps + j
                            if m >= 4:
                                pe.wait_ge(att_exp, self.m0 + m - 3)
                            pe.matmul(bank[m % 4][:, 0:it["keys"]], q, k, start=True, stop=True)\
                                .then_inc(att_scored, 1)
                        self.fill_pe(i)
                    if 2 <= i < n + 2:
                        t_, it = i - 2, self.items[i - 2]
                        pe.wait_ge(att_p, self.i0 + t_ + 1)
                        if t_ >= 1:
                            pe.wait_ge(att_pt, self.i0 + t_)
                        for kt in range(it["keys"] // P):
                            ins = pe.transpose(bank[6][:, kt * P:(kt + 1) * P],
                                               attn_p[:, t_ % 2, kt * P:(kt + 1) * P], ident[:])
                        ins.then_inc(att_turned, 1)
                    if i >= 3:
                        t_, it = i - 3, self.items[i - 3]
                        pe.wait_ge(att_pt, self.i0 + t_ + 1)
                        if t_ >= 2:
                            if self.kind == "da":
                                pe.wait_ge(att_o, self.i0 + t_ - 1)
                            else:
                                pe.wait_ge(att_olo, self.o0 + t_ - 1)
                        lo, hi = it["rows"]
                        nk = it["keys"] // P
                        for kt in range(nk):
                            ins = pe.matmul(bank[4 + t_ % 2 * 3][lo:hi, 0:P], it["v"](kt),
                                            attn_pt[:, t_ % 2, kt], start=kt == 0, stop=kt == nk - 1)
                        ins.then_inc(att_pv, 1)

            def act(self):
                act = nc.scalar
                n = len(self.items)
                for i in range(n + 4):
                    if i < n:
                        it = self.items[i]
                        for j in range(self.n_maps):
                            m = i * self.n_maps + j
                            act.wait_ge(att_max, self.m0 + m + 1)
                            if m >= 4:
                                act.wait_ge(att_p, self.i0 + (m - 4) // self.n_maps + 1)
                            act.activation(attn_e[:, m % 4, 0:it["keys"]], bank[m % 4][:, 0:it["keys"]], ACT.Exp,
                                           bias=attn_cols[:, 0, m:m + 1],
                                           accum_out=attn_cols[:, 1, m:m + 1]).then_inc(att_exp, 1)
                        if self.kind == "ev":
                            act.activation(sink_e[:, i:i + 1], pcol("sink", it["head"], it["head"] + 1), ACT.Exp,
                                           bias=attn_cols[:, 0, i:i + 1]).then_inc(att_sum, 1)
                        self.fill_act(i)
                    if 2 <= i < n + 2:
                        t_, it = i - 2, self.items[i - 2]
                        act.wait_ge(att_turned, self.i0 + t_ + 1)
                        if t_ >= 2:
                            act.wait_ge(att_pv, self.i0 + t_ - 1)
                        nk = it["keys"] // P
                        act.activation(attn_pt[:, t_ % 2, 0:nk],
                                       bank[6][:, 0:nk * P].rearrange("p (k q) -> p k q", q=P),
                                       ACT.Copy).then_inc(att_pt, 1)
                    if 3 <= i < n + 3:
                        t_, it = i - 3, self.items[i - 3]
                        act.wait_ge(att_pv, self.i0 + t_ + 1)
                        lo, hi = it["rows"]
                        act.activation(it["out"][0], bank[4 + t_ % 2 * 3][lo:hi, 0:P], ACT.Copy)\
                            .then_inc(att_o, 1)

            def dve(self):
                dve = nc.vector
                n = len(self.items)
                nm = self.n_maps
                for i in range(n + 4):
                    if i < n:
                        it = self.items[i]
                        for j in range(nm):
                            m = i * nm + j
                            dve.wait_ge(att_scored, self.m0 + m + 1)
                            ps = bank[m % 4][:, 0:it["keys"]]
                            if "bias" in it:
                                part = bank[m % 4][:, 0:SEQ]
                                dve.tensor_tensor(part, part, it["bias"], ALU.add).then_inc(att_biased, 1)
                                dve.wait_ge(att_biased, self.b0 + i + 1)
                            if self.kind == "ev":
                                link(dve, dve.tensor_reduce(attn_cols[:, 0, m:m + 1], ps, AX_X, ALU.max, negate=True))
                                dve.tensor_tensor(attn_cols[:, 0, m:m + 1], attn_cols[:, 0, m:m + 1],
                                                  minus_sink[:, it["head"]:it["head"] + 1], ALU.min)\
                                    .then_inc(att_max, 1)
                            else:
                                dve.tensor_reduce(attn_cols[:, 0, m:m + 1], ps, AX_X, ALU.max, negate=True)\
                                    .then_inc(att_max, 1)
                        self.fill_dve(i)
                    if 1 <= i <= n:
                        t_, it = i - 1, self.items[i - 1]
                        m = t_ * nm
                        dve.wait_ge(att_exp, self.m0 + m + nm)
                        if self.kind == "ev":
                            dve.wait_ge(att_sum, self.s0 + t_ + 1)
                            link(dve, dve.tensor_tensor(attn_cols[:, 1, m:m + 1], attn_cols[:, 1, m:m + 1],
                                                        sink_e[:, t_:t_ + 1], ALU.add))
                        link(dve, dve.reciprocal(attn_cols[:, 2, m:m + nm], attn_cols[:, 1, m:m + nm]))
                        if t_ >= 2:
                            dve.wait_ge(att_turned, self.i0 + t_ - 1)
                        keys = it["keys"]
                        dst = attn_p[:, t_ % 2, 0:keys]
                        ins = dve.tensor_scalar(dst, attn_e[:, m % 4, 0:keys], attn_cols[:, 2, m:m + 1], None, ALU.mult)
                        if nm == 2:
                            link(dve, ins)
                            link(dve, dve.tensor_tensor(attn_cols[:, 2, m + 1:m + 2], attn_cols[:, 2, m + 1:m + 2],
                                                        minus_lam, ALU.mult))
                            ins = dve.scalar_tensor_tensor(dst, attn_e[:, (m + 1) % 4, 0:keys],
                                                           attn_cols[:, 2, m + 1:m + 2], dst, ALU.mult, ALU.add)
                        ins.then_inc(att_p, 1)
                    if i >= 4 and self.kind != "da":
                        t_, it = i - 4, self.items[i - 4]
                        dve.wait_ge(att_o, self.i0 + t_ + 1)
                        lo, hi = it["rows"]
                        dve.tensor_tensor(it["out"][1], bank[4 + t_ % 2 * 3][lo:hi, 0:P],
                                          it["out"][0].bitcast(F32), ALU.subtract).then_inc(att_olo, 1)

        ident = place("identity", [P, P], F32)
        minus_lam = small[:, 4:5]
        subln = small[:, 5:6]
        minus_sink = place("minus_sink", [P, EV_QH], F32)
        sink_e = place("sink_exp", [P, 2 * EV_QH], F32)
        mixers = {}
        heads_in = lambda h_: slice(h_ % 2 * HD, h_ % 2 * HD + HD)

        def rope_pe(r0, t_, m, src, rot, taken):
            pe = nc.tensor
            pe.wait_ge(proj_taken, taken)
            if t_ >= 2:
                pe.wait_ge(rope_done, r0 + t_ - 1)
            pe.matmul(bank[6 + t_ % 2][:, 0:SEQ], rot, src[:, m, 0:SEQ], start=True, stop=True)\
                .then_inc(rot_ready, 1)

        def rope_dve(r0, t_, m, src, cos, sin):
            dve = nc.vector
            dve.wait_ge(rot_ready, r0 + t_ + 1)
            if t_:
                dve.wait_ge(rope_done, r0 + t_)
            link(dve, dve.tensor_tensor(ta[:, 0, 0:SEQ], src[:, m, 0:SEQ], cos, ALU.mult))
            link(dve, dve.tensor_tensor(ta[:, 1, 0:SEQ], bank[6 + t_ % 2][:, 0:SEQ], sin, ALU.mult))
            dve.tensor_tensor(src[:, m, 0:SEQ], ta[:, 0, 0:SEQ], ta[:, 1, 0:SEQ], ALU.add).then_inc(rope_done, 1)

        class DiffAttention:
            def __init__(self, s=1):
                put = region()
                self.s = s
                self.qk = put("da_qk", [P, 16, BOTH])
                self.v = put("da_v", [P, 4, D])
                self.o = put("da_o", [P, KT, BOTH])
                self.rope = put("da_rope", [P, P + 2 * SEQ])
                self.ohi = place("da_o_high", [P, KT, BOTH], F32R, offset=mix_at)
                self.olo = place("da_o_rest", [P, KT, BOTH], F32R, offset=mix_at + KT * BOTH * 4)
                self.proj = Projection(s, f"in{s}", ["f"] * 8 + ["t"] * 4, [BOTH] * 12)
                self.r0 = total["rope"]
                total["rope"] += 16
                total["const"] += 1
                self.const = total["const"]
                items = []
                for hh in range(KT):
                    for qt in range(4):
                        k0 = 0 if qt < 2 else SEQ
                        keys = BOTH - k0
                        items.append({
                            "maps": [(self.qk[j * HD:(j + 1) * HD, hh, qt * P:(qt + 1) * P],
                                      self.qk[j * HD:(j + 1) * HD, 8 + hh, k0:BOTH]) for j in range(2)],
                            "keys": keys, "rows": (0, P),
                            "v": (lambda kt, hh=hh, k0=k0: self.v[:, k0 // P + kt, hh * P:(hh + 1) * P]),
                            "out": (self.o[:, hh, qt * P:(qt + 1) * P],)})
                self.att = Attention(items, 2, None, [(0, 5), (0, 6), (0, 7), (0, 8)], "da")
                self.sq_done, self.stat_done, self.root_done = sem("hn_squares"), sem("hn_summed"), sem("hn_root")
                self.inv, self.scaled, self.hi_done, self.lo_done = (sem("hn_inverse"), sem("hn_scaled"),
                                                                     sem("hn_high"), sem("hn_rest"))

            def loads(self, sp):
                sp.dma_start(self.rope[:], t["rope1"]).then_inc(const_landed, 16)

            def pe(self, pe):
                for c in range(12):
                    self.proj.pe_chunk(c, c == 0)
                    if c == 1:
                        pe.wait_ge(const_landed, 16 * self.const)
                    if 1 <= c <= 8:
                        for m in (2 * c - 2, 2 * c - 1):
                            rope_pe(self.r0, m, m, self.qk, self.rope[:, 0:P], self.proj.base + m + 1)
                pe.wait_ge(rope_done, self.r0 + 16)
                pe.wait_ge(proj_taken, self.proj.base + self.proj.n)
                self.att.pe()
                for hh in range(KT):
                    pe.wait_ge(self.sq_done, hh + 1)
                    if hh >= 2:
                        pe.wait_ge(self.root_done, hh - 1)
                    pe.matmul(bank[6 + hh % 2][:, :], ones[:], sq[:, hh % 2], start=True, stop=True)\
                        .then_inc(self.stat_done, 1)

            def out(self, pe):
                out_pe(self.s, lambda k, n: self.ohi[:, k, 0:n], lambda k, n: self.olo[:, k, 0:n],
                       lambda: pe.wait_ge(self.lo_done, KT))

            def act(self, act):
                g0 = self.proj.g0
                for c in range(12):
                    make_high(g0 + c + 1)
                    act.wait_ge(w_used, g0 + c + 1)
                    for m in range(self.proj.count(c)):
                        e = self.proj.first[c] + m
                        if c < 8:
                            ins = act.activation(self.qk[:, e], bank[e % 4][:], ACT.Copy, scale=0.125 if e < 8 else 1.0)
                        else:
                            ins = act.activation(self.v[:, m, (c - 8) * CHUNK:(c - 7) * CHUNK], bank[e % 4][:, 0:CHUNK],
                                                 ACT.Copy)
                        ins.then_inc(proj_taken, 1)
                self.att.act()
                act.wait_ge(att_o, self.att.i0 + 32)

                def squares(hh):
                    if hh >= 2:
                        act.wait_ge(self.stat_done, hh - 1)
                    act.activation(sq[:, hh % 2], self.o[:, hh], ACT.Square).then_inc(self.sq_done, 1)

                def high(hh):
                    act.wait_ge(self.scaled, hh + 1)
                    act.activation(self.ohi[:, hh], ta[:, hh % 2], ACT.Copy).then_inc(self.hi_done, 1)

                squares(0)
                for hh in range(KT):
                    if hh + 1 < KT:
                        squares(hh + 1)
                    act.wait_ge(self.stat_done, hh + 1)
                    if hh >= 2:
                        act.wait_ge(self.scaled, hh - 1)
                    act.activation(tb[:, hh % 2], bank[6 + hh % 2][:], ACT.Sqrt, scale=1.0 / P, bias=eps_col)\
                        .then_inc(self.root_done, 1)
                    if hh:
                        high(hh - 1)
                high(KT - 1)

            def dve(self, dve):
                g0 = self.proj.g0
                for c in range(12):
                    make_rest(g0 + c + 1)
                    if c == 1:
                        dve.wait_ge(const_landed, 16 * self.const)
                    if 1 <= c <= 8:
                        for m in (2 * c - 2, 2 * c - 1):
                            rope_dve(self.r0, m, m, self.qk, self.rope[:, P:P + SEQ], self.rope[:, P + SEQ:])
                self.att.dve()
                for hh in range(KT):
                    dve.wait_ge(self.root_done, hh + 1)
                    dve.reciprocal(tb[:, hh % 2], tb[:, hh % 2]).then_inc(self.inv, 1)
                    dve.wait_ge(self.inv, hh + 1)
                    if hh >= 2:
                        dve.wait_ge(self.lo_done, hh - 1)
                    dve.scalar_tensor_tensor(ta[:, hh % 2], self.o[:, hh], subln, tb[:, hh % 2], ALU.mult, ALU.mult)\
                        .then_inc(self.scaled, 1)
                    dve.wait_ge(self.hi_done, hh + 1)
                    dve.tensor_tensor(self.olo[:, hh], ta[:, hh % 2], self.ohi[:, hh].bitcast(F32), ALU.subtract)\
                        .then_inc(self.lo_done, 1)

            def pool(self, pool):
                pass

        class Neighbourhood:
            def __init__(self, s=4):
                put = region()
                self.s = s
                self.q = put("na_q", [P, KT, SEQ])
                self.k = put("na_k", [P, KT, BOTH])
                self.v = put("na_v", [P, 4, D])
                self.bias = put("na_bias", [P, 2 * NA_H, SEQ])
                self.mask = put("na_mask", [P, SEQ])
                self.ohi = place("na_o_high", [P, KT, SEQ], F32R, offset=over_ulo)
                self.olo = place("na_o_rest", [P, KT, SEQ], F32R, offset=over_ulo + KT * SEQ * 4)
                self.proj = Projection(s, f"in{s}", ["f"] * 8 + ["t"] * 4, [SEQ] * 4 + [BOTH] * 8)
                total["const"] += 2
                self.const = total["const"]
                self.masked = sem("na_bias_masked")
                items = []
                for pair in range(KT):
                    for qt in range(2):
                        for hh in (2 * pair, 2 * pair + 1):
                            r = heads_in(hh)
                            items.append({
                                "maps": [(self.q[r, pair, qt * P:(qt + 1) * P], self.k[r, pair, :])],
                                "keys": BOTH, "rows": (r.start, r.stop), "bias": self.bias[:, 2 * hh + qt],
                                "v": (lambda kt, hh=hh: self.v[:, kt, hh * HD:(hh + 1) * HD]),
                                "out": (self.ohi[r, pair, qt * P:(qt + 1) * P],
                                        self.olo[r, pair, qt * P:(qt + 1) * P])})
                self.att = Attention(items, 1, None, [(1, 6), (1, 7), (1, 8)], "na")

            def loads(self, sp):
                sp.dma_start(self.bias[:].rearrange("p a b -> p (a b)"), t["na_bias"]).then_inc(const_landed, 16)
                sp.dma_start(self.mask[:], t["na_mask"]).then_inc(const_landed, 16)

            def pool(self, pool):
                pool.wait_ge(const_landed, 16 * self.const)
                for n in range(2 * NA_H):
                    pool.tensor_tensor(self.bias[:, n], self.bias[:, n], self.mask[:], ALU.add)\
                        .then_inc(self.masked, 1)

            def pe(self, pe):
                for c in range(12):
                    self.proj.pe_chunk(c, c == 0)
                pe.wait_ge(proj_taken, self.proj.base + self.proj.n)
                self.att.pe()

            def out(self, pe):
                out_pe(self.s, lambda k, n: self.ohi[:, k, 0:n], lambda k, n: self.olo[:, k, 0:n],
                       lambda: pe.wait_ge(att_olo, self.att.o0 + 2 * NA_H))

            def act(self, act):
                g0 = self.proj.g0
                for c in range(12):
                    make_high(g0 + c + 1)
                    act.wait_ge(w_used, g0 + c + 1)
                    for m in range(self.proj.count(c)):
                        e = self.proj.first[c] + m
                        if c < 4:
                            ins = act.activation(self.q[:, e], bank[e % 4][:, 0:SEQ], ACT.Copy, scale=0.125)
                        elif c < 8:
                            ins = act.activation(self.k[:, e - 8], bank[e % 4][:], ACT.Copy)
                        else:
                            ins = act.activation(self.v[:, m, (c - 8) * CHUNK:(c - 7) * CHUNK], bank[e % 4][:, 0:CHUNK],
                                                 ACT.Copy)
                        ins.then_inc(proj_taken, 1)
                self.att.act()

            def dve(self, dve):
                for c in range(12):
                    make_rest(self.proj.g0 + c + 1)
                dve.wait_ge(self.masked, 2 * NA_H)
                self.att.dve()

        class Even:
            def __init__(self, s=7):
                put = region()
                self.s = s
                self.u = put("ev_u", [P, 2, CHUNK])
                self.v = put("ev_v", [P, 2, CHUNK])
                self.q = put("ev_qk", [P, 8, SEQ])
                self.const_tile = put("ev_const", [P, 2 * SEQ + 8 * SEQ])
                self.rope = put("ev_rope", [P, P + 2 * SEQ])
                self.pw = put("ev_pool_w", [P, 2 * HD])
                self.pooled = put("ev_pooled", [P, 2, SEQ])
                self.ohi = put("ev_o_high", [P, KT, SEQ], F32R)
                self.olo = put("ev_o_rest", [P, KT, SEQ], F32R)
                self.proj = Projection(s, f"in{s}", ["t"] * 2 + ["f"] * 4, [SEQ] * 6)
                self.r0 = total["rope"]
                total["rope"] += 8
                total["const"] += 3
                self.const = total["const"]
                self.mixed, self.taken, self.done = sem("pool_mixed"), sem("pool_taken"), sem("pool_done")
                items = []
                for n, hh in enumerate(EV_HEADS):
                    kv = hh // 3
                    for qt in range(2):
                        r = heads_in(n)
                        assert kv % 2 == n % 2
                        items.append({
                            "maps": [(self.q[r, n // 2, qt * P:(qt + 1) * P], self.q[r, 6 + kv // 2, :])],
                            "keys": SEQ, "rows": (r.start, r.stop), "head": n,
                            "bias": self.const_tile[:, qt * SEQ:(qt + 1) * SEQ],
                            "v": (lambda kt, kv=kv: self.v[:, kt, kv * HD:(kv + 1) * HD]),
                            "out": (self.ohi[r, 2 + n // 2, qt * P:(qt + 1) * P],
                                    self.olo[r, 2 + n // 2, qt * P:(qt + 1) * P])})
                self.att = Attention(items, 1, None, [], "ev")

            def loads(self, sp):
                sp.dma_start(self.const_tile[:], t["ev_const"]).then_inc(const_landed, 16)
                sp.dma_start(self.rope[:], t["rope2"]).then_inc(const_landed, 16)
                sp.dma_start(self.pw[:], t["pool_w"]).then_inc(const_landed, 16)

            def pool(self, pool):
                pass

            def pe(self, pe):
                for c in range(6):
                    self.proj.pe_chunk(c, c == 0)
                    if c == 1:
                        pe.wait_ge(const_landed, 16 * self.const)
                    if c >= 3:
                        for t_ in (2 * c - 6, 2 * c - 5):
                            rope_pe(self.r0, t_, t_, self.q, self.rope[:, 0:P], self.proj.base + 4 + t_ + 1)
                    if c == 1:
                        pe.wait_ge(proj_taken, self.proj.base + 2)
                        for g in range(4):
                            r = heads_in(g)
                            for kt in range(2):
                                m_w = self.const_tile[:, (2 + 2 * g + kt) * SEQ:(3 + 2 * g + kt) * SEQ]
                                ins = pe.matmul(bank[6 + g // 2][r, 0:SEQ], self.u[:, kt, g * HD:(g + 1) * HD], m_w,
                                                start=kt == 0, stop=kt == 1)
                            if g % 2:
                                ins.then_inc(self.mixed, 1)
                    if c == 2:
                        pe.wait_ge(self.taken, 2)
                        for g in range(4):
                            r = heads_in(g)
                            ins = pe.matmul(bank[4 + g // 2][r, 0:SEQ], self.pw[r, g // 2 * HD:(g // 2 + 1) * HD],
                                            self.pooled[r, g // 2], start=True, stop=True)
                        ins.then_inc(self.mixed, 1)
                pe.wait_ge(proj_taken, self.proj.base + self.proj.n)
                for t_ in (6, 7):
                    rope_pe(self.r0, t_, t_, self.q, self.rope[:, 0:P], self.proj.base + 4 + t_ + 1)
                pe.wait_ge(rope_done, self.r0 + 8)
                pe.wait_ge(self.done, 4)
                self.att.pe()

            def out(self, pe):
                out_pe(self.s, lambda k, n: self.ohi[:, k, 0:n], lambda k, n: self.olo[:, k, 0:n],
                       lambda: pe.wait_ge(att_olo, self.att.o0 + 2 * EV_QH))

            def act(self, act):
                g0 = self.proj.g0
                for c in range(6):
                    make_high(g0 + c + 1)
                    act.wait_ge(w_used, g0 + c + 1)
                    for m in range(2):
                        e = self.proj.first[c] + m
                        if c < 2:
                            ins = act.activation((self.u, self.v)[c][:, m], bank[e % 4][:, 0:CHUNK], ACT.Copy)
                        else:
                            ins = act.activation(self.q[:, e - 4], bank[e % 4][:, 0:SEQ], ACT.Copy,
                                                 scale=0.125 if e < 10 else 1.0)
                        ins.then_inc(proj_taken, 1)
                    if c == 1:
                        for n in range(2):
                            act.wait_ge(self.mixed, n + 1)
                            act.activation(self.pooled[:, n], bank[6 + n][:, 0:SEQ], ACT.Copy).then_inc(self.taken, 1)
                    if c == 2:
                        act.wait_ge(self.mixed, 3)
                        for n in range(2):
                            act.activation(self.ohi[:, n], bank[4 + n][:, 0:SEQ], ACT.Copy,
                                           scale=pcol("pool_scale", n, n + 1)).then_inc(self.taken, 1)
                self.att.act()

            def dve(self, dve):
                g0 = self.proj.g0
                for c in range(6):
                    make_rest(g0 + c + 1)
                    if c == 2:
                        dve.wait_ge(const_landed, 16 * self.const)
                    if c >= 3:
                        for t_ in (2 * c - 6, 2 * c - 5):
                            rope_dve(self.r0, t_, t_, self.q, self.rope[:, P:P + SEQ], self.rope[:, P + SEQ:])
                    if c == 2:
                        for n in range(2):
                            dve.wait_ge(self.taken, 3 + n)
                            dve.scalar_tensor_tensor(self.olo[:, n], bank[4 + n][:, 0:SEQ], pcol("pool_scale", n, n + 1),
                                                     self.ohi[:, n].bitcast(F32), ALU.mult, ALU.subtract)\
                                .then_inc(self.done, 2)
                for t_ in (6, 7):
                    rope_dve(self.r0, t_, t_, self.q, self.rope[:, P:P + SEQ], self.rope[:, P + SEQ:])
                self.att.dve()

        mixers[1] = DiffAttention()
        mixers[4] = Neighbourhood()
        mixers[7] = Even()

        def attention_setup_dve(dve):
            lam_init = 0.8 - 0.6
            lv = pcol("lam").rearrange("p (a d) -> p a d", d=HD)
            link(dve, dve.tensor_tensor_reduce(ta[:, 0, 0:HD], lv[:, 0], lv[:, 1], 1.0, 0.0, ALU.mult, ALU.add,
                                               small[:, 1:2]))
            dve.tensor_tensor_reduce(ta[:, 1, 0:HD], lv[:, 2], lv[:, 3], 1.0, 0.0, ALU.mult, ALU.add,
                                     small[:, 2:3]).then_inc(lam_step, 1)
            dve.wait_ge(lam_step, 2)
            link(dve, dve.tensor_tensor(small[:, 3:4], small[:, 7:8], small[:, 6:7], ALU.subtract))
            link(dve, dve.tensor_scalar(minus_lam, small[:, 3:4], -lam_init, None, ALU.add))
            link(dve, dve.tensor_scalar(subln, pcol("subln"), 1.0 - lam_init, None, ALU.mult))
            link(dve, dve.tensor_scalar(minus_sink[:], pcol("sink"), -1.0, None, ALU.mult))

        def attention_setup_act(act):
            act.wait_ge(lam_step, 1)
            act.activation(small[:, 6:8], small[:, 1:3], ACT.Exp).then_inc(lam_step, 1)

        lam_step = sem("lam_step")

        class Odd:

            DVE_TAPS = 2 * CONV_K
            SPANS = [(0, 0, SEQ), (1, P, SEQ), (0, 0, P), (1, 0, SEQ)]
            OFFSETS = [0, SEQ, SEQ + P, 2 * SEQ]

            def __init__(self, s=10):
                put = region()
                self.s = s
                self.gp = put("od_glu_padded", [P, 4, SEQ + CONV_K - 1])
                self.g = put("od_glu", [P, 4, SEQ])
                self.xp = put("od_xbc_padded", [P, 16, SEQ + 3])
                self.x = put("od_xbc", [P, 16, SEQ])
                self.z = put("od_z", [P, KT, SEQ])
                self.sums = put("od_sums", [P, 2, 2, SEQ])
                self.tri = put("od_masks", [P, 2, SEQ])
                self.ohi = put("od_o_high", [P, 12, SEQ], F32R)
                self.olo = put("od_o_rest", [P, 12, SEQ], F32R)
                self.dt = put("od_dt", [P, 6, 2 * 2 * SSM_H])
                self.cols = put("od_decay_columns", [P, 2, 2, SSM_H])
                self.ea = put("od_a", [P, 2 * SSM_H])
                self.xt = place("od_x_tokens", [P, 2, D], F32, offset=u_at)
                self.yz = place("od_y", [P, KT, SEQ], F32, offset=u_at + 2 * D * 4)
                self.seg = place("od_decays", [P, 2, 3 * SEQ], F32, offset=over_ulo)
                self.m = place("od_maps", [P, 2, 3 * SEQ], F32, offset=over_ulo + 6 * SEQ * 4)
                self.base = total["taken"]
                self.proj = Projection(s, f"in{s}", ["f"] * 4 + ["d"] + ["f"] * 12, [SEQ] * 17)
                self.proj.release = self.release
                total["const"] += 2
                self.const = total["const"]
                names = ["pads", "sigmoid", "glu", "pool_tap", "glu_dve", "glu_pool", "dt_exp", "dt_u", "dt_log",
                         "a_exp", "a_ready", "cum_ready", "cum_taken", "conv", "x_done", "turned", "xt_ready",
                         "cb", "rowsum", "seg_ready", "decay", "maps", "y_ps", "y_taken", "ln_sum", "ln_centred",
                         "ln_sq", "ln_var", "ln_root", "ln_scaled", "ln_act", "ln_hi", "ln_lo", "sq", "sq_used",
                         "root", "scaled", "hi", "lo"]
                self.sem = {n: sem("od_" + n) for n in names}

            def release(self, e):
                return (self.sem["glu"], e // 2 + 1) if e < 8 else (proj_taken, self.base + e - 8 + 1)

            def loads(self, sp):
                sp.dma_start(self.sums[:].rearrange("p a b c -> p (a b c)"), t["od_const"][:, 0:4 * SEQ])\
                    .then_inc(const_landed, 16)
                sp.dma_start(self.tri[:].rearrange("p a b -> p (a b)"), t["od_const"][:, 4 * SEQ:])\
                    .then_inc(const_landed, 16)

            def dve_tap(self, dve, j):
                n, k, S = j % 2, j // 2, self.sem
                if j >= self.DVE_TAPS:
                    return
                w, src = pcol("dw_w", n * CONV_K + k, n * CONV_K + k + 1), self.gp[:, n, k:k + SEQ]
                if k == 0:
                    ins = dve.tensor_scalar(self.g[:, n], src, w, pcol("dw_b", n, n + 1), ALU.mult, ALU.add)
                else:
                    dve.wait_ge(S["glu_dve"], j - 1)
                    ins = dve.scalar_tensor_tensor(self.g[:, n], src, w, self.g[:, n], ALU.mult, ALU.add)
                ins.then_inc(S["glu_dve"], 1)

            def pool_tap(self, pool, n, k):
                S = self.sem
                w, src = pcol("dw_w", n * CONV_K + k, n * CONV_K + k + 1), self.gp[:, n, k:k + SEQ]
                count = (n - 2) * CONV_K + k
                if k == 0:
                    pool.tensor_scalar(self.g[:, n], src, w, pcol("dw_b", n, n + 1), ALU.mult, ALU.add)\
                        .then_inc(S["glu_pool"], 1)
                    return
                if count >= 2:
                    pool.wait_ge(S["glu_pool"], count - 1)
                pool.tensor_scalar(tb[:, k % 2, 0:SEQ], src, w, None, ALU.mult).then_inc(S["pool_tap"], 1)
                pool.wait_ge(S["pool_tap"], count - (n - 2))
                pool.wait_ge(S["glu_pool"], count)
                pool.tensor_tensor(self.g[:, n], self.g[:, n], tb[:, k % 2, 0:SEQ], ALU.add)\
                    .then_inc(S["glu_pool"], 1)

            def pool(self, pool):
                S = self.sem
                pool.wait_ge(w_used, self.proj.g0)
                half = CONV_K // 2
                pool.memset(self.gp[:, :, 0:half], 0.0).then_inc(S["pads"], 1)
                pool.memset(self.gp[:, :, half + SEQ:], 0.0).then_inc(S["pads"], 1)
                pool.memset(self.xp[:, :, 0:2], 0.0).then_inc(S["pads"], 1)
                pool.memset(self.xp[:, :, 2 + SEQ:], 0.0).then_inc(S["pads"], 1)
                pool.wait_ge(S["pads"], 4)
                for n in (2, 3):
                    pool.wait_ge(S["glu"], n + 1)
                    for k in range(CONV_K):
                        self.pool_tap(pool, n, k)

            def conv(self, dve, idx):
                S = self.sem
                dve.wait_ge(proj_taken, self.base + 2 + idx + 1)
                for k in range(4):
                    w, src = pcol("cw", idx * 4 + k, idx * 4 + k + 1), self.xp[:, idx, k:k + SEQ]
                    if k == 0:
                        ins = dve.tensor_scalar(self.x[:, idx], src, w, pcol("cb", idx, idx + 1), ALU.mult, ALU.add)
                    else:
                        ins = dve.scalar_tensor_tensor(self.x[:, idx], src, w, self.x[:, idx], ALU.mult, ALU.add)
                    if k < 3:
                        link(dve, ins)
                ins.then_inc(S["conv"], 1)

            def act(self, act):
                S, g0 = self.sem, self.proj.g0

                def silu_x(idx):
                    act.wait_ge(S["conv"], idx + 1)
                    act.activation(self.x[:, idx], self.x[:, idx], ACT.Silu).then_inc(S["x_done"], 1)

                for c in range(17):
                    make_high(g0 + c + 1)
                    act.wait_ge(w_used, g0 + c + 1)
                    if c < 4:
                        act.activation(ta[:, c % 2, 0:SEQ], bank[(2 * c + 1) % 4][:, 0:SEQ], ACT.Sigmoid)\
                            .then_inc(S["sigmoid"], 1)
                    elif c == 4:
                        for m in range(2):
                            act.activation(self.dt[:, 0, 32 * m:32 * m + 32], bank[m][:, 0:2 * SSM_H], ACT.Copy)\
                                .then_inc(proj_taken, 1)
                    else:
                        for m in range(2):
                            e = self.proj.first[c] + m
                            if c < 13:
                                if e == 10:
                                    act.wait_ge(S["pads"], 4)
                                ins = act.activation(self.xp[:, e - 10, 2:2 + SEQ], bank[e % 4][:, 0:SEQ], ACT.Copy)
                            else:
                                ins = act.activation(self.z[:, e - 26], bank[e % 4][:, 0:SEQ], ACT.Silu)
                            ins.then_inc(proj_taken, 1)
                    if c == 6:
                        act.wait_ge(S["dt_exp"], 1)
                        act.activation(self.dt[:, 1], self.dt[:, 1], ACT.Exp, scale=-1.0).then_inc(S["dt_exp"], 1)
                        act.activation(self.ea[:], pcol("a_log"), ACT.Exp).then_inc(S["a_exp"], 1)
                        act.wait_ge(S["dt_u"], 1)
                        act.activation(self.dt[:, 3], self.dt[:, 2], ACT.Ln).then_inc(S["dt_log"], 1)
                    if c >= 8:
                        for idx in range(2 * (c - 8), min(2 * (c - 8) + 2, 16)):
                            silu_x(idx)
                act.wait_ge(S["cum_ready"], 1)
                act.activation(self.cols[:].rearrange("p a b c -> p (a b c)"), bank[6][:, 0:4 * SSM_H], ACT.Copy)\
                    .then_inc(S["cum_taken"], 1)
                for n in range(4):
                    act.wait_ge(S["turned"], n + 1)
                    act.activation(self.xt[:, n // 2, n % 2 * 512:(n % 2 + 1) * 512], bank[2 + n % 2][:], ACT.Copy)\
                        .then_inc(S["xt_ready"], 1)
                for hh in range(SSM_H):
                    act.wait_ge(S["seg_ready"], hh + 1)
                    act.activation(self.seg[:, hh % 2], self.seg[:, hh % 2], ACT.Exp).then_inc(S["decay"], 1)
                for n in range(4):
                    act.wait_ge(S["ln_centred"], n + 1)
                    if n >= 2:
                        act.wait_ge(S["ln_var"], n - 1)
                    act.activation(sq[:, n % 2, 0:SEQ], self.g[:, n], ACT.Square).then_inc(S["ln_sq"], 1)
                act.wait_ge(S["ln_var"], 4)
                act.activation(sd[:, 0:SEQ], bank[4][:, 0:SEQ], ACT.Sqrt, scale=1.0 / 512, bias=eps_col)\
                    .then_inc(S["ln_root"], 1)
                for kt in range(KT):
                    act.wait_ge(S["y_taken"], kt + 1)
                    if kt >= 2:
                        act.wait_ge(S["sq_used"], kt - 1)
                    act.activation(sq[:, kt % 2, 0:SEQ], self.yz[:, kt], ACT.Square).then_inc(S["sq"], 1)
                act.wait_ge(S["sq_used"], KT)
                act.activation(tb[:, 1, 0:SEQ], bank[5][:, 0:SEQ], ACT.Sqrt, scale=1.0 / D, bias=eps_col)\
                    .then_inc(S["root"], 1)
                for n in range(4):
                    act.wait_ge(S["ln_scaled"], n + 1)
                    act.activation(self.g[:, n], self.g[:, n], ACT.Silu, bias=pcol("ln_b", n, n + 1))\
                        .then_inc(S["ln_act"], 1)
                    act.wait_ge(S["ln_act"], n + 1)
                    act.activation(self.ohi[:, n], self.g[:, n], ACT.Copy).then_inc(S["ln_hi"], 1)
                for kt in range(KT):
                    act.wait_ge(S["scaled"], kt + 1)
                    act.activation(self.ohi[:, 4 + kt], self.yz[:, kt], ACT.Copy).then_inc(S["hi"], 1)

            def dve(self, dve):
                S, g0 = self.sem, self.proj.g0
                for c in range(17):
                    make_rest(g0 + c + 1)
                    if c < 4:
                        dve.wait_ge(S["pads"], 4)
                        dve.wait_ge(S["sigmoid"], c + 1)
                        dve.tensor_tensor(self.gp[:, c, CONV_K // 2:CONV_K // 2 + SEQ], bank[2 * c % 4][:, 0:SEQ],
                                          ta[:, c % 2, 0:SEQ], ALU.mult).then_inc(S["glu"], 1)
                        if c == 1:
                            dve.wait_ge(S["glu"], 2)
                    else:
                        for j in range(5 * (c - 4), 5 * (c - 3)):
                            self.dve_tap(dve, j)
                    dt = self.dt
                    if c == 5:
                        dve.wait_ge(proj_taken, self.base + 2)
                        for m in range(2):
                            cols = slice(32 * m, 32 * m + 32)
                            ins = dve.tensor_tensor(dt[:, 0, cols], dt[:, 0, cols], pcol("dt_bias"), ALU.add)
                            link(dve, ins)
                        dve.scalar_tensor_tensor(dt[:, 1], dt[:, 0], -1.0, dt[:, 0], ALU.mult, ALU.max)\
                            .then_inc(S["dt_exp"], 1)
                    if c == 6:
                        dve.wait_ge(S["dt_exp"], 2)
                        dve.tensor_scalar(dt[:, 2], dt[:, 1], 1.0, None, ALU.add).then_inc(S["dt_u"], 1)
                        dve.wait_ge(S["dt_u"], 1)
                        link(dve, dve.tensor_scalar(dt[:, 4], dt[:, 2], -1.0, None, ALU.add))
                        link(dve, dve.tensor_tensor(dt[:, 4], dt[:, 1], dt[:, 4], ALU.subtract))
                        link(dve, dve.reciprocal(dt[:, 5], dt[:, 2]))
                        link(dve, dve.tensor_tensor(dt[:, 4], dt[:, 4], dt[:, 5], ALU.mult))
                        dve.wait_ge(S["dt_log"], 1)
                        link(dve, dve.tensor_tensor(dt[:, 4], dt[:, 4], dt[:, 3], ALU.add))
                        link(dve, dve.scalar_tensor_tensor(dt[:, 3], dt[:, 0], 0.0, dt[:, 4], ALU.max, ALU.add))
                        dve.wait_ge(S["a_exp"], 1)
                        for m in range(2):
                            cols = slice(32 * m, 32 * m + 32)
                            dve.scalar_tensor_tensor(dt[:, 5, cols], dt[:, 3, cols], -1.0, self.ea[:], ALU.mult,
                                                     ALU.mult).then_inc(S["a_ready"], 1)
                    if c >= 8:
                        for idx in range(2 * (c - 8), min(2 * (c - 8) + 2, 16)):
                            self.conv(dve, idx)
                dve.wait_ge(const_landed, 16 * self.const)
                dve.wait_ge(S["cum_taken"], 1)
                for hh in range(SSM_H):
                    self.decays(dve, hh)
                    if hh:
                        self.maps(dve, hh - 1)
                    if hh == 8:
                        self.centre(dve)
                self.maps(dve, SSM_H - 1)
                dve.wait_ge(S["ln_root"], 1)
                link(dve, dve.reciprocal(sd[:, 0:SEQ], sd[:, 0:SEQ]))
                for n in range(4):
                    dve.scalar_tensor_tensor(self.g[:, n], self.g[:, n], pcol("ln_g", n, n + 1), sd[:, 0:SEQ], ALU.mult,
                                             ALU.mult).then_inc(S["ln_scaled"], 1)
                dve.wait_ge(S["root"], 1)
                link(dve, dve.reciprocal(tb[:, 1, 0:SEQ], tb[:, 1, 0:SEQ]))
                for n in range(4):
                    dve.wait_ge(S["ln_hi"], n + 1)
                    dve.tensor_tensor(self.olo[:, n], self.g[:, n], self.ohi[:, n].bitcast(F32), ALU.subtract)\
                        .then_inc(S["ln_lo"], 1)
                for kt in range(KT):
                    dve.scalar_tensor_tensor(self.yz[:, kt], self.yz[:, kt], pcol("ssm_norm", kt, kt + 1),
                                             tb[:, 1, 0:SEQ], ALU.mult, ALU.mult).then_inc(S["scaled"], 1)
                for kt in range(KT):
                    dve.wait_ge(S["hi"], kt + 1)
                    dve.tensor_tensor(self.olo[:, 4 + kt], self.yz[:, kt], self.ohi[:, 4 + kt].bitcast(F32),
                                      ALU.subtract).then_inc(S["lo"], 1)

            def decays(self, dve, hh):
                S = self.sem
                dve.wait_ge(S["rowsum"], hh + 1)
                if hh >= 2:
                    dve.wait_ge(S["maps"], hh - 1)
                ps = bank[6 + hh % 2]
                for (st, a, b), o, way in zip(self.SPANS, self.OFFSETS, (0, 0, 1, 1)):
                    mask = self.tri[:, way, 0:b - a] if way == 0 else self.tri[:, way, SEQ - (b - a):]
                    ins = dve.scalar_tensor_tensor(self.seg[:, hh % 2, o:o + b - a], ps[:, way * SEQ + a:way * SEQ + b],
                                                   self.cols[:, way, st, hh:hh + 1], mask, ALU.subtract, ALU.add)
                ins.then_inc(S["seg_ready"], 1)

            def maps(self, dve, hh):
                S = self.sem
                dve.wait_ge(S["decay"], hh + 1)
                dve.wait_ge(S["cb"], hh // 4 + 1)
                if hh >= 2:
                    dve.wait_ge(S["y_ps"], hh - 1)
                for (st, a, b), o, way in zip(self.SPANS, self.OFFSETS, (0, 0, 1, 1)):
                    dt = self.dt[:, 3, 32 * st + 16 * way + hh:32 * st + 16 * way + hh + 1]
                    ins = dve.scalar_tensor_tensor(self.m[:, hh % 2, o:o + b - a], self.seg[:, hh % 2, o:o + b - a], dt,
                                                   bank[4 + hh // 4 % 2][:, st * SEQ + a:st * SEQ + b], ALU.mult,
                                                   ALU.mult)
                ins.then_inc(S["maps"], 1)
                if hh % 2 == 0 and hh:
                    self.gate(dve, hh // 2 - 1)
                if hh == SSM_H - 1:
                    self.gate(dve, KT - 1)

            def gate(self, dve, kt):
                S = self.sem
                dve.wait_ge(S["y_ps"], 2 * kt + 2)
                link(dve, dve.scalar_tensor_tensor(self.yz[:, kt], self.x[:, 8 + kt], pcol("skip", kt, kt + 1),
                                                   bank[kt % 2][:, 0:SEQ], ALU.mult, ALU.add))
                dve.tensor_tensor(self.yz[:, kt], self.yz[:, kt], self.z[:, kt], ALU.mult).then_inc(S["y_taken"], 1)

            def centre(self, dve):
                S = self.sem
                dve.wait_ge(S["ln_sum"], 1)
                for n in range(4):
                    dve.scalar_tensor_tensor(self.g[:, n], bank[3][:, 0:SEQ], -1.0 / 512, self.g[:, n], ALU.mult,
                                             ALU.add).then_inc(S["ln_centred"], 1)

            def pe(self, pe):
                S = self.sem
                for c in range(17):
                    self.proj.pe_chunk(c, c == 0)
                pe.wait_ge(const_landed, 16 * self.const)
                pe.wait_ge(S["a_ready"], 2)
                a = lambda kt, c0, c1: self.dt[:, 5, 32 * kt + c0:32 * kt + c1]
                for way in range(2):
                    for lt in range(2):
                        o = (2 * way + lt) * SSM_H
                        for kt in range(2):
                            ins = pe.matmul(bank[6][:, o:o + SSM_H], self.sums[:, way, kt, lt * P:(lt + 1) * P],
                                            a(kt, way * SSM_H, (way + 1) * SSM_H), start=kt == 0, stop=kt == 1)
                ins.then_inc(S["cum_ready"], 1)
                pe.wait_ge(S["x_done"], 16)
                pe.wait_ge(proj_taken, self.base + self.proj.n - 8)
                for n in range(4):
                    if n >= 2:
                        pe.wait_ge(S["xt_ready"], n - 1)
                    for k in range(4):
                        ins = pe.transpose(bank[2 + n % 2][:, k * P:(k + 1) * P],
                                           self.x[:, 8 + n % 2 * 4 + k, n // 2 * P:(n // 2 + 1) * P], ident[:])
                    ins.then_inc(S["turned"], 1)
                self.c_dot_b(pe, 0)
                pe.wait_ge(S["cum_taken"], 1)
                self.row_sums(pe, 0, a)
                pe.wait_ge(S["xt_ready"], 4)
                pe.wait_ge(S["glu_dve"], 2 * CONV_K)
                pe.wait_ge(S["glu_pool"], 2 * CONV_K)
                for n in range(4):
                    ins = pe.matmul(bank[3][:, 0:SEQ], ones[:], self.g[:, n], start=n == 0, stop=n == 3)
                ins.then_inc(S["ln_sum"], 1)
                for hh in range(SSM_H):
                    if hh + 1 < SSM_H:
                        self.row_sums(pe, hh + 1, a)
                    if hh % 4 == 2 and hh < 12:
                        self.c_dot_b(pe, hh // 4 + 1)
                    kt, r = hh // 2, heads_in(hh)
                    pe.wait_ge(S["maps"], hh + 1)
                    if kt >= 2 and hh % 2 == 0:
                        pe.wait_ge(S["y_taken"], kt - 1)
                    for n, ((st, a0, b0), o) in enumerate(zip(self.SPANS, self.OFFSETS)):
                        ins = pe.matmul(bank[kt % 2][r, a0:b0], self.xt[:, st, hh * HD:(hh + 1) * HD],
                                        self.m[:, hh % 2, o:o + b0 - a0], start=n == 0, stop=n == 3)
                    ins.then_inc(S["y_ps"], 1)
                for n in range(4):
                    pe.wait_ge(S["ln_sq"], n + 1)
                    if n == 0:
                        pe.wait_ge(S["maps"], SSM_H)
                    pe.matmul(bank[4][:, 0:SEQ], ones[:], sq[:, n % 2, 0:SEQ], start=n == 0, stop=n == 3)\
                        .then_inc(S["ln_var"], 1)
                for kt in range(KT):
                    pe.wait_ge(S["sq"], kt + 1)
                    pe.matmul(bank[5][:, 0:SEQ], ones[:], sq[:, kt % 2, 0:SEQ], start=kt == 0, stop=kt == KT - 1)\
                        .then_inc(S["sq_used"], 1)

            def c_dot_b(self, pe, g):
                S = self.sem
                if g >= 2:
                    pe.wait_ge(S["maps"], 4 * (g - 1))
                for st in range(2):
                    ins = pe.matmul(bank[4 + g % 2][:, st * SEQ:(st + 1) * SEQ], self.x[:, g, st * P:(st + 1) * P],
                                    self.x[:, 4 + g], start=True, stop=True)
                ins.then_inc(S["cb"], 1)

            def row_sums(self, pe, hh, a):
                S = self.sem
                if hh >= 2:
                    pe.wait_ge(S["seg_ready"], hh - 1)
                for way in range(2):
                    for kt in range(2):
                        col_ = a(kt, way * SSM_H + hh, way * SSM_H + hh + 1)
                        ins = pe.matmul(bank[6 + hh % 2][:, way * SEQ:(way + 1) * SEQ], col_.to_broadcast([P, P]),
                                        self.sums[:, way, kt], start=kt == 0, stop=kt == 1)
                ins.then_inc(S["rowsum"], 1)

            def out(self, pe):
                def ready():
                    pe.wait_ge(self.sem["ln_lo"], 4)
                    pe.wait_ge(self.sem["lo"], KT)

                out_pe(self.s, lambda k, n: self.ohi[:, k, 0:n], lambda k, n: self.olo[:, k, 0:n], ready)

        mixers[10] = Odd()

        block = ctx.enter_context(nc.Block())

        @block.sync
        def _(sp):
            sp.dma_start(par[:], t["params"]).then_inc(par_landed, 16)
            sp.dma_start(ident[:], t["identity"]).then_inc(par_landed, 16)
            for name, src, row, n, cols in plan:
                g0 = first_chunk[name]
                for j in range(n):
                    load_chunk(sp, name, src, row, g0, j, None)
                    s = {("in1", 5): 1, ("in4", 5): 4, ("in7", 5): 7, ("in10b", 1): 10}.get((name, j))
                    if s in mixers:
                        sp.wait_ge(w_used, first_chunk[f"in{s}"])
                        mixers[s].loads(sp)
                if name == "ada0_0":
                    sp.dma_start(h[:], t["tokens"]).then_inc(in_landed, 16)
            last = subs[-1]
            for kt in range(KT):
                await_h(sp, last, kt)
                sp.dma_start(out[:, kt], h[:, kt, 0:out.shape[2]]).then_inc(out_done, 16)
            sp.wait_ge(out_done, 16 * KT)

        @block.gpsimd
        def _(pool):
            for s in subs:
                if s in mixers:
                    mixers[s].pool(pool)
                out_pool(s)
                post_pool(s)

        @block.scalar
        def _(act):
            act.wait_ge(par_landed, 32)
            silu_in = pcol("silu_in").rearrange("p (k c) -> p k c", c=2)
            act.wait_ge(const_ready, 3)
            act.activation(cond4[:, 0, :, 0:2], silu_in, ACT.Silu).then_inc(cond_ready, 1)
            act.activation(cond4[:, 1, :, 2:4], silu_in, ACT.Silu).then_inc(cond_ready, 1)
            attention_setup_act(act)
            act.wait_ge(in_landed, 16)
            mod_copy(0, 0)
            norm_act(0, 0, BOTH)
            mod_copy(0, 1)
            make_high(first_chunk["in0"])
            mod_copy(0, 2)
            pre_act(0, BOTH)
            for s in subs:
                if s in mixers:
                    mixers[s].act(act)
                else:
                    ffn_in_act(s)
                out_act(s)
                if s != subs[-1]:
                    norm_act(s + 1, round_h(s), width_in(s + 1))
                    if behind(s):
                        mod_copy(*behind(s)[0])
                        make_high(first_chunk[f"in{s + 1}"])
                        mod_copy(*behind(s)[1])
                    pre_act(s + 1, width_in(s + 1))

        @block.vector
        def _(dve):
            dve.memset(small[:, 0:1], EPS).then_inc(const_ready, 1)
            dve.memset(cond4[:], 0.0).then_inc(const_ready, 1)
            dve.memset(ones[:], 1.0).then_inc(const_ready, 1)
            dve.wait_ge(par_landed, 32)
            for s in range(6, 12):
                for c in range(2):
                    ins = dve.tensor_scalar(G[:, s, :, c],
                                            pcol("gain2", (2 * (s - 6) + 1) * KT, (2 * (s - 6) + 2) * KT),
                                            1.0 if s % 3 == 1 else 0.5, None, ALU.mult)
            link(dve, ins)
            attention_setup_dve(dve)
            take_mod(0, 0)
            invert(0, BOTH)
            take_mod(0, 1)
            make_rest(first_chunk["in0"])
            await_mod(dve, 0, 1)
            pre_dve(0, BOTH)
            take_mod(0, 2)
            for s in subs:
                if s in mixers:
                    mixers[s].dve(dve)
                else:
                    ffn_in_dve(s)
                out_dve(s)
                if s < 6:
                    await_mod(dve, s, 2)
                post_dve(s)
                if s == subs[-1]:
                    continue
                groups = behind(s)
                invert(round_h(s), width_in(s + 1))
                if groups:
                    take_mod(*groups[0])
                    make_rest(first_chunk[f"in{s + 1}"])
                if s == 0:
                    take_mod(*groups[1])
                if s < 5:
                    await_mod(dve, s + 1, 1)
                pre_dve(s + 1, width_in(s + 1))
                if s and groups:
                    take_mod(*groups[1])

        @block.tensor
        def _(pe):
            pe.wait_ge(const_ready, 3)
            pe.wait_ge(par_landed, 32)
            pe.wait_ge(cond_ready, 2)
            mod_products(0, 0)
            mod_turn(0, 0)
            mod_products(0, 1)
            pre_pe(0, BOTH)
            mod_turn(0, 1)
            mod_products(0, 2)
            mod_turn(0, 2)
            for s in subs:
                if s in mixers:
                    mixers[s].pe(pe)
                    mixers[s].out(pe)
                else:
                    ffn_in_pe(s)
                    ffn_out_pe(s)
                groups = behind(s)
                if groups:
                    mod_products(*groups[0], range(2))
                if s != subs[-1]:
                    pre_pe(round_h(s), width_in(s + 1))
                if groups:
                    mod_products(*groups[0], range(2, 4))
                    mod_turn(*groups[0])
                    mod_products(*groups[1])
                    mod_turn(*groups[1])


def chunks_of(w, n=CHUNK):
    k, cols = w.shape
    return w.reshape(k // P, P, cols // n, n).transpose(2, 1, 0, 3).reshape(cols // n, P, k // P * n)


def ffn_in_chunks(a, b):
    both = np.stack([a.reshape(KT, P, FT, P), b.reshape(KT, P, FT, P)], axis=3)
    return both.transpose(2, 1, 0, 3, 4).reshape(FT, P, CHUNK_COLS)


def ffn_out_chunks(w):
    return w.reshape(2, HALF_FT, P, KT, P).transpose(3, 0, 2, 1, 4).reshape(2 * KT, P, OUT_COLS)


def col(v):
    return np.ascontiguousarray(v.reshape(-1, P).T)


def twice(v):
    return np.repeat(v, 2, axis=1)


def rows(v):
    return np.broadcast_to(v.reshape(1, -1), (P, v.size))


def toeplitz_bias(rpb):
    pad = np.zeros((NA_H, rpb.shape[1], 2 * GRID_W), rpb.dtype)
    lead = GRID_W - NA_WIN
    pad[:, :, lead:lead + rpb.shape[2]] = rpb
    row, qc, kc = np.arange(4), np.arange(GRID_W), np.arange(GRID_W)
    off_r = row[None, :] - row[:, None] + 7
    off_c = kc[None, :] - qc[:, None] + GRID_W - 1
    b = pad[:, off_r[:, None, :, None], off_c[None, :, None, :]]
    return b.reshape(NA_H, 2, P, SEQ).transpose(2, 0, 1, 3).reshape(P, NA_H * 2 * SEQ)


def constants():
    p = np.arange(P)
    t_ = np.arange(SEQ)
    d = p % HD
    freq = (np.float32(10000.0) ** (-np.arange(16, dtype=np.float32) / np.float32(16))).astype(np.float32)
    pos = np.stack([t_ // GRID_W, t_ % GRID_W]).astype(np.float32)
    ang1 = pos[d // 32] * freq[d % 16][:, None]
    rot1 = np.zeros((P, P), np.float32)
    for i in p:
        if i % 32 < 16:
            rot1[i + 16, i] = -1.0
        else:
            rot1[i - 16, i] = 1.0
    inv = (np.float32(1.0) / (np.float32(10000.0) ** (np.arange(0, HD, 2, dtype=np.float32) / np.float32(HD))))
    ang2 = t_.astype(np.float32)[None, :] * inv.astype(np.float32)[d % 32][:, None]
    rot2 = np.zeros((P, P), np.float32)
    for i in p:
        if i % HD < 32:
            rot2[i + 32, i] = -1.0
        else:
            rot2[i - 32, i] = 1.0
    qc, kc = p % GRID_W, t_ % GRID_W
    start = np.clip(qc - NA_WIN // 2, 0, GRID_W - NA_WIN)
    near = (kc[None] >= start[:, None]) & (kc[None] < start[:, None] + NA_WIN)
    na_mask = np.where(near, 0.0, NEG).astype(np.float32)
    q = np.arange(SEQ)
    ev = np.where(np.abs(q[:, None] - t_[None]) <= 128, 0.0, FAR).astype(np.float32)
    ev_mask = ev.reshape(2, P, SEQ).transpose(1, 0, 2)
    pool = []
    for w in (2, 4, 8, 16):
        lo, hi = np.clip(t_ - w // 2, 0, SEQ), np.clip(t_ + w - w // 2, 0, SEQ)
        inside = (t_[:, None] >= lo[None]) & (t_[:, None] < hi[None])
        pool.append(inside / (hi - lo)[None].astype(np.float32) - np.eye(SEQ))
    pool = np.stack(pool).astype(np.float32).reshape(4, 2, P, SEQ).transpose(2, 0, 1, 3)
    le = (t_[:, None] <= t_[None]).astype(np.float32)
    sums = np.stack([le, le.T]).reshape(2, 2, P, SEQ).transpose(2, 0, 1, 3)
    whole = np.zeros((P, P))
    tri = np.stack([np.concatenate([np.where(p[:, None] <= p[None], 0.0, FAR), whole], axis=1),
                    np.concatenate([whole, np.where(p[:, None] >= p[None], 0.0, FAR)], axis=1)])
    tri = tri.astype(np.float32).transpose(1, 0, 2)
    f = np.float32
    return {
        "identity": np.eye(P, dtype=f),
        "rope1": np.concatenate([rot1, np.cos(ang1).astype(f), np.sin(ang1).astype(f)], axis=1),
        "rope2": np.concatenate([rot2, np.cos(ang2).astype(f), np.sin(ang2).astype(f)], axis=1),
        "na_mask": na_mask,
        "ev_const": np.concatenate([ev_mask.reshape(P, -1), pool.reshape(P, -1)], axis=1),
        "od_const": np.concatenate([sums.reshape(P, -1), tri.reshape(P, -1)], axis=1),
    }


def kernel(**inputs):
    import concourse.bacc as bacc
    from concourse.bass_utils import run_bass_kernel_spmd

    v = {k: np.asarray(a) for k, a in inputs.items()}
    f = np.float32
    cat = np.concatenate
    hd = np.arange(HD)
    q_cols = cat([h * HD + hd for h in EV_HEADS])
    ev_in, ev_out = v["ev_w_in_2"][0], v["ev_w_out_2"][0]
    od_in = v["od_w_in_2"][0]
    glu = cat([od_in[:, c * 512 + n * P:c * 512 + (n + 1) * P] for n in range(4) for c in range(2)], axis=1)
    layers = [(0, 0), (0, 1), (1, 0), (1, 1)]
    ada = v["ada_w"]
    arrays = {
        "tokens": np.ascontiguousarray(cat([v["x"][0], v["ctx"][0]]).T.reshape(KT, P, BOTH).transpose(1, 0, 2)),
        "w_ada": cat([chunks_of(ada[0]), chunks_of(ada[1])]),
        "w_ffn_in": cat([ffn_in_chunks(v["ffn_w_in"][a, b][:, :DFF], v["ffn_w_in"][a, b][:, DFF:]) for a, b in layers]
                        + [ffn_in_chunks(v["ffn_w_gate_2"][a, b], v["ffn_w_up_2"][a, b]) for a, b in layers]),
        "w_ffn_out": cat([ffn_out_chunks(v["ffn_w_out"][a, b]) for a, b in layers]
                         + [ffn_out_chunks(v["ffn_w_down_2"][a, b]) for a, b in layers]),
        "w_mix": cat([chunks_of(w) for w in (
            v["da_w_in"][0], v["da_w_out"][0], v["na_w_in"][0], v["na_w_out"][0],
            ev_in[:, :256], ev_in[:, 1280:1536], ev_in[:, 256:1024][:, q_cols], ev_in[:, 1024:1280],
            cat([ev_out[:256], ev_out[256:][q_cols]]),
            glu, od_in[:, 3072:4096], od_in[:, 2048:3072], od_in[:, 1024:2048])]),
        "w_dt": chunks_of(od_in[:, 4096:4128], 2 * SSM_H),
        "w_od_out": chunks_of(v["od_w_out_2"][0], P),
        "na_bias": toeplitz_bias(v["na_rpb"][0]),
        "pool_w": np.ascontiguousarray(v["ev_pool_w_2"][0].reshape(2, P, HD).transpose(1, 0, 2).reshape(P, 2 * HD)),
    }
    parts = {
        "silu_in": np.stack([col(v["c"][0]), col(v["c_ctx"])], axis=2).reshape(P, -1),
        "gain": twice(col(v["norm_g"])),
        "gain2": col(v["norm_w_2"]),
        "ada_b": twice(col(v["ada_b"])),
        "lam": rows(v["da_lambda"][0]),
        "subln": col(v["da_subln_g"][0]),
        "sink": rows(v["ev_sink_2"][0][EV_HEADS]),
        "pool_scale": col(v["ev_pool_scale_2"][0]),
        "dw_w": v["cv_dw_w_2"][0].reshape(CONV_K, 4, P).transpose(2, 1, 0).reshape(P, -1),
        "dw_b": col(v["cv_dw_b_2"][0]),
        "ln_g": col(v["cv_ln_g_2"][0]),
        "ln_b": col(v["cv_ln_b_2"][0]),
        "cw": np.roll(v["ssm_conv_w_2"][0].reshape(4, 16, P), 8, axis=1).transpose(2, 1, 0).reshape(P, -1),
        "cb": np.roll(col(v["ssm_conv_b_2"][0]), 8, axis=1),
        "a_log": rows(v["ssm_A_log_2"][0]),
        "dt_bias": rows(v["ssm_dt_bias_2"][0]),
        "skip": np.repeat(v["ssm_D_2"][0].reshape(KT, 2), HD, axis=1).T,
        "ssm_norm": col(v["ssm_norm_w_2"][0]),
    }
    columns, n_columns = param_columns()
    params = np.zeros((P, n_columns), f)
    for name, (o, n) in columns.items():
        params[:, o:o + n] = parts[name]
    arrays["params"] = params
    arrays.update(constants())
    arrays = {name: np.ascontiguousarray(a) for name, a in arrays.items()}

    nc = bacc.Bacc("TRN2", target_bir_lowering=False, num_devices=1, dynamic_dma_scratch_size=1024)
    t = {name: nc.dram_tensor(f"in_{name}", a.shape, mybir.dt.from_np(a.dtype), kind="ExternalInput").ap()
         for name, a in arrays.items()}
    out = nc.dram_tensor("out_x", (P, KT, SEQ), F32, kind="ExternalOutput").ap()
    build_program(nc, t, out)
    r = run_bass_kernel_spmd(nc, [{f"in_{name}": a for name, a in arrays.items()}], core_ids=[0])
    got = r.results[0]["out_x"]
    return got.transpose(2, 1, 0).reshape(1, SEQ, D)
```

```python
from contextlib import ExitStack

import numpy as np

import concourse.bass as bass
from concourse import mybir

F32 = mybir.dt.float32
F32R = mybir.dt.float32r
ACT = mybir.ActivationFunctionType
ALU = mybir.AluOpType
AX_X = mybir.AxisListType.X

P = 128
D = 1024
KT = D // P
SEQ = 256
CTX = 256
BOTH = SEQ + CTX
DFF = 2816
FT = DFF // P
HALF_FT = FT // 2
EPS = 1e-6
HD = 64
CHUNK = 2 * P
CHUNK_COLS = KT * CHUNK
OUT_COLS = HALF_FT * P
N_MOD = 9
GRID_W = 64
NA_H, NA_WIN = 16, 16
EV_QH = 12
CONV_K = 31
SSM_H = 16
NEG = -1e9
FAR = -1e30
RAW_RING, PART_RING = 4, 2
WARM = 18, 16
POOL_RESTS = [2, 5]
DVE_ADDS = [2, 5, 7]
EV_HEADS = [0, 3, 1, 4, 2, 5, 6, 9, 7, 10, 8, 11]


def param_columns():
    sizes = [("silu_in", KT * 2), ("gain", 12 * KT * 2), ("gain2", 12 * KT), ("ada_b", 2 * N_MOD * KT * 2),
             ("lam", 4 * HD), ("subln", 1), ("sink", EV_QH), ("pool_scale", 2), ("dw_w", 4 * CONV_K),
             ("dw_b", 4), ("ln_g", 4), ("ln_b", 4), ("cw", 16 * 4), ("cb", 16), ("a_log", 2 * SSM_H),
             ("dt_bias", 2 * SSM_H), ("skip", KT), ("ssm_norm", KT)]
    at, out = 0, {}
    for name, n in sizes:
        out[name] = (at, n)
        at += n
    return out, at


def weight_plan():
    plan = []

    def ada(layer, m):
        plan.append((f"ada{layer}_{m}", "w_ada", (layer * N_MOD + m) * 4, 4, CHUNK_COLS))

    def ffn(s):
        n = s // 3 * 2 + (s % 3 == 2)
        plan.append((f"in{s}", "w_ffn_in", n * FT, FT, CHUNK_COLS))
        plan.append((f"out{s}", "w_ffn_out", n * 2 * KT, 2 * KT, OUT_COLS))

    for m in (0, 1, 2):
        ada(0, m)
    ffn(0)
    for m in (3, 4):
        ada(0, m)
    plan.append(("in1", "w_mix", 0, 12, CHUNK_COLS))
    for m in (5, 6, 7, 8):
        ada(0, m)
    plan.append(("out1", "w_mix", 12, 4, CHUNK_COLS))
    for m in (0, 1):
        ada(1, m)
    ffn(2)
    for m in (2, 3):
        ada(1, m)
    ffn(3)
    for m in (4, 5):
        ada(1, m)
    plan.append(("in4", "w_mix", 16, 12, CHUNK_COLS))
    for m in (6, 7, 8):
        ada(1, m)
    plan.append(("out4", "w_mix", 28, 4, CHUNK_COLS))
    ffn(5)
    ffn(6)
    plan.append(("in7", "w_mix", 32, 6, CHUNK_COLS))
    plan.append(("out7", "w_mix", 38, 4, CHUNK_COLS))
    ffn(8)
    ffn(9)
    plan.append(("in10", "w_mix", 42, 4, CHUNK_COLS))
    plan.append(("dt10", "w_dt", 0, 1, KT * 2 * SSM_H))
    plan.append(("in10b", "w_mix", 46, 12, CHUNK_COLS))
    plan.append(("out10", "w_od_out", 0, KT, 12 * P))
    ffn(11)
    return plan


def at(base, step, i):
    return base if i is None else i * step + base


def build_program(nc, t, out):
    plan = weight_plan()
    chunk_cols, first_chunk = [], {}
    for name, _, _, n, cols in plan:
        first_chunk[name] = len(chunk_cols)
        chunk_cols += [cols] * n
    parted = [g for name, _, _, n, _ in plan if not name.startswith("ada")
              for g in range(first_chunk[name], first_chunk[name] + n)]
    part_of = {g: q for q, g in enumerate(parted)}
    columns, n_columns = param_columns()
    subs = list(range(12))

    with ExitStack() as ctx:
        top = [(nc.sbuf_base + 31) // 32 * 32]

        def place(name, shape, dt, offset=None):
            size = (int(np.prod(shape[1:])) * 4 + 31) // 32 * 32
            where = top[0] if offset is None else offset
            if offset is None:
                top[0] += size
            assert where + size <= nc.sbuf_usable_end, (name, where + size, nc.sbuf_usable_end)
            return nc.alloc_sbuf_tensor_at(name, shape, dt, offset=where)

        def sem(name):
            return ctx.enter_context(nc.semaphore(name))

        raw = place("w_raw", [P, RAW_RING, CHUNK_COLS], F32)
        whi = place("w_high", [P, PART_RING, CHUNK_COLS], F32R)
        wlo = place("w_rest", [P, PART_RING, CHUNK_COLS], F32R)
        h = place("residual", [P, KT, BOTH], F32)
        u_at = top[0]
        uhi = place("u_high", [P, KT, BOTH], F32R)
        ulo = place("u_rest", [P, KT, BOTH], F32R)
        y = place("sublayer_out", [P, KT, BOTH], F32, offset=u_at)
        mix_at = top[0]
        ghi = place("gated_high", [P, FT, BOTH], F32R)
        glo = place("gated_rest", [P, FT, BOTH], F32R)
        mix_end = top[0]
        sq = place("squares", [P, 2, BOTH], F32)
        ta = place("work_a", [P, 2, BOTH], F32)
        tb = place("work_b", [P, 2, BOTH], F32)
        sd, rinv = tb[:, 0], tb[:, 1]
        par = place("params", [P, n_columns], F32)
        A = place("pre_scale", [P, 6, KT, 2], F32)
        B = place("pre_shift", [P, 6, KT, 2], F32)
        G = place("post_scale", [P, 12, KT, 2], F32)
        cond4 = place("cond_silu", [P, 2, KT, 4], F32)
        mod_rows = place("mod_rows", [P, 4 * P], F32)[0:4, :]
        msum = place("mod_sum", [P, KT, 2], F32)
        ones = place("ones", [P, P], F32)
        small = place("small", [P, 16], F32)
        table_out = place("table_out", [P, 24], F32)

        def pcol(name, a=0, b=None):
            o, n = columns[name]
            return par[:, o + a:o + (n if b is None else b)]

        bank = [ctx.enter_context(nc.psum_tensor(f"bank{n}", [P, 512], F32)) for n in range(8)]
        stat, mod = bank[4], bank[5]

        in_landed = sem("in_landed")
        par_landed = sem("par_landed")
        raw_landed = [sem(f"raw_landed{n}") for n in range(RAW_RING)]
        w_hi_ready = sem("w_hi_ready")
        w_lo_ready = sem("w_lo_ready")
        w_used = sem("w_used")
        const_ready = sem("const_ready")
        cond_ready = sem("cond_ready")
        mod_copied = sem("mod_copied")
        mod_turned = sem("mod_turned")
        mod_read = sem("mod_read")
        dve_step = sem("dve_step")
        act_step = sem("act_step")
        silu_done = sem("silu_done")
        gate_done = sem("gate_done")
        ghi_done = sem("ghi_done")
        glo_done = sem("glo_done")
        sq_ready = sem("sq_ready")
        sq_used = sem("sq_used")
        sd_ready = sem("sd_ready")
        rinv_ready = sem("rinv_ready")
        y_ready = sem("y_ready")
        post_ready = sem("post_ready")
        h_ready_pool = sem("h_ready_pool")
        h_ready_dve = sem("h_ready_dve")
        pre_ready = sem("pre_ready")
        uhi_ready = sem("uhi_ready")
        ulo_by_dve = sem("ulo_by_dve")
        ulo_by_pool = sem("ulo_by_pool")
        out_done = sem("out_done")

        chain = {"dve": 0, "act": 0, "table": 0}

        def link(eng, ins):
            which, s = ("dve", dve_step) if eng is nc.vector else ("act", act_step)
            chain[which] += 1
            ins.then_inc(s, 1)
            eng.wait_ge(s, chain[which])

        def width(s):
            return BOTH if s <= 3 else SEQ

        def width_in(s):
            return BOTH if s <= 4 else SEQ

        def halves(n):
            return [(0, slice(0, SEQ)), (1, slice(SEQ, BOTH))][:n // SEQ]

        def round_y(s):
            return 2 * s + 1

        def round_h(s):
            return 2 * s + 2

        ada_index = {}
        for name, *_ in plan:
            if name.startswith("ada"):
                ada_index[name] = len(ada_index)

        def behind(s):
            if s == subs[-1]:
                return []
            return {0: [(0, 3), (0, 4)], 1: [(1, 0), (1, 1)], 2: [(1, 2), (1, 3)], 3: [(1, 4), (1, 5)]}.get(s, [])

        def await_mod(eng, s, m):
            eng.wait_ge(mod_read, ada_index[f"ada{s // 3}_{3 * (s % 3) + m}"] + 1)

        def ring_loop(eng, n, body, peel=RAW_RING):
            for j in range(min(n, peel)):
                body(j, None)
            turns = (n - 1 - peel) // RAW_RING
            if turns > 0:
                with eng.Fori(0, turns) as i:
                    for j in range(peel, peel + RAW_RING):
                        body(j, i)
            for j in range(peel + RAW_RING * max(turns, 0), n):
                body(j, None)

        def load_chunk(sp, name, src, row, g0, j, i):
            g = g0 + j
            if g >= RAW_RING:
                old = g - RAW_RING
                if old in part_of:
                    sp.wait_ge(w_lo_ready, part_of[old] + 1)
                else:
                    sp.wait_ge(w_used, old + 1)
            n = chunk_cols[g]
            sp.dma_start(raw[:, g % RAW_RING, 0:n], t[src][row + j]).then_inc(raw_landed[g % RAW_RING], 16)

        rest_by_pool = {first_chunk[f"in{s}"] + 1 for s in subs if s == 0 or behind(s - 1)}
        made_ahead = {first_chunk[f"in{s}"] + 1 for s in subs}

        def make_high(g, i=None, ahead=False):
            if g not in part_of or (g in made_ahead) != ahead:
                return
            q = part_of[g]
            nc.scalar.wait_ge(raw_landed[g % RAW_RING], at(16 * (g // RAW_RING + 1), 16, i))
            if q >= PART_RING:
                nc.scalar.wait_ge(w_used, at(parted[q - PART_RING] + 1, RAW_RING, i))
            n = chunk_cols[g]
            nc.scalar.activation(whi[:, q % PART_RING, 0:n], raw[:, g % RAW_RING, 0:n], ACT.Copy)\
                .then_inc(w_hi_ready, 1)

        def make_rest(g, i=None, ahead=False):
            if g not in part_of or (g in made_ahead) != ahead:
                return
            q, eng = part_of[g], nc.gpsimd if g in rest_by_pool else nc.vector
            eng.wait_ge(w_hi_ready, at(q + 1, RAW_RING, i))
            if g in rest_by_pool or g - 1 in rest_by_pool:
                eng.wait_ge(w_lo_ready, q)
            n = chunk_cols[g]
            eng.tensor_tensor(wlo[:, q % PART_RING, 0:n], raw[:, g % RAW_RING, 0:n],
                              whi[:, q % PART_RING, 0:n].bitcast(F32), ALU.subtract).then_inc(w_lo_ready, 1)

        def await_parts(g, i=None):
            nc.tensor.wait_ge(w_lo_ready, at(part_of[g] + 1, RAW_RING, i))

        def block_of(part, g, kt, m, cols=CHUNK):
            return part[:, part_of[g] % PART_RING, kt * cols + m * P:kt * cols + (m + 1) * P]

        def products(ps, g, kts, weights, acts_hi, acts_lo, first=True, last=True):
            pe = nc.tensor
            kts = list(kts)
            for n, kt in enumerate(kts):
                hi, lo = weights(whi, kt), weights(wlo, kt)
                a, b = acts_hi(kt), acts_lo(kt)
                pe.matmul(ps, hi, a, start=first and n == 0, stop=False)
                pe.matmul(ps, hi, b, start=False, stop=False)
                ins = pe.matmul(ps, lo, a, start=False, stop=last and n == len(kts) - 1)
            return ins

        def mod_products(layer, m, steps=range(4)):
            pe = nc.tensor
            g0, q = first_chunk[f"ada{layer}_{m}"], ada_index[f"ada{layer}_{m}"]
            for j in steps:
                g = g0 + j
                pe.wait_ge(raw_landed[g % RAW_RING], 16 * (g // RAW_RING + 1))
                if j == 0 and q:
                    pe.wait_ge(mod_read, q)
                c = CHUNK * (j % 2)
                for kt in range(KT):
                    ins = pe.matmul(mod[0:4, c:c + CHUNK], cond4[:, j // 2, kt, :],
                                    raw[:, g % RAW_RING, kt * CHUNK:(kt + 1) * CHUNK],
                                    start=j == 0 and kt == 0, stop=j == 3 and kt == KT - 1)
                ins.then_inc(w_used, 1)

        def mod_copy(layer, m):
            nc.scalar.wait_ge(w_used, first_chunk[f"ada{layer}_{m}"] + 4)
            nc.scalar.activation(mod_rows, mod[0:4, :], ACT.Copy).then_inc(mod_copied, 1)

        def mod_turn(layer, m):
            nc.tensor.wait_ge(mod_copied, ada_index[f"ada{layer}_{m}"] + 1)
            for k in range(KT // 2):
                ins = nc.tensor.transpose(mod[:, 4 * k:4 * k + 4], mod_rows[:, k * P:(k + 1) * P], ident[0:4, 0:4])
            ins.then_inc(mod_turned, 1)

        def take_mod(layer, m):
            dve = nc.vector
            dve.wait_ge(mod_turned, ada_index[f"ada{layer}_{m}"] + 1)
            ps = mod[:, 0:2 * KT].rearrange("p (k h c) -> p h k c", h=2, c=2)

            def split(ap):
                return ap.rearrange("p (h k) c -> p h k c", h=2)

            bias = pcol("ada_b", (layer * N_MOD + m) * 2 * KT, (layer * N_MOD + m + 1) * 2 * KT)\
                .rearrange("p (k c) -> p k c", c=2)
            s = 3 * layer + m // 3
            if m % 3 == 0:
                dve.tensor_tensor(split(B[:, s]), ps, split(bias), ALU.add).then_inc(mod_read, 1)
                return
            gain = pcol("gain", (2 * s + (m % 3 == 2)) * 2 * KT, (2 * s + 1 + (m % 3 == 2)) * 2 * KT)\
                .rearrange("p (k c) -> p k c", c=2)
            link(dve, dve.tensor_tensor(split(msum[:]), ps, split(bias), ALU.add))
            if m % 3 == 1:
                dve.scalar_tensor_tensor(A[:, s], msum[:], 1.0, gain, ALU.add, ALU.mult).then_inc(mod_read, 1)
            else:
                dve.scalar_tensor_tensor(G[:, s], msum[:], 0.5 if s % 3 != 1 else 1.0, gain, ALU.mult,
                                         ALU.mult).then_inc(mod_read, 1)

        def square(q, kt, src, n, i=None, step=0):
            k = 8 * q + kt
            if k >= 2 or i is not None:
                nc.scalar.wait_ge(sq_used, at(k - 1, step, i))
            dst = sq[:, kt % 2, 0:n] if i is None else sq[:, kt % 2:kt % 2 + 1, 0:n]
            nc.scalar.activation(dst, src, ACT.Square).then_inc(sq_ready, 1)

        def slots(ring, n):
            return (2, lambda k: ring[:, k % 2, 0:n]) if n > SEQ else \
                (4, lambda k: ring[:, k % 4 // 2, k % 2 * SEQ:(k % 2 + 1) * SEQ])

        def sum_squares(q, kt, n):
            pe = nc.tensor
            pe.wait_ge(sq_ready, 8 * q + kt + 1)
            if kt == 0 and q:
                pe.wait_ge(sd_ready, q)
            pe.matmul(stat[:, 0:n], ones[:], slots(sq, n)[1](kt), start=kt == 0, stop=kt == KT - 1)\
                .then_inc(sq_used, 1)

        def root(q, n):
            nc.scalar.wait_ge(sq_used, 8 * q + 8)
            nc.scalar.activation(sd[:, 0:n], stat[:, 0:n], ACT.Sqrt, scale=1.0 / D, bias=eps_col)\
                .then_inc(sd_ready, 1)

        def invert(q, n):
            nc.vector.wait_ge(sd_ready, q + 1)
            nc.vector.reciprocal(rinv[:, 0:n], sd[:, 0:n]).then_inc(rinv_ready, 1)
            nc.vector.wait_ge(rinv_ready, q + 1)

        eps_col = small[:, 0:1]

        def keep_warm(n):
            for _ in range(n):
                nc.tensor.matmul(bank[3][:, 0:P], ident[:], ident[:], start=True, stop=True)

        def load_table(func):
            n = chain["table"]
            chain["table"] += 1
            nc.scalar.activation(table_out[:, n:n + 1], eps_col, func)

        def pre_pe(q, n):
            for kt in range(KT):
                sum_squares(q, kt, n)

        def norm_act(s, q, n):
            ring, slot = slots(sq, n)
            for kt in range(KT):
                if s:
                    await_h(nc.scalar, s - 1, kt)
                if kt >= ring:
                    nc.scalar.wait_ge(sq_used, 8 * q + kt - ring + 1)
                nc.scalar.activation(slot(kt), h[:, kt, 0:n], ACT.Square).then_inc(sq_ready, 1)
            root(q, n)

        def pre_act(s, n):
            act = nc.scalar
            slot = slots(ta, n)[1]
            for kt in range(KT):
                act.wait_ge(pre_ready, 8 * s + kt + 1)
                if s < 6:
                    for c, sl in halves(n):
                        ins = act.activation(uhi[:, kt, sl], slot(kt)[:, sl], ACT.Identity, bias=B[:, s, kt, c:c + 1])
                else:
                    ins = act.activation(uhi[:, kt, 0:n], slot(kt), ACT.Copy)
                ins.then_inc(uhi_ready, 1)
                if kt == 1 and first_chunk[f"in{s}"] + 1 in rest_by_pool:
                    make_high(first_chunk[f"in{s}"] + 1, ahead=True)

        def pool_rests(s):
            return POOL_RESTS if s >= 6 else []

        def take_rest(eng, s, kt, n):
            eng.wait_ge(uhi_ready, 8 * s + kt + 1)
            slot = slots(ta, n)[1](kt)
            if s < 6:
                for c, sl in halves(n):
                    ins = eng.scalar_tensor_tensor(ulo[:, kt, sl], slot[:, sl], B[:, s, kt, c:c + 1],
                                                   uhi[:, kt, sl].bitcast(F32), ALU.add, ALU.subtract)
            else:
                ins = eng.tensor_tensor(ulo[:, kt, 0:n], slot, uhi[:, kt, 0:n].bitcast(F32), ALU.subtract)
            ins.then_inc(ulo_by_pool if kt in pool_rests(s) else ulo_by_dve, 1)

        def pre_pool(s, n):
            if first_chunk[f"in{s}"] + 1 in rest_by_pool:
                make_rest(first_chunk[f"in{s}"] + 1, ahead=True)
            for kt in pool_rests(s):
                take_rest(nc.gpsimd, s, kt, n)

        def await_u(eng, s, kt):
            mine = kt in pool_rests(s)
            count = sum((k in pool_rests(r)) == mine for r in range(s + 1) for k in range(KT) if (r, k) <= (s, kt))
            eng.wait_ge(ulo_by_pool if mine else ulo_by_dve, count)

        def pre_dve(s, n):
            dve = nc.vector
            ring, slot = slots(ta, n)
            for kt in range(KT):
                if kt >= ring:
                    await_u(dve, s, kt - ring)
                for c, sl in halves(n):
                    a = A[:, s, kt, c:c + 1] if s < 6 else pcol("gain2", (2 * (s - 6)) * KT + kt,
                                                               (2 * (s - 6)) * KT + kt + 1)
                    ins = dve.scalar_tensor_tensor(slot(kt)[:, sl], h[:, kt, sl], a, rinv[:, sl], ALU.mult, ALU.mult)
                ins.then_inc(pre_ready, 1)
                if kt and kt - 1 not in pool_rests(s):
                    take_rest(dve, s, kt - 1, n)
            take_rest(dve, s, KT - 1, n)

        def post_dve(s):
            dve = nc.vector
            n = width(s)
            invert(round_y(s), n)

            def add(kt):
                if kt in DVE_ADDS:
                    dve.wait_ge(post_ready, 8 * s + kt + 1)
                    dve.tensor_tensor(h[:, kt, 0:n], h[:, kt, 0:n], y[:, kt, 0:n], ALU.add).then_inc(h_ready_dve, 1)

            for kt in range(KT):
                for c, sl in halves(n):
                    ins = dve.scalar_tensor_tensor(y[:, kt, sl], y[:, kt, sl], G[:, s, kt, c:c + 1],
                                                   rinv[:, sl], ALU.mult, ALU.mult)
                ins.then_inc(post_ready, 1)
                add(kt - 1)
            add(KT - 1)

        def post_pool(s):
            pool = nc.gpsimd
            n = width(s)
            for kt in range(KT):
                if kt not in DVE_ADDS:
                    pool.wait_ge(post_ready, 8 * s + kt + 1)
                    pool.tensor_tensor(h[:, kt, 0:n], h[:, kt, 0:n], y[:, kt, 0:n], ALU.add).then_inc(h_ready_pool, 1)

        def await_h(eng, s, kt):
            if kt in DVE_ADDS:
                eng.wait_ge(h_ready_dve, len(DVE_ADDS) * s + DVE_ADDS.index(kt) + 1)
            else:
                eng.wait_ge(h_ready_pool, (KT - len(DVE_ADDS)) * s + kt - sum(d < kt for d in DVE_ADDS) + 1)

        def ffn_in_pe(s):
            pe = nc.tensor
            g0, n, f = first_chunk[f"in{s}"], width_in(s), FT * (s // 3 * 2 + (s % 3 == 2))

            def body(j, i):
                g = g0 + j
                await_parts(g, i)
                if j >= 2:
                    pe.wait_ge(gate_done, at(f + j - 1, RAW_RING, i))
                if j == 0:
                    for kt in range(KT):
                        await_u(pe, s, kt)
                        for m in range(2):
                            ins = products(bank[2 * m][:, 0:n], g, [kt], lambda w, k: block_of(w, g, k, m),
                                           lambda k: uhi[:, k, 0:n], lambda k: ulo[:, k, 0:n],
                                           first=kt == 0, last=kt == KT - 1)
                else:
                    for m in range(2):
                        ins = products(bank[2 * m + j % 2][:, 0:n], g, range(KT), lambda w, k: block_of(w, g, k, m),
                                       lambda k: uhi[:, k, 0:n], lambda k: ulo[:, k, 0:n])
                ins.then_inc(w_used, 1)

            ring_loop(pe, FT, body)

        def ffn_in_act(s):
            act = nc.scalar
            g0, n, f = first_chunk[f"in{s}"], width_in(s), FT * (s // 3 * 2 + (s % 3 == 2))

            def high(j, i):
                act.wait_ge(gate_done, at(f + j + 1, RAW_RING, i))
                dst = ghi[:, j, 0:n] if i is None else ghi[:, bass.ds(at(j, RAW_RING, i), 1), 0:n]
                src = tb[:, j % 2, 0:n] if i is None else tb[:, j % 2:j % 2 + 1, 0:n]
                act.activation(dst, src, ACT.Copy).then_inc(ghi_done, 1)

            def body(j, i):
                make_high(g0 + j + 1, i)
                if j == 0:
                    load_table(ACT.Silu)
                if j:
                    high(j - 1, i)
                act.wait_ge(w_used, at(g0 + j + 1, RAW_RING, i))
                act.activation(ta[:, j % 2, 0:n], bank[j % 2][:, 0:n], ACT.Silu).then_inc(silu_done, 1)

            ring_loop(act, FT, body)
            high(FT - 1, None)

        def ffn_in_dve(s):
            dve = nc.vector
            g0, n, f = first_chunk[f"in{s}"], width_in(s), FT * (s // 3 * 2 + (s % 3 == 2))

            def rest(j, i):
                dve.wait_ge(ghi_done, at(f + j + 1, RAW_RING, i))
                if i is None:
                    dst, hi, src = glo[:, j, 0:n], ghi[:, j, 0:n], tb[:, j % 2, 0:n]
                else:
                    w = bass.ds(at(j, RAW_RING, i), 1)
                    dst, hi, src = glo[:, w, 0:n], ghi[:, w, 0:n], tb[:, j % 2:j % 2 + 1, 0:n]
                dve.tensor_tensor(dst, src, hi.bitcast(F32), ALU.subtract).then_inc(glo_done, 1)

            def body(j, i):
                make_rest(g0 + j + 1, i)
                if j:
                    rest(j - 1, i)
                dve.wait_ge(silu_done, at(f + j + 1, RAW_RING, i))
                if j >= 2:
                    dve.wait_ge(glo_done, at(f + j - 1, RAW_RING, i))
                dve.tensor_tensor(tb[:, j % 2, 0:n], ta[:, j % 2, 0:n], bank[2 + j % 2][:, 0:n], ALU.mult)\
                    .then_inc(gate_done, 1)

            ring_loop(dve, FT, body)
            rest(FT - 1, None)

        def out_shape(s):
            return (2 * KT, -2, HALF_FT) if s % 3 != 1 else (KT, 1, 12) if s == 10 else (4, 2, KT)

        def tiles_of(s, j):
            _, per, _ = out_shape(s)
            return [j // 2] if per == -2 and j % 2 else [] if per == -2 else list(range(per * j, per * (j + 1)))

        def out_pe(s, acts_hi, acts_lo, ready=None, ready_tile=None):
            pe = nc.tensor
            chunks, per, nk = out_shape(s)
            g0, n, q = first_chunk[f"out{s}"], width(s), round_y(s)

            def body(j, i):
                g = g0 + j
                await_parts(g, i)
                if j < 2 and ready:
                    ready(j)
                tiles = [j // 2] if per == -2 else tiles_of(s, j)
                k0 = nk * (j % 2) if per == -2 else 0
                cols = CHUNK if per == 2 else P
                steps = [[k] for k in range(nk)] if j == 0 and ready_tile else [range(nk)]
                for ks in steps:
                    if j == 0 and ready_tile:
                        ready_tile(ks[0])
                    for d in tiles:
                        if d >= 2 and (per != -2 or j % 2 == 0):
                            pe.wait_ge(y_ready, at(8 * s + d - 1, 2, i))
                        m = d % 2 if per == 2 else 0
                        ins = products(bank[d % 2][:, 0:n], g, ks, lambda w, k: block_of(w, g, k, m, cols),
                                       lambda k: acts_hi(k0 + k, n), lambda k: acts_lo(k0 + k, n),
                                       first=k0 + ks[0] == 0, last=k0 + ks[-1] + 1 >= (FT if per == -2 else nk))
                ins.then_inc(w_used, 1)
            ring_loop(pe, chunks, body)
            pe.wait_ge(sq_used, 8 * q + pool_sums(s))
            pe.wait_ge(sd_ready, q)
            pe.matmul(stat[:, 0:n], ones[:], ta[:, 0, 0:n], start=True, stop=False)
            for d in range(pool_sums(s), KT):
                pe.wait_ge(sq_ready, 8 * q + d + 1)
                pe.matmul(stat[:, 0:n], ones[:], sq[:, d % 2, 0:n], start=False, stop=d == KT - 1)\
                    .then_inc(sq_used, 1)

        def pool_sums(s):
            return tiles_of(s, out_shape(s)[0] - 1)[0]

        def out_pool(s):
            pool = nc.gpsimd
            n, q = width(s), round_y(s)
            for d in range(1, pool_sums(s)):
                pool.wait_ge(sq_ready, 8 * q + d + 1)
                if d == 1:
                    pool.tensor_tensor(ta[:, 0, 0:n], sq[:, 0, 0:n], sq[:, 1, 0:n], ALU.add).then_inc(sq_used, 2)
                else:
                    pool.wait_ge(sq_used, 8 * q + d)
                    pool.tensor_tensor(ta[:, 0, 0:n], ta[:, 0, 0:n], sq[:, d % 2, 0:n], ALU.add)\
                        .then_inc(sq_used, 1)

        def out_done_count(s, d):
            _, per, _ = out_shape(s)
            return 2 * d + 2 if per == -2 else d // per + 1

        def out_act(s):
            act = nc.scalar
            chunks, per, nk = out_shape(s)
            g0, n, q = first_chunk[f"out{s}"], width(s), round_y(s)

            def squares(j, i):
                for d in tiles_of(s, j):
                    act.wait_ge(y_ready, at(8 * s + d + 1, 2, i))
                    square(q, d, y[:, d, 0:n] if i is None else y[:, bass.ds(at(d, 2, i), 1), 0:n], n, i, 2)

            def body(j, i):
                make_high(g0 + j + 1, i)
                if j:
                    squares(j - 1, i)
                else:
                    load_table(ACT.Sqrt)

            ring_loop(act, chunks, body)
            squares(chunks - 1, None)
            root(q, n)

        def out_dve(s):
            dve = nc.vector
            chunks, per, nk = out_shape(s)
            g0, n = first_chunk[f"out{s}"], width(s)

            def copies(j, i):
                for d in tiles_of(s, j):
                    dve.wait_ge(w_used, at(g0 + out_done_count(s, d), RAW_RING, i))
                    if i is None:
                        dve.tensor_copy(y[:, d, 0:n], bank[d % 2][:, 0:n]).then_inc(y_ready, 1)
                    else:
                        dve.tensor_copy(y[:, bass.ds(at(d, 2, i), 1), 0:n],
                                        bank[d % 2][:, 0:n].rearrange("p (a n) -> p a n", a=1)).then_inc(y_ready, 1)

            def body(j, i):
                if j:
                    copies(j - 1, i)
                make_rest(g0 + j + 1, i)

            ring_loop(dve, chunks, body)
            copies(chunks - 1, None)

        def ffn_out_pe(s):
            f = FT * (s // 3 * 2 + (s % 3 == 2)) + FT

            def ready(j):
                nc.tensor.wait_ge(glo_done, f if j else f - HALF_FT)

            out_pe(s, lambda k, n: ghi[:, k, 0:n], lambda k, n: glo[:, k, 0:n], ready)

        proj_taken = sem("proj_taken")
        tile_done = sem("tile_done")
        const_landed = sem("const_landed")
        rot_ready = sem("rot_ready")
        rope_done = sem("rope_done")
        att_scored = sem("att_scored")
        att_biased = sem("att_biased")
        att_max = sem("att_max")
        att_exp = sem("att_exp")
        att_sum = sem("att_sum")
        att_p = sem("att_p")
        att_turned = sem("att_turned")
        att_pt = sem("att_pt")
        att_pv = sem("att_pv")
        att_o = sem("att_o")
        att_olo = sem("att_olo")
        total = {"taken": 0, "rope": 0, "map": 0, "item": 0, "biased": 0, "olo": 0, "sum": 0, "const": 0, "quads": 0}

        def region():
            where = [mix_at]

            def put(name, shape, dt=F32):
                size = (int(np.prod(shape[1:])) * 4 + 31) // 32 * 32
                where[0] += size
                assert where[0] <= mix_end, (name, where[0], mix_end)
                return place(name, shape, dt, offset=where[0] - size)

            return put

        attn_e = place("attn_exp", [P, 4, BOTH], F32, offset=u_at)
        attn_p = place("attn_probs", [P, 2, BOTH], F32, offset=u_at + 4 * BOTH * 4)
        attn_pt = place("attn_probs_turned", [P, 2, 4, P], F32, offset=u_at + 6 * BOTH * 4)
        over_ulo = u_at + KT * BOTH * 4
        attn_cols = place("attn_columns", [P, 3, 64], F32)

        class Projection:

            def __init__(self, s, seg, kinds, widths):
                self.s, self.g0, self.kinds, self.widths = s, first_chunk.get(seg), kinds, widths
                self.base = total["taken"]
                self.release = None
                self.first = []
                e = 0
                for kind, n in zip(kinds, widths):
                    self.first.append(e)
                    e += 2 if kind == "f" else n // P
                self.n = e
                total["taken"] += e
                self.quads = total["quads"]
                total["quads"] += 3 * sum(self.count(c) == 4 for c in range(len(kinds)))

            def count(self, c):
                return 2 if self.kinds[c] == "f" else self.widths[c] // P

            def await_tile(self, act, c, m):
                if self.count(c) == 4 and m < 3:
                    act.wait_ge(tile_done, self.quads + 3 * sum(self.count(d) == 4 for d in range(c)) + m + 1)
                else:
                    act.wait_ge(w_used, self.g0 + c + 1)

            def pe_chunk(self, c, wait_input=False):
                pe = nc.tensor
                g, n = self.g0 + c, self.widths[c]
                await_parts(g)
                wide = CHUNK if self.kinds[c] == "t" else 2 * SSM_H
                spots = []
                for m in range(self.count(c)):
                    e = self.first[c] + m
                    if e >= 4:
                        s_, count = self.release(e - 4) if self.release else (proj_taken, self.base + e - 3)
                        pe.wait_ge(s_, count)
                    spots.append(bank[e % 4][:, 0:n] if self.kinds[c] == "f" else bank[e % 4][:, 0:wide])

                def step(m, k):
                    nonlocal ins
                    if self.kinds[c] == "f":
                        ins = products(spots[m], g, [k], lambda w, k: block_of(w, g, k, m),
                                       lambda k: uhi[:, k, 0:n], lambda k: ulo[:, k, 0:n],
                                       first=k == 0, last=k == KT - 1)
                    else:
                        tok, cols = slice(m * P, (m + 1) * P), slice(k * wide, (k + 1) * wide)
                        w_hi, w_lo = whi[:, part_of[g] % PART_RING, cols], wlo[:, part_of[g] % PART_RING, cols]
                        pe.matmul(spots[m], uhi[:, k, tok], w_hi, start=k == 0, stop=False)
                        pe.matmul(spots[m], uhi[:, k, tok], w_lo, start=False, stop=False)
                        ins = pe.matmul(spots[m], ulo[:, k, tok], w_hi, start=False, stop=k == KT - 1)

                ins = None
                if wait_input:
                    for k in range(KT):
                        await_u(pe, self.s, k)
                        for m in range(self.count(c)):
                            step(m, k)
                else:
                    for m in range(self.count(c)):
                        for k in range(KT):
                            step(m, k)
                        if self.count(c) == 4 and m < 3:
                            ins.then_inc(tile_done, 1)
                ins.then_inc(w_used, 1)

        class Attention:

            def __init__(self, items, n_maps, fillers, kind, norm=None):
                self.items, self.n_maps, self.kind, self.fillers = items, n_maps, kind, fillers
                self.m0, self.i0, self.b0, self.o0, self.s0 = (total["map"], total["item"], total["biased"],
                                                               total["olo"], total["sum"])
                total["map"] += len(items) * n_maps
                total["item"] += len(items)
                if kind != "da":
                    total["biased"] += len(items)
                    total["olo"] += len(items)
                if kind == "ev":
                    total["sum"] += len(items)
                self.norm = norm

            def filler(self, i):
                return self.fillers[i // 8] if i // 8 < len(self.fillers) else None

            def fill_pe(self, i):
                group, step = self.filler(i), {0: 0, 1: 1, 2: 2, 3: 3}.get(i % 8)
                if group and self.norm:
                    self.norm.release_pe(i)
                if group and step is not None:
                    mod_products(*group, [step])
                if group and i % 8 == 5:
                    mod_turn(*group)

            def fill_act(self, i):
                group = self.filler(i)
                if group and i % 8 == 4:
                    mod_copy(*group)
                if group and group == self.fillers[-1] and i % 8 == 4:
                    make_high(first_chunk[f"ada{group[0]}_{group[1]}"] + 4)

            def fill_dve(self, i):
                group = self.filler(i)
                if group and i % 8 == 5:
                    if group == self.fillers[-1]:
                        make_rest(first_chunk[f"ada{group[0]}_{group[1]}"] + 4)
                    take_mod(*group)

            def pe(self):
                pe = nc.tensor
                n = len(self.items)
                for i in range(n + 3):
                    if i < n:
                        it = self.items[i]
                        for j, (q, k) in enumerate(it["maps"]):
                            m = i * self.n_maps + j
                            if m >= 4:
                                pe.wait_ge(att_exp, self.m0 + m - 3)
                            pe.matmul(bank[m % 4][:, 0:it["keys"]], q, k, start=True, stop=True)\
                                .then_inc(att_scored, 1)
                        self.fill_pe(i)
                    if 2 <= i < n + 2:
                        t_, it = i - 2, self.items[i - 2]
                        pe.wait_ge(att_p, self.i0 + t_ + 1)
                        if t_ >= 1:
                            pe.wait_ge(att_pt, self.i0 + t_)
                        for kt in range(it["keys"] // P):
                            ins = pe.transpose(bank[6][:, kt * P:(kt + 1) * P],
                                               attn_p[:, t_ % 2, kt * P:(kt + 1) * P], ident[:])
                        ins.then_inc(att_turned, 1)
                    if i >= 3:
                        t_, it = i - 3, self.items[i - 3]
                        pe.wait_ge(att_pt, self.i0 + t_ + 1)
                        if t_ >= 2:
                            if self.kind == "da":
                                pe.wait_ge(att_o, self.i0 + t_ - 1)
                            else:
                                pe.wait_ge(att_olo, self.o0 + t_ - 1)
                        lo, hi = it["rows"]
                        nk = it["keys"] // P
                        for kt in range(nk):
                            ins = pe.matmul(bank[4 + t_ % 2 * 3][lo:hi, 0:P], it["v"](kt),
                                            attn_pt[:, t_ % 2, kt], start=kt == 0, stop=kt == nk - 1)
                        ins.then_inc(att_pv, 1)
                    if self.norm:
                        self.norm.between_pe(i)

            def act(self):
                act = nc.scalar
                n = len(self.items)
                for i in range(n + 4):
                    if i < n:
                        it = self.items[i]
                        for j in range(self.n_maps):
                            m = i * self.n_maps + j
                            act.wait_ge(att_max, self.m0 + m + 1)
                            if m >= 4:
                                act.wait_ge(att_p, self.i0 + (m - 4) // self.n_maps + 1)
                            act.activation(attn_e[:, m % 4, 0:it["keys"]], bank[m % 4][:, 0:it["keys"]], ACT.Exp,
                                           bias=attn_cols[:, 0, m:m + 1],
                                           accum_out=attn_cols[:, 1, m:m + 1]).then_inc(att_exp, 1)
                        if self.kind == "ev":
                            act.activation(sink_e[:, i:i + 1], pcol("sink", it["head"], it["head"] + 1), ACT.Exp,
                                           bias=attn_cols[:, 0, i:i + 1]).then_inc(att_sum, 1)
                        self.fill_act(i)
                    if 2 <= i < n + 2:
                        t_, it = i - 2, self.items[i - 2]
                        act.wait_ge(att_turned, self.i0 + t_ + 1)
                        if t_ >= 2:
                            act.wait_ge(att_pv, self.i0 + t_ - 1)
                        nk = it["keys"] // P
                        act.activation(attn_pt[:, t_ % 2, 0:nk],
                                       bank[6][:, 0:nk * P].rearrange("p (k q) -> p k q", q=P),
                                       ACT.Copy).then_inc(att_pt, 1)
                    if 3 <= i < n + 3:
                        t_, it = i - 3, self.items[i - 3]
                        act.wait_ge(att_pv, self.i0 + t_ + 1)
                        lo, hi = it["rows"]
                        act.activation(it["out"][0], bank[4 + t_ % 2 * 3][lo:hi, 0:P], ACT.Copy)\
                            .then_inc(att_o, 1)
                    if self.norm:
                        self.norm.between_act(i)

            def dve(self):
                dve = nc.vector
                n = len(self.items)
                nm = self.n_maps
                for i in range(n + 4):
                    if i < n:
                        it = self.items[i]
                        for j in range(nm):
                            m = i * nm + j
                            dve.wait_ge(att_scored, self.m0 + m + 1)
                            ps = bank[m % 4][:, 0:it["keys"]]
                            if "bias" in it:
                                part = bank[m % 4][:, 0:SEQ]
                                dve.tensor_tensor(part, part, it["bias"], ALU.add).then_inc(att_biased, 1)
                                dve.wait_ge(att_biased, self.b0 + i + 1)
                            if self.kind == "ev":
                                link(dve, dve.tensor_reduce(attn_cols[:, 0, m:m + 1], ps, AX_X, ALU.max, negate=True))
                                dve.tensor_tensor(attn_cols[:, 0, m:m + 1], attn_cols[:, 0, m:m + 1],
                                                  minus_sink[:, it["head"]:it["head"] + 1], ALU.min)\
                                    .then_inc(att_max, 1)
                            else:
                                dve.tensor_reduce(attn_cols[:, 0, m:m + 1], ps, AX_X, ALU.max, negate=True)\
                                    .then_inc(att_max, 1)
                        self.fill_dve(i)
                    if 1 <= i <= n:
                        t_, it = i - 1, self.items[i - 1]
                        m = t_ * nm
                        dve.wait_ge(att_exp, self.m0 + m + nm)
                        if self.kind == "ev":
                            dve.wait_ge(att_sum, self.s0 + t_ + 1)
                            link(dve, dve.tensor_tensor(attn_cols[:, 1, m:m + 1], attn_cols[:, 1, m:m + 1],
                                                        sink_e[:, t_:t_ + 1], ALU.add))
                        link(dve, dve.reciprocal(attn_cols[:, 2, m:m + nm], attn_cols[:, 1, m:m + nm]))
                        if t_ >= 2:
                            dve.wait_ge(att_turned, self.i0 + t_ - 1)
                        keys = it["keys"]
                        dst = attn_p[:, t_ % 2, 0:keys]
                        ins = dve.tensor_scalar(dst, attn_e[:, m % 4, 0:keys], attn_cols[:, 2, m:m + 1], None, ALU.mult)
                        if nm == 2:
                            link(dve, ins)
                            link(dve, dve.tensor_tensor(attn_cols[:, 2, m + 1:m + 2], attn_cols[:, 2, m + 1:m + 2],
                                                        minus_lam, ALU.mult))
                            ins = dve.scalar_tensor_tensor(dst, attn_e[:, (m + 1) % 4, 0:keys],
                                                           attn_cols[:, 2, m + 1:m + 2], dst, ALU.mult, ALU.add)
                        ins.then_inc(att_p, 1)
                    if i >= 4 and self.kind != "da":
                        t_, it = i - 4, self.items[i - 4]
                        dve.wait_ge(att_o, self.i0 + t_ + 1)
                        lo, hi = it["rows"]
                        dve.tensor_tensor(it["out"][1], bank[4 + t_ % 2 * 3][lo:hi, 0:P],
                                          it["out"][0].bitcast(F32), ALU.subtract).then_inc(att_olo, 1)
                    if self.norm:
                        self.norm.between_dve(i)

        ident = place("identity", [P, P], F32)
        minus_lam = small[:, 4:5]
        subln = small[:, 5:6]
        minus_sink = place("minus_sink", [P, EV_QH], F32)
        sink_e = place("sink_exp", [P, 2 * EV_QH], F32)
        mixers = {}
        heads_in = lambda h_: slice(h_ % 2 * HD, h_ % 2 * HD + HD)

        def rope_pe(r0, t_, m, src, rot, taken):
            pe = nc.tensor
            pe.wait_ge(proj_taken, taken)
            if t_ >= 2:
                pe.wait_ge(rope_done, r0 + t_ - 1)
            pe.matmul(bank[6 + t_ % 2][:, 0:SEQ], rot, src[:, m, 0:SEQ], start=True, stop=True)\
                .then_inc(rot_ready, 1)

        def rope_dve(r0, t_, m, src, cos, sin):
            dve = nc.vector
            dve.wait_ge(rot_ready, r0 + t_ + 1)
            if t_:
                dve.wait_ge(rope_done, r0 + t_)
            link(dve, dve.tensor_tensor(ta[:, 0, 0:SEQ], src[:, m, 0:SEQ], cos, ALU.mult))
            link(dve, dve.tensor_tensor(ta[:, 1, 0:SEQ], bank[6 + t_ % 2][:, 0:SEQ], sin, ALU.mult))
            dve.tensor_tensor(src[:, m, 0:SEQ], ta[:, 0, 0:SEQ], ta[:, 1, 0:SEQ], ALU.add).then_inc(rope_done, 1)

        class DiffAttention:
            def __init__(self, s=1):
                put = region()
                self.s = s
                self.qk = put("da_qk", [P, 16, BOTH])
                self.v = put("da_v", [P, 4, D])
                self.o = put("da_o", [P, KT, BOTH])
                self.rope = put("da_rope", [P, P + 2 * SEQ])
                self.ohi = place("da_o_high", [P, KT, BOTH], F32R, offset=mix_at)
                self.olo = place("da_o_rest", [P, KT, BOTH], F32R, offset=mix_at + KT * BOTH * 4)
                self.proj = Projection(s, f"in{s}", ["f"] * 8 + ["t"] * 4, [BOTH] * 12)
                self.r0 = total["rope"]
                total["rope"] += 16
                total["const"] += 1
                self.const = total["const"]
                items = []
                for hh in range(KT):
                    for qt in range(4):
                        k0 = 0 if qt < 2 else SEQ
                        keys = BOTH - k0
                        items.append({
                            "maps": [(self.qk[j * HD:(j + 1) * HD, hh, qt * P:(qt + 1) * P],
                                      self.qk[j * HD:(j + 1) * HD, 8 + hh, k0:BOTH]) for j in range(2)],
                            "keys": keys, "rows": (0, P),
                            "v": (lambda kt, hh=hh, k0=k0: self.v[:, k0 // P + kt, hh * P:(hh + 1) * P]),
                            "out": (self.o[:, hh, qt * P:(qt + 1) * P],)})
                self.att = Attention(items, 2, [(0, 5), (0, 6), (0, 7), (0, 8)], "da", norm=self)
                self.sq_done, self.stat_done, self.root_done = sem("hn_squares"), sem("hn_summed"), sem("hn_root")
                self.inv, self.scaled, self.hi_done, self.lo_done = (sem("hn_inverse"), sem("hn_scaled"),
                                                                     sem("hn_high"), sem("hn_rest"))

            def loads(self, sp):
                sp.dma_start(self.rope[:], t["rope1"]).then_inc(const_landed, 16)

            def pe(self, pe):
                for c in range(12):
                    self.proj.pe_chunk(c, c == 0)
                    if c == 1:
                        pe.wait_ge(const_landed, 16 * self.const)
                    if 1 <= c <= 8:
                        for m in (2 * c - 2, 2 * c - 1):
                            rope_pe(self.r0, m, m, self.qk, self.rope[:, 0:P], self.proj.base + m + 1)
                pe.wait_ge(rope_done, self.r0 + 16)
                pe.wait_ge(proj_taken, self.proj.base + self.proj.n)
                self.att.pe()
                self.sum_head(KT - 1)

            def out(self, pe):
                out_pe(self.s, lambda k, n: self.ohi[:, k, 0:n], lambda k, n: self.olo[:, k, 0:n],
                       ready_tile=lambda k: pe.wait_ge(self.lo_done, k + 1))

            def act(self, act):
                g0 = self.proj.g0
                load_table(ACT.Exp)
                for c in range(12):
                    make_high(g0 + c + 1)
                    for m in range(self.proj.count(c)):
                        self.proj.await_tile(act, c, m)
                        e = self.proj.first[c] + m
                        if c < 8:
                            ins = act.activation(self.qk[:, e], bank[e % 4][:], ACT.Copy, scale=0.125 if e < 8 else 1.0)
                        else:
                            ins = act.activation(self.v[:, m, (c - 8) * CHUNK:(c - 7) * CHUNK], bank[e % 4][:, 0:CHUNK],
                                                 ACT.Copy)
                        ins.then_inc(proj_taken, 1)
                self.att.act()
                self.root(KT - 1)
                self.high(KT - 1)

            def dve(self, dve):
                g0 = self.proj.g0
                for c in range(12):
                    make_rest(g0 + c + 1)
                    if c == 1:
                        dve.wait_ge(const_landed, 16 * self.const)
                    if 1 <= c <= 8:
                        for m in (2 * c - 2, 2 * c - 1):
                            rope_dve(self.r0, m, m, self.qk, self.rope[:, P:P + SEQ], self.rope[:, P + SEQ:])
                self.att.dve()
                self.inverse(KT - 1)
                self.scale(KT - 1)
                self.rest(KT - 1)

            def heads(self, i, step):
                n = (i - step) // 8
                return [hh for hh in (2 * n - 1, 2 * n) if 0 <= hh < KT - 1] if i >= step and i % 8 == step % 8 else []

            def squares(self, hh):
                act = nc.scalar
                act.wait_ge(att_o, self.att.i0 + 4 * hh + 4)
                if hh >= 2:
                    act.wait_ge(self.stat_done, hh - 1)
                act.activation(sq[:, hh % 2], self.o[:, hh], ACT.Square).then_inc(self.sq_done, 1)

            def sum_head(self, hh):
                pe = nc.tensor
                pe.wait_ge(self.sq_done, hh + 1)
                if hh:
                    pe.wait_ge(self.root_done, hh)
                pe.matmul(mod[:], ones[:], sq[:, hh % 2], start=True, stop=True).then_inc(self.stat_done, 1)

            def root(self, hh):
                act = nc.scalar
                act.wait_ge(self.stat_done, hh + 1)
                if hh >= 2:
                    act.wait_ge(self.scaled, hh - 1)
                act.activation(tb[:, hh % 2], mod[:], ACT.Sqrt, scale=1.0 / P, bias=eps_col).then_inc(self.root_done, 1)

            def inverse(self, hh):
                nc.vector.wait_ge(self.root_done, hh + 1)
                nc.vector.reciprocal(tb[:, hh % 2], tb[:, hh % 2]).then_inc(self.inv, 1)

            def scale(self, hh):
                dve = nc.vector
                dve.wait_ge(self.inv, hh + 1)
                if hh >= 2:
                    dve.wait_ge(self.lo_done, hh - 1)
                dve.scalar_tensor_tensor(ta[:, hh % 2], self.o[:, hh], subln, tb[:, hh % 2], ALU.mult, ALU.mult)\
                    .then_inc(self.scaled, 1)

            def high(self, hh):
                nc.scalar.wait_ge(self.scaled, hh + 1)
                nc.scalar.activation(self.ohi[:, hh], ta[:, hh % 2], ACT.Copy).then_inc(self.hi_done, 1)

            def rest(self, hh):
                nc.vector.wait_ge(self.hi_done, hh + 1)
                nc.vector.tensor_tensor(self.olo[:, hh], ta[:, hh % 2], self.ohi[:, hh].bitcast(F32), ALU.subtract)\
                    .then_inc(self.lo_done, 1)

            def release_pe(self, i):
                if i and i % 8 == 0:
                    nc.tensor.wait_ge(self.root_done, i // 4 - 1)

            def between_pe(self, i):
                for hh in self.heads(i, 7):
                    nc.tensor.wait_ge(mod_read, ada_index["ada0_5"] + i // 8 + 1)
                    self.sum_head(hh)

            def between_act(self, i):
                for hh in self.heads(i, 6):
                    self.squares(hh)
                for hh in self.heads(i, 7):
                    self.root(hh)
                if i == len(self.att.items) + 2:
                    self.squares(KT - 1)
                for hh in self.heads(i, 9)[:1]:
                    self.high(hh)
                for hh in self.heads(i, 10)[1:]:
                    self.high(hh)

            def between_dve(self, i):
                for hh in self.heads(i, 7)[:1]:
                    self.inverse(hh)
                for hh in self.heads(i, 8)[:1]:
                    self.scale(hh)
                for hh in self.heads(i, 8)[1:]:
                    self.inverse(hh)
                for hh in self.heads(i, 9)[1:]:
                    self.scale(hh)
                for hh in self.heads(i, 11):
                    self.rest(hh)

            def pool(self, pool):
                pass

        class Neighbourhood:
            def __init__(self, s=4):
                put = region()
                self.s = s
                self.q = put("na_q", [P, KT, SEQ])
                self.k = put("na_k", [P, KT, BOTH])
                self.v = put("na_v", [P, 4, D])
                self.bias = put("na_bias", [P, 2 * NA_H, SEQ])
                self.mask = put("na_mask", [P, SEQ])
                self.ohi = place("na_o_high", [P, KT, SEQ], F32R, offset=over_ulo)
                self.olo = place("na_o_rest", [P, KT, SEQ], F32R, offset=over_ulo + KT * SEQ * 4)
                self.proj = Projection(s, f"in{s}", ["f"] * 8 + ["t"] * 4, [SEQ] * 4 + [BOTH] * 8)
                total["const"] += 2
                self.const = total["const"]
                self.masked = sem("na_bias_masked")
                items = []
                for pair in range(KT):
                    for qt in range(2):
                        for hh in (2 * pair, 2 * pair + 1):
                            r = heads_in(hh)
                            items.append({
                                "maps": [(self.q[r, pair, qt * P:(qt + 1) * P], self.k[r, pair, :])],
                                "keys": BOTH, "rows": (r.start, r.stop), "bias": self.bias[:, 2 * hh + qt],
                                "v": (lambda kt, hh=hh: self.v[:, kt, hh * HD:(hh + 1) * HD]),
                                "out": (self.ohi[r, pair, qt * P:(qt + 1) * P],
                                        self.olo[r, pair, qt * P:(qt + 1) * P])})
                self.att = Attention(items, 1, [(1, 6), (1, 7), (1, 8)], "na")

            def loads(self, sp):
                sp.dma_start(self.bias[:].rearrange("p a b -> p (a b)"), t["na_bias"]).then_inc(const_landed, 16)
                sp.dma_start(self.mask[:], t["na_mask"]).then_inc(const_landed, 16)

            def pool(self, pool):
                pool.wait_ge(const_landed, 16 * self.const)
                for n in range(2 * NA_H):
                    pool.tensor_tensor(self.bias[:, n], self.bias[:, n], self.mask[:], ALU.add)\
                        .then_inc(self.masked, 1)

            def pe(self, pe):
                for c in range(12):
                    self.proj.pe_chunk(c, c == 0)
                pe.wait_ge(proj_taken, self.proj.base + self.proj.n)
                self.att.pe()

            def out(self, pe):
                out_pe(self.s, lambda k, n: self.ohi[:, k, 0:n], lambda k, n: self.olo[:, k, 0:n],
                       ready_tile=lambda k: pe.wait_ge(att_olo, self.att.o0 + 4 * k + 4))

            def act(self, act):
                g0 = self.proj.g0
                load_table(ACT.Exp)
                for c in range(12):
                    make_high(g0 + c + 1)
                    for m in range(self.proj.count(c)):
                        self.proj.await_tile(act, c, m)
                        e = self.proj.first[c] + m
                        if c < 4:
                            ins = act.activation(self.q[:, e], bank[e % 4][:, 0:SEQ], ACT.Copy, scale=0.125)
                        elif c < 8:
                            ins = act.activation(self.k[:, e - 8], bank[e % 4][:], ACT.Copy)
                        else:
                            ins = act.activation(self.v[:, m, (c - 8) * CHUNK:(c - 7) * CHUNK], bank[e % 4][:, 0:CHUNK],
                                                 ACT.Copy)
                        ins.then_inc(proj_taken, 1)
                self.att.act()

            def dve(self, dve):
                for c in range(12):
                    make_rest(self.proj.g0 + c + 1)
                dve.wait_ge(self.masked, 2 * NA_H)
                self.att.dve()

        class Even:
            def __init__(self, s=7):
                put = region()
                self.s = s
                self.u = put("ev_u", [P, 2, CHUNK])
                self.v = put("ev_v", [P, 2, CHUNK])
                self.q = put("ev_qk", [P, 8, SEQ])
                self.const_tile = put("ev_const", [P, 2 * SEQ + 8 * SEQ])
                self.rope = put("ev_rope", [P, P + 2 * SEQ])
                self.pw = put("ev_pool_w", [P, 2 * HD])
                self.pooled = put("ev_pooled", [P, 2, SEQ])
                self.ohi = put("ev_o_high", [P, KT, SEQ], F32R)
                self.olo = put("ev_o_rest", [P, KT, SEQ], F32R)
                self.proj = Projection(s, f"in{s}", ["t"] * 2 + ["f"] * 4, [SEQ] * 6)
                self.r0 = total["rope"]
                total["rope"] += 8
                total["const"] += 3
                self.const = total["const"]
                self.mixed, self.taken, self.done = sem("pool_mixed"), sem("pool_taken"), sem("pool_done")
                items = []
                for n, hh in enumerate(EV_HEADS):
                    kv = hh // 3
                    for qt in range(2):
                        r = heads_in(n)
                        assert kv % 2 == n % 2
                        items.append({
                            "maps": [(self.q[r, n // 2, qt * P:(qt + 1) * P], self.q[r, 6 + kv // 2, :])],
                            "keys": SEQ, "rows": (r.start, r.stop), "head": n,
                            "bias": self.const_tile[:, qt * SEQ:(qt + 1) * SEQ],
                            "v": (lambda kt, kv=kv: self.v[:, kt, kv * HD:(kv + 1) * HD]),
                            "out": (self.ohi[r, 2 + n // 2, qt * P:(qt + 1) * P],
                                    self.olo[r, 2 + n // 2, qt * P:(qt + 1) * P])})
                self.att = Attention(items, 1, [], "ev")

            def loads(self, sp):
                sp.dma_start(self.const_tile[:], t["ev_const"]).then_inc(const_landed, 16)
                sp.dma_start(self.rope[:], t["rope2"]).then_inc(const_landed, 16)
                sp.dma_start(self.pw[:], t["pool_w"]).then_inc(const_landed, 16)

            def pool(self, pool):
                pass

            def pe(self, pe):
                for c in range(6):
                    self.proj.pe_chunk(c, c == 0)
                    if c == 1:
                        pe.wait_ge(const_landed, 16 * self.const)
                    if c >= 3:
                        for t_ in (2 * c - 6, 2 * c - 5):
                            rope_pe(self.r0, t_, t_, self.q, self.rope[:, 0:P], self.proj.base + 4 + t_ + 1)
                    if c == 1:
                        pe.wait_ge(proj_taken, self.proj.base + 2)
                        for g in range(4):
                            r = heads_in(g)
                            for kt in range(2):
                                m_w = self.const_tile[:, (2 + 2 * g + kt) * SEQ:(3 + 2 * g + kt) * SEQ]
                                ins = pe.matmul(bank[6 + g // 2][r, 0:SEQ], self.u[:, kt, g * HD:(g + 1) * HD], m_w,
                                                start=kt == 0, stop=kt == 1)
                            if g % 2:
                                ins.then_inc(self.mixed, 1)
                    if c == 2:
                        pe.wait_ge(self.taken, 2)
                        for g in range(4):
                            r = heads_in(g)
                            ins = pe.matmul(bank[4 + g // 2][r, 0:SEQ], self.pw[r, g // 2 * HD:(g // 2 + 1) * HD],
                                            self.pooled[r, g // 2], start=True, stop=True)
                        ins.then_inc(self.mixed, 1)
                pe.wait_ge(proj_taken, self.proj.base + self.proj.n)
                for t_ in (6, 7):
                    rope_pe(self.r0, t_, t_, self.q, self.rope[:, 0:P], self.proj.base + 4 + t_ + 1)
                pe.wait_ge(rope_done, self.r0 + 8)
                pe.wait_ge(self.done, 4)
                self.att.pe()

            def out(self, pe):
                out_pe(self.s, lambda k, n: self.ohi[:, k, 0:n], lambda k, n: self.olo[:, k, 0:n],
                       ready_tile=lambda k: pe.wait_ge(att_olo, self.att.o0 + 4 * max(k - 1, 1)))

            def act(self, act):
                g0 = self.proj.g0
                load_table(ACT.Exp)
                for c in range(6):
                    make_high(g0 + c + 1)
                    act.wait_ge(w_used, g0 + c + 1)
                    for m in range(2):
                        e = self.proj.first[c] + m
                        if c < 2:
                            ins = act.activation((self.u, self.v)[c][:, m], bank[e % 4][:, 0:CHUNK], ACT.Copy)
                        else:
                            ins = act.activation(self.q[:, e - 4], bank[e % 4][:, 0:SEQ], ACT.Copy,
                                                 scale=0.125 if e < 10 else 1.0)
                        ins.then_inc(proj_taken, 1)
                    if c == 1:
                        for n in range(2):
                            act.wait_ge(self.mixed, n + 1)
                            act.activation(self.pooled[:, n], bank[6 + n][:, 0:SEQ], ACT.Copy).then_inc(self.taken, 1)
                    if c == 2:
                        act.wait_ge(self.mixed, 3)
                        for n in range(2):
                            act.activation(self.ohi[:, n], bank[4 + n][:, 0:SEQ], ACT.Copy,
                                           scale=pcol("pool_scale", n, n + 1)).then_inc(self.taken, 1)
                self.att.act()

            def dve(self, dve):
                g0 = self.proj.g0
                for c in range(6):
                    make_rest(g0 + c + 1)
                    if c == 2:
                        dve.wait_ge(const_landed, 16 * self.const)
                    if c >= 3:
                        for t_ in (2 * c - 6, 2 * c - 5):
                            rope_dve(self.r0, t_, t_, self.q, self.rope[:, P:P + SEQ], self.rope[:, P + SEQ:])
                    if c == 2:
                        for n in range(2):
                            dve.wait_ge(self.taken, 3 + n)
                            dve.scalar_tensor_tensor(self.olo[:, n], bank[4 + n][:, 0:SEQ], pcol("pool_scale", n, n + 1),
                                                     self.ohi[:, n].bitcast(F32), ALU.mult, ALU.subtract)\
                                .then_inc(self.done, 2)
                for t_ in (6, 7):
                    rope_dve(self.r0, t_, t_, self.q, self.rope[:, P:P + SEQ], self.rope[:, P + SEQ:])
                self.att.dve()

        mixers[1] = DiffAttention()
        mixers[4] = Neighbourhood()
        mixers[7] = Even()

        def attention_setup_dve(dve):
            lam_init = 0.8 - 0.6
            lv = pcol("lam").rearrange("p (a d) -> p a d", d=HD)
            link(dve, dve.tensor_tensor_reduce(ta[:, 0, 0:HD], lv[:, 0], lv[:, 1], 1.0, 0.0, ALU.mult, ALU.add,
                                               small[:, 1:2]))
            dve.tensor_tensor_reduce(ta[:, 1, 0:HD], lv[:, 2], lv[:, 3], 1.0, 0.0, ALU.mult, ALU.add,
                                     small[:, 2:3]).then_inc(lam_step, 1)
            dve.wait_ge(lam_step, 2)
            link(dve, dve.tensor_tensor(small[:, 3:4], small[:, 7:8], small[:, 6:7], ALU.subtract))
            link(dve, dve.tensor_scalar(minus_lam, small[:, 3:4], -lam_init, None, ALU.add))
            link(dve, dve.tensor_scalar(subln, pcol("subln"), 1.0 - lam_init, None, ALU.mult))
            link(dve, dve.tensor_scalar(minus_sink[:], pcol("sink"), -1.0, None, ALU.mult))

        def attention_setup_act(act):
            act.wait_ge(lam_step, 1)
            act.activation(small[:, 6:8], small[:, 1:3], ACT.Exp).then_inc(lam_step, 1)

        lam_step = sem("lam_step")

        class Odd:

            DVE_TAPS = 2 * CONV_K
            SPANS = [(0, 0, SEQ), (1, P, SEQ), (0, 0, P), (1, 0, SEQ)]
            OFFSETS = [0, SEQ, SEQ + P, 2 * SEQ]

            def __init__(self, s=10):
                put = region()
                self.s = s
                self.gp = put("od_glu_padded", [P, 4, SEQ + CONV_K - 1])
                self.g = put("od_glu", [P, 4, SEQ])
                self.xp = put("od_xbc_padded", [P, 16, SEQ + 3])
                self.x = put("od_xbc", [P, 16, SEQ])
                self.z = put("od_z", [P, KT, SEQ])
                self.sums = put("od_sums", [P, 2, 2, SEQ])
                self.tri = put("od_masks", [P, 2, SEQ])
                self.ohi = put("od_o_high", [P, 12, SEQ], F32R)
                self.olo = put("od_o_rest", [P, 12, SEQ], F32R)
                self.dt = put("od_dt", [P, 6, 2 * 2 * SSM_H])
                self.cols = put("od_decay_columns", [P, 2, 2, SSM_H])
                self.ea = put("od_a", [P, 2 * SSM_H])
                self.xt = place("od_x_tokens", [P, 2, D], F32, offset=u_at)
                self.yz = place("od_y", [P, KT, SEQ], F32, offset=u_at + 2 * D * 4)
                self.seg = place("od_decays", [P, 2, 3 * SEQ], F32, offset=over_ulo)
                self.m = place("od_maps", [P, 2, 3 * SEQ], F32, offset=over_ulo + 6 * SEQ * 4)
                self.base = total["taken"]
                self.proj = Projection(s, f"in{s}", ["f"] * 4 + ["d"] + ["f"] * 12, [SEQ] * 17)
                self.proj.release = self.release
                total["const"] += 2
                self.const = total["const"]
                names = ["pads", "sigmoid", "glu", "pool_tap", "glu_dve", "glu_pool", "conv_first", "dt_exp", "dt_u", "dt_log",
                         "a_exp", "a_ready", "cum_ready", "cum_taken", "conv", "x_done", "turned", "xt_ready",
                         "cb", "rowsum", "seg_ready", "decay", "maps", "y_ps", "y_taken", "ln_sum", "ln_centred",
                         "ln_sq", "ln_var", "ln_root", "ln_scaled", "ln_act", "ln_hi", "ln_lo", "sq", "sq_used",
                         "root", "scaled", "hi", "lo"]
                self.sem = {n: sem("od_" + n) for n in names}

            def release(self, e):
                return (self.sem["glu"], e // 2 + 1) if e < 8 else (proj_taken, self.base + e - 8 + 1)

            def loads(self, sp):
                sp.dma_start(self.sums[:].rearrange("p a b c -> p (a b c)"), t["od_const"][:, 0:4 * SEQ])\
                    .then_inc(const_landed, 16)
                sp.dma_start(self.tri[:].rearrange("p a b -> p (a b)"), t["od_const"][:, 4 * SEQ:])\
                    .then_inc(const_landed, 16)

            def dve_tap(self, dve, j):
                n, k, S = j % 2, j // 2, self.sem
                if j >= self.DVE_TAPS:
                    return
                w, src = pcol("dw_w", n * CONV_K + k, n * CONV_K + k + 1), self.gp[:, n, k:k + SEQ]
                if k == 0:
                    ins = dve.tensor_scalar(self.g[:, n], src, w, pcol("dw_b", n, n + 1), ALU.mult, ALU.add)
                else:
                    dve.wait_ge(S["glu_dve"], j - 1)
                    ins = dve.scalar_tensor_tensor(self.g[:, n], src, w, self.g[:, n], ALU.mult, ALU.add)
                ins.then_inc(S["glu_dve"], 1)

            def pool_tap(self, pool, n, k):
                S = self.sem
                w, src = pcol("dw_w", n * CONV_K + k, n * CONV_K + k + 1), self.gp[:, n, k:k + SEQ]
                count = (n - 2) * CONV_K + k
                if k == 0:
                    pool.tensor_scalar(self.g[:, n], src, w, pcol("dw_b", n, n + 1), ALU.mult, ALU.add)\
                        .then_inc(S["glu_pool"], 1)
                    return
                if count >= 2:
                    pool.wait_ge(S["glu_pool"], count - 1)
                pool.tensor_scalar(tb[:, k % 2, 0:SEQ], src, w, None, ALU.mult).then_inc(S["pool_tap"], 1)
                pool.wait_ge(S["pool_tap"], count - (n - 2))
                pool.wait_ge(S["glu_pool"], count)
                pool.tensor_tensor(self.g[:, n], self.g[:, n], tb[:, k % 2, 0:SEQ], ALU.add)\
                    .then_inc(S["glu_pool"], 1)

            def pool(self, pool):
                S = self.sem
                pool.wait_ge(w_used, self.proj.g0)
                half = CONV_K // 2
                pool.memset(self.gp[:, :, 0:half], 0.0).then_inc(S["pads"], 1)
                pool.memset(self.gp[:, :, half + SEQ:], 0.0).then_inc(S["pads"], 1)
                pool.memset(self.xp[:, :, 0:2], 0.0).then_inc(S["pads"], 1)
                pool.memset(self.xp[:, :, 2 + SEQ:], 0.0).then_inc(S["pads"], 1)
                pool.wait_ge(S["pads"], 4)
                for n in (2, 3):
                    pool.wait_ge(S["glu"], n + 1)
                    for k in range(CONV_K):
                        self.pool_tap(pool, n, k)

            def conv(self, dve, idx):
                S = self.sem
                dve.wait_ge(S["conv_first"], idx + 1)
                for k in range(1, 4):
                    w, src = pcol("cw", idx * 4 + k, idx * 4 + k + 1), self.xp[:, idx, k:k + SEQ]
                    ins = dve.scalar_tensor_tensor(self.x[:, idx], src, w, self.x[:, idx], ALU.mult, ALU.add)
                    if k < 3:
                        link(dve, ins)
                ins.then_inc(S["conv"], 1)

            def act(self, act):
                S, g0 = self.sem, self.proj.g0
                ln_slot = slots(ta, SEQ)[1]

                def silu_x(idx):
                    act.wait_ge(S["conv"], idx + 1)
                    act.activation(self.x[:, idx], self.x[:, idx], ACT.Silu).then_inc(S["x_done"], 1)

                for c in range(17):
                    make_high(g0 + c + 1)
                    if 6 <= c < 14:
                        for idx in (2 * c - 12, 2 * c - 11):
                            act.wait_ge(proj_taken, self.base + 2 + idx + 1)
                            act.activation(self.x[:, idx], self.xp[:, idx, 0:SEQ], ACT.Identity,
                                           scale=pcol("cw", idx * 4, idx * 4 + 1),
                                           bias=pcol("cb", idx, idx + 1)).then_inc(S["conv_first"], 1)
                    if c >= 9:
                        for idx in range(2 * (c - 9), min(2 * (c - 9) + 2, 16)):
                            silu_x(idx)
                    act.wait_ge(w_used, g0 + c + 1)
                    if c < 4:
                        act.activation(ta[:, c % 2, 0:SEQ], bank[(2 * c + 1) % 4][:, 0:SEQ], ACT.Sigmoid)\
                            .then_inc(S["sigmoid"], 1)
                    elif c == 4:
                        for m in range(2):
                            act.activation(self.dt[:, 0, 32 * m:32 * m + 32], bank[m][:, 0:2 * SSM_H], ACT.Copy)\
                                .then_inc(proj_taken, 1)
                    else:
                        for m in range(2):
                            e = self.proj.first[c] + m
                            if c < 13:
                                if e == 10:
                                    act.wait_ge(S["pads"], 4)
                                ins = act.activation(self.xp[:, e - 10, 2:2 + SEQ], bank[e % 4][:, 0:SEQ], ACT.Copy)
                            else:
                                ins = act.activation(self.z[:, e - 26], bank[e % 4][:, 0:SEQ], ACT.Silu)
                            ins.then_inc(proj_taken, 1)
                    if c == 6:
                        act.wait_ge(S["dt_exp"], 1)
                        act.activation(self.dt[:, 1], self.dt[:, 1], ACT.Exp, scale=-1.0).then_inc(S["dt_exp"], 1)
                        act.activation(self.ea[:], pcol("a_log"), ACT.Exp).then_inc(S["a_exp"], 1)
                        act.wait_ge(S["dt_u"], 1)
                        act.activation(self.dt[:, 3], self.dt[:, 2], ACT.Ln).then_inc(S["dt_log"], 1)
                def square_y(kt):
                    act.wait_ge(S["y_taken"], kt + 1)
                    if kt >= 4:
                        act.wait_ge(S["sq_used"], kt - 3)
                    act.activation(slots(sq, SEQ)[1](kt), self.yz[:, kt], ACT.Square).then_inc(S["sq"], 1)

                act.wait_ge(S["cum_ready"], 1)
                act.activation(self.cols[:].rearrange("p a b c -> p (a b c)"), bank[6][:, 0:4 * SSM_H], ACT.Copy)\
                    .then_inc(S["cum_taken"], 1)
                for n in range(4):
                    act.wait_ge(S["turned"], n + 1)
                    act.activation(self.xt[:, n // 2, n % 2 * 512:(n % 2 + 1) * 512], bank[2 + n % 2][:], ACT.Copy)\
                        .then_inc(S["xt_ready"], 1)
                for hh in range(SSM_H):
                    act.wait_ge(S["seg_ready"], hh + 1)
                    act.activation(self.seg[:, hh % 2], self.seg[:, hh % 2], ACT.Exp).then_inc(S["decay"], 1)
                    if hh >= 3 and hh % 2:
                        square_y((hh - 3) // 2)
                    if hh == 9:
                        for n in range(4):
                            act.wait_ge(S["ln_centred"], n + 1)
                            act.activation(ln_slot(n), self.g[:, n], ACT.Square).then_inc(S["ln_sq"], 1)
                    if hh == 12:
                        act.wait_ge(S["ln_var"], 4)
                        act.activation(sd[:, 0:SEQ], bank[2][:, 0:SEQ], ACT.Sqrt, scale=1.0 / 512, bias=eps_col)\
                            .then_inc(S["ln_root"], 1)
                    if hh == 14:
                        for n in range(4):
                            act.wait_ge(S["ln_scaled"], n + 1)
                            act.activation(self.g[:, n], self.g[:, n], ACT.Silu, bias=pcol("ln_b", n, n + 1))\
                                .then_inc(S["ln_act"], 1)
                            act.wait_ge(S["ln_act"], n + 1)
                            act.activation(self.ohi[:, n], self.g[:, n], ACT.Copy).then_inc(S["ln_hi"], 1)
                load_table(ACT.Sqrt)
                square_y(KT - 1)
                act.wait_ge(S["sq_used"], KT)
                act.activation(tb[:, 1, 0:SEQ], bank[3][:, 0:SEQ], ACT.Sqrt, scale=1.0 / D, bias=eps_col)\
                    .then_inc(S["root"], 1)
                for kt in range(KT):
                    act.wait_ge(S["scaled"], kt + 1)
                    act.activation(self.ohi[:, 4 + kt], self.yz[:, kt], ACT.Copy).then_inc(S["hi"], 1)

            def dve(self, dve):
                S, g0 = self.sem, self.proj.g0
                for c in range(17):
                    make_rest(g0 + c + 1)
                    if c < 4:
                        dve.wait_ge(S["pads"], 4)
                        dve.wait_ge(S["sigmoid"], c + 1)
                        dve.tensor_tensor(self.gp[:, c, CONV_K // 2:CONV_K // 2 + SEQ], bank[2 * c % 4][:, 0:SEQ],
                                          ta[:, c % 2, 0:SEQ], ALU.mult).then_inc(S["glu"], 1)
                        if c == 1:
                            dve.wait_ge(S["glu"], 2)
                    else:
                        for j in range(5 * (c - 4), 5 * (c - 3)):
                            self.dve_tap(dve, j)
                    dt = self.dt
                    if c == 5:
                        dve.wait_ge(proj_taken, self.base + 2)
                        for m in range(2):
                            cols = slice(32 * m, 32 * m + 32)
                            ins = dve.tensor_tensor(dt[:, 0, cols], dt[:, 0, cols], pcol("dt_bias"), ALU.add)
                            link(dve, ins)
                        dve.scalar_tensor_tensor(dt[:, 1], dt[:, 0], -1.0, dt[:, 0], ALU.mult, ALU.max)\
                            .then_inc(S["dt_exp"], 1)
                    if c == 6:
                        dve.wait_ge(S["dt_exp"], 2)
                        dve.tensor_scalar(dt[:, 2], dt[:, 1], 1.0, None, ALU.add).then_inc(S["dt_u"], 1)
                        dve.wait_ge(S["dt_u"], 1)
                        link(dve, dve.tensor_scalar(dt[:, 4], dt[:, 2], -1.0, None, ALU.add))
                        link(dve, dve.tensor_tensor(dt[:, 4], dt[:, 1], dt[:, 4], ALU.subtract))
                        link(dve, dve.reciprocal(dt[:, 5], dt[:, 2]))
                        link(dve, dve.tensor_tensor(dt[:, 4], dt[:, 4], dt[:, 5], ALU.mult))
                        dve.wait_ge(S["dt_log"], 1)
                        link(dve, dve.tensor_tensor(dt[:, 4], dt[:, 4], dt[:, 3], ALU.add))
                        link(dve, dve.scalar_tensor_tensor(dt[:, 3], dt[:, 0], 0.0, dt[:, 4], ALU.max, ALU.add))
                        dve.wait_ge(S["a_exp"], 1)
                        for m in range(2):
                            cols = slice(32 * m, 32 * m + 32)
                            dve.scalar_tensor_tensor(dt[:, 5, cols], dt[:, 3, cols], -1.0, self.ea[:], ALU.mult,
                                                     ALU.mult).then_inc(S["a_ready"], 1)
                    if c >= 8:
                        for idx in range(2 * (c - 8), min(2 * (c - 8) + 2, 16)):
                            self.conv(dve, idx)
                dve.wait_ge(const_landed, 16 * self.const)
                dve.wait_ge(S["cum_taken"], 1)
                for hh in range(SSM_H):
                    self.decays(dve, hh)
                    if hh:
                        self.maps(dve, hh - 1)
                    if hh == 8:
                        self.centre(dve)
                    if hh == 13:
                        dve.wait_ge(S["ln_root"], 1)
                        link(dve, dve.reciprocal(sd[:, 0:SEQ], sd[:, 0:SEQ]))
                        for n in range(4):
                            dve.scalar_tensor_tensor(self.g[:, n], self.g[:, n], pcol("ln_g", n, n + 1),
                                                     sd[:, 0:SEQ], ALU.mult, ALU.mult).then_inc(S["ln_scaled"], 1)
                    if hh == 15:
                        for n in range(4):
                            dve.wait_ge(S["ln_hi"], n + 1)
                            dve.tensor_tensor(self.olo[:, n], self.g[:, n], self.ohi[:, n].bitcast(F32),
                                              ALU.subtract).then_inc(S["ln_lo"], 1)
                self.maps(dve, SSM_H - 1)
                dve.wait_ge(S["root"], 1)
                link(dve, dve.reciprocal(tb[:, 1, 0:SEQ], tb[:, 1, 0:SEQ]))

                def rest(kt):
                    dve.wait_ge(S["hi"], kt + 1)
                    dve.tensor_tensor(self.olo[:, 4 + kt], self.yz[:, kt], self.ohi[:, 4 + kt].bitcast(F32),
                                      ALU.subtract).then_inc(S["lo"], 1)

                for kt in range(KT):
                    dve.scalar_tensor_tensor(self.yz[:, kt], self.yz[:, kt], pcol("ssm_norm", kt, kt + 1),
                                             tb[:, 1, 0:SEQ], ALU.mult, ALU.mult).then_inc(S["scaled"], 1)
                    if kt:
                        rest(kt - 1)
                rest(KT - 1)

            def decays(self, dve, hh):
                S = self.sem
                dve.wait_ge(S["rowsum"], hh + 1)
                if hh >= 2:
                    dve.wait_ge(S["maps"], hh - 1)
                ps = bank[6 + hh % 2]
                for (st, a, b), o, way in zip(self.SPANS, self.OFFSETS, (0, 0, 1, 1)):
                    mask = self.tri[:, way, 0:b - a] if way == 0 else self.tri[:, way, SEQ - (b - a):]
                    ins = dve.scalar_tensor_tensor(self.seg[:, hh % 2, o:o + b - a], ps[:, way * SEQ + a:way * SEQ + b],
                                                   self.cols[:, way, st, hh:hh + 1], mask, ALU.subtract, ALU.add)
                ins.then_inc(S["seg_ready"], 1)

            def maps(self, dve, hh):
                S = self.sem
                dve.wait_ge(S["decay"], hh + 1)
                dve.wait_ge(S["cb"], hh // 4 + 1)
                if hh >= 2:
                    dve.wait_ge(S["y_ps"], hh - 1)
                for (st, a, b), o, way in zip(self.SPANS, self.OFFSETS, (0, 0, 1, 1)):
                    dt = self.dt[:, 3, 32 * st + 16 * way + hh:32 * st + 16 * way + hh + 1]
                    ins = dve.scalar_tensor_tensor(self.m[:, hh % 2, o:o + b - a], self.seg[:, hh % 2, o:o + b - a], dt,
                                                   bank[4 + hh // 4 % 2][:, st * SEQ + a:st * SEQ + b], ALU.mult,
                                                   ALU.mult)
                ins.then_inc(S["maps"], 1)
                if hh % 2 == 0 and hh:
                    self.gate(dve, hh // 2 - 1)
                if hh == SSM_H - 1:
                    self.gate(dve, KT - 1)

            def gate(self, dve, kt):
                S = self.sem
                dve.wait_ge(S["y_ps"], 2 * kt + 2)
                link(dve, dve.scalar_tensor_tensor(self.yz[:, kt], self.x[:, 8 + kt], pcol("skip", kt, kt + 1),
                                                   bank[kt % 2][:, 0:SEQ], ALU.mult, ALU.add))
                dve.tensor_tensor(self.yz[:, kt], self.yz[:, kt], self.z[:, kt], ALU.mult).then_inc(S["y_taken"], 1)

            def centre(self, dve):
                S = self.sem
                dve.wait_ge(S["ln_sum"], 1)
                for n in range(4):
                    dve.scalar_tensor_tensor(self.g[:, n], bank[2][:, 0:SEQ], -1.0 / 512, self.g[:, n], ALU.mult,
                                             ALU.add).then_inc(S["ln_centred"], 1)

            def pe(self, pe):
                S = self.sem
                for c in range(17):
                    self.proj.pe_chunk(c, c == 0)
                pe.wait_ge(const_landed, 16 * self.const)
                pe.wait_ge(S["a_ready"], 2)
                a = lambda kt, c0, c1: self.dt[:, 5, 32 * kt + c0:32 * kt + c1]
                for way in range(2):
                    for lt in range(2):
                        o = (2 * way + lt) * SSM_H
                        for kt in range(2):
                            ins = pe.matmul(bank[6][:, o:o + SSM_H], self.sums[:, way, kt, lt * P:(lt + 1) * P],
                                            a(kt, way * SSM_H, (way + 1) * SSM_H), start=kt == 0, stop=kt == 1)
                ins.then_inc(S["cum_ready"], 1)
                pe.wait_ge(S["x_done"], 16)
                pe.wait_ge(proj_taken, self.base + self.proj.n - 8)
                for n in range(4):
                    if n >= 2:
                        pe.wait_ge(S["xt_ready"], n - 1)
                    for k in range(4):
                        ins = pe.transpose(bank[2 + n % 2][:, k * P:(k + 1) * P],
                                           self.x[:, 8 + n % 2 * 4 + k, n // 2 * P:(n // 2 + 1) * P], ident[:])
                    ins.then_inc(S["turned"], 1)
                self.c_dot_b(pe, 0)
                pe.wait_ge(S["cum_taken"], 1)
                self.row_sums(pe, 0, a)
                self.row_sums(pe, 1, a)
                pe.wait_ge(S["xt_ready"], 4)
                for hh in range(SSM_H):
                    if hh + 2 < SSM_H:
                        self.row_sums(pe, hh + 2, a)
                    if hh % 4 == 2 and hh < 12:
                        self.c_dot_b(pe, hh // 4 + 1)
                    if hh == 6:
                        pe.wait_ge(S["glu_dve"], 2 * CONV_K)
                        pe.wait_ge(S["glu_pool"], 2 * CONV_K)
                        for n in range(4):
                            ins = pe.matmul(bank[2][:, 0:SEQ], ones[:], self.g[:, n], start=n == 0, stop=n == 3)
                        ins.then_inc(S["ln_sum"], 1)
                    if hh == 11:
                        for n in range(4):
                            pe.wait_ge(S["ln_sq"], n + 1)
                            pe.matmul(bank[2][:, 0:SEQ], ones[:], slots(ta, SEQ)[1](n), start=n == 0, stop=n == 3)\
                                .then_inc(S["ln_var"], 1)
                    if hh >= 5 and hh % 2:
                        self.sum_y(pe, (hh - 5) // 2)
                    kt, r = hh // 2, heads_in(hh)
                    pe.wait_ge(S["maps"], hh + 1)
                    if kt >= 2 and hh % 2 == 0:
                        pe.wait_ge(S["y_taken"], kt - 1)
                    for n, ((st, a0, b0), o) in enumerate(zip(self.SPANS, self.OFFSETS)):
                        ins = pe.matmul(bank[kt % 2][r, a0:b0], self.xt[:, st, hh * HD:(hh + 1) * HD],
                                        self.m[:, hh % 2, o:o + b0 - a0], start=n == 0, stop=n == 3)
                    ins.then_inc(S["y_ps"], 1)
                for kt in (KT - 2, KT - 1):
                    self.sum_y(pe, kt)

            def sum_y(self, pe, kt):
                S = self.sem
                pe.wait_ge(S["sq"], kt + 1)
                pe.matmul(bank[3][:, 0:SEQ], ones[:], slots(sq, SEQ)[1](kt), start=kt == 0, stop=kt == KT - 1)\
                    .then_inc(S["sq_used"], 1)

            def c_dot_b(self, pe, g):
                S = self.sem
                if g >= 2:
                    pe.wait_ge(S["maps"], 4 * (g - 1))
                for st in range(2):
                    ins = pe.matmul(bank[4 + g % 2][:, st * SEQ:(st + 1) * SEQ], self.x[:, g, st * P:(st + 1) * P],
                                    self.x[:, 4 + g], start=True, stop=True)
                ins.then_inc(S["cb"], 1)

            def row_sums(self, pe, hh, a):
                S = self.sem
                if hh >= 2:
                    pe.wait_ge(S["seg_ready"], hh - 1)
                for way in range(2):
                    for kt in range(2):
                        col_ = a(kt, way * SSM_H + hh, way * SSM_H + hh + 1)
                        ins = pe.matmul(bank[6 + hh % 2][:, way * SEQ:(way + 1) * SEQ], col_.to_broadcast([P, P]),
                                        self.sums[:, way, kt], start=kt == 0, stop=kt == 1)
                ins.then_inc(S["rowsum"], 1)

            def out(self, pe):
                def ready_tile(k):
                    if k < 4:
                        pe.wait_ge(self.sem["ln_lo"], k + 1)
                    else:
                        pe.wait_ge(self.sem["lo"], k - 3)

                out_pe(self.s, lambda k, n: self.ohi[:, k, 0:n], lambda k, n: self.olo[:, k, 0:n],
                       ready_tile=ready_tile)

        mixers[10] = Odd()

        block = ctx.enter_context(nc.Block())

        @block.sync
        def _(sp):
            sp.dma_start(par[:], t["params"]).then_inc(par_landed, 16)
            sp.dma_start(ident[:], t["identity"]).then_inc(par_landed, 16)
            for name, src, row, n, cols in plan:
                g0 = first_chunk[name]
                for j in range(n):
                    load_chunk(sp, name, src, row, g0, j, None)
                    s = {("in1", 5): 1, ("in4", 5): 4, ("in7", 5): 7, ("in10b", 1): 10}.get((name, j))
                    if s in mixers:
                        sp.wait_ge(w_used, first_chunk[f"in{s}"])
                        mixers[s].loads(sp)
                if name == "ada0_0":
                    sp.dma_start(h[:], t["tokens"]).then_inc(in_landed, 16)
            last = subs[-1]
            for kt in range(KT):
                await_h(sp, last, kt)
                sp.dma_start(out[:, kt], h[:, kt, 0:out.shape[2]]).then_inc(out_done, 16)
            sp.wait_ge(out_done, 16 * KT)

        @block.gpsimd
        def _(pool):
            for s in subs:
                pre_pool(s, width_in(s))
                if s in mixers:
                    mixers[s].pool(pool)
                out_pool(s)
                post_pool(s)

        @block.scalar
        def _(act):
            act.wait_ge(par_landed, 32)
            silu_in = pcol("silu_in").rearrange("p (k c) -> p k c", c=2)
            act.wait_ge(const_ready, 3)
            act.activation(cond4[:, 0, :, 0:2], silu_in, ACT.Silu).then_inc(cond_ready, 1)
            act.activation(cond4[:, 1, :, 2:4], silu_in, ACT.Silu).then_inc(cond_ready, 1)
            attention_setup_act(act)
            act.wait_ge(in_landed, 16)
            mod_copy(0, 0)
            norm_act(0, 0, BOTH)
            mod_copy(0, 1)
            make_high(first_chunk["in0"])
            mod_copy(0, 2)
            pre_act(0, BOTH)
            for s in subs:
                if s in mixers:
                    mixers[s].act(act)
                else:
                    ffn_in_act(s)
                out_act(s)
                if s != subs[-1]:
                    if not behind(s):
                        make_high(first_chunk[f"in{s + 1}"] + 1, ahead=True)
                    norm_act(s + 1, round_h(s), width_in(s + 1))
                    if behind(s):
                        mod_copy(*behind(s)[0])
                        make_high(first_chunk[f"in{s + 1}"])
                        mod_copy(*behind(s)[1])
                    pre_act(s + 1, width_in(s + 1))

        @block.vector
        def _(dve):
            dve.memset(small[:, 0:1], EPS).then_inc(const_ready, 1)
            dve.memset(cond4[:], 0.0).then_inc(const_ready, 1)
            dve.memset(ones[:], 1.0).then_inc(const_ready, 1)
            dve.wait_ge(par_landed, 32)
            for s in range(6, 12):
                for c in range(2):
                    ins = dve.tensor_scalar(G[:, s, :, c],
                                            pcol("gain2", (2 * (s - 6) + 1) * KT, (2 * (s - 6) + 2) * KT),
                                            1.0 if s % 3 == 1 else 0.5, None, ALU.mult)
            link(dve, ins)
            attention_setup_dve(dve)
            take_mod(0, 0)
            invert(0, BOTH)
            take_mod(0, 1)
            make_rest(first_chunk["in0"])
            await_mod(dve, 0, 1)
            pre_dve(0, BOTH)
            take_mod(0, 2)
            for s in subs:
                if s in mixers:
                    mixers[s].dve(dve)
                else:
                    ffn_in_dve(s)
                out_dve(s)
                if s < 6:
                    await_mod(dve, s, 2)
                post_dve(s)
                if s == subs[-1]:
                    continue
                groups = behind(s)
                if not groups:
                    make_rest(first_chunk[f"in{s + 1}"] + 1, ahead=True)
                invert(round_h(s), width_in(s + 1))
                if groups:
                    take_mod(*groups[0])
                    make_rest(first_chunk[f"in{s + 1}"])
                if s == 0:
                    take_mod(*groups[1])
                if s < 5:
                    await_mod(dve, s + 1, 1)
                pre_dve(s + 1, width_in(s + 1))
                if s and groups:
                    take_mod(*groups[1])

        @block.tensor
        def _(pe):
            pe.wait_ge(const_ready, 3)
            pe.wait_ge(par_landed, 32)
            pe.wait_ge(cond_ready, 2)
            mod_products(0, 0)
            mod_turn(0, 0)
            mod_products(0, 1)
            pre_pe(0, BOTH)
            mod_turn(0, 1)
            mod_products(0, 2)
            mod_turn(0, 2)
            for s in subs:
                if s in mixers:
                    mixers[s].pe(pe)
                    mixers[s].out(pe)
                else:
                    ffn_in_pe(s)
                    ffn_out_pe(s)
                groups = behind(s)
                if groups:
                    mod_products(*groups[0], range(2))
                elif s != subs[-1]:
                    keep_warm(WARM[0])
                if s != subs[-1]:
                    pre_pe(round_h(s), width_in(s + 1))
                    if not groups:
                        keep_warm(WARM[1])
                if groups:
                    mod_products(*groups[0], range(2, 4))
                    mod_turn(*groups[0])
                    mod_products(*groups[1])
                    mod_turn(*groups[1])


def chunks_of(w, n=CHUNK):
    k, cols = w.shape
    return w.reshape(k // P, P, cols // n, n).transpose(2, 1, 0, 3).reshape(cols // n, P, k // P * n)


def ffn_in_chunks(a, b):
    both = np.stack([a.reshape(KT, P, FT, P), b.reshape(KT, P, FT, P)], axis=3)
    return both.transpose(2, 1, 0, 3, 4).reshape(FT, P, CHUNK_COLS)


def ffn_out_chunks(w):
    return w.reshape(2, HALF_FT, P, KT, P).transpose(3, 0, 2, 1, 4).reshape(2 * KT, P, OUT_COLS)


def col(v):
    return np.ascontiguousarray(v.reshape(-1, P).T)


def twice(v):
    return np.repeat(v, 2, axis=1)


def rows(v):
    return np.broadcast_to(v.reshape(1, -1), (P, v.size))


def toeplitz_bias(rpb):
    pad = np.zeros((NA_H, rpb.shape[1], 2 * GRID_W), rpb.dtype)
    lead = GRID_W - NA_WIN
    pad[:, :, lead:lead + rpb.shape[2]] = rpb
    row, qc, kc = np.arange(4), np.arange(GRID_W), np.arange(GRID_W)
    off_r = row[None, :] - row[:, None] + 7
    off_c = kc[None, :] - qc[:, None] + GRID_W - 1
    b = pad[:, off_r[:, None, :, None], off_c[None, :, None, :]]
    return b.reshape(NA_H, 2, P, SEQ).transpose(2, 0, 1, 3).reshape(P, NA_H * 2 * SEQ)


def constants():
    p = np.arange(P)
    t_ = np.arange(SEQ)
    d = p % HD
    freq = (np.float32(10000.0) ** (-np.arange(16, dtype=np.float32) / np.float32(16))).astype(np.float32)
    pos = np.stack([t_ // GRID_W, t_ % GRID_W]).astype(np.float32)
    ang1 = pos[d // 32] * freq[d % 16][:, None]
    rot1 = np.zeros((P, P), np.float32)
    for i in p:
        if i % 32 < 16:
            rot1[i + 16, i] = -1.0
        else:
            rot1[i - 16, i] = 1.0
    inv = (np.float32(1.0) / (np.float32(10000.0) ** (np.arange(0, HD, 2, dtype=np.float32) / np.float32(HD))))
    ang2 = t_.astype(np.float32)[None, :] * inv.astype(np.float32)[d % 32][:, None]
    rot2 = np.zeros((P, P), np.float32)
    for i in p:
        if i % HD < 32:
            rot2[i + 32, i] = -1.0
        else:
            rot2[i - 32, i] = 1.0
    qc, kc = p % GRID_W, t_ % GRID_W
    start = np.clip(qc - NA_WIN // 2, 0, GRID_W - NA_WIN)
    near = (kc[None] >= start[:, None]) & (kc[None] < start[:, None] + NA_WIN)
    na_mask = np.where(near, 0.0, NEG).astype(np.float32)
    q = np.arange(SEQ)
    ev = np.where(np.abs(q[:, None] - t_[None]) <= 128, 0.0, FAR).astype(np.float32)
    ev_mask = ev.reshape(2, P, SEQ).transpose(1, 0, 2)
    pool = []
    for w in (2, 4, 8, 16):
        lo, hi = np.clip(t_ - w // 2, 0, SEQ), np.clip(t_ + w - w // 2, 0, SEQ)
        inside = (t_[:, None] >= lo[None]) & (t_[:, None] < hi[None])
        pool.append(inside / (hi - lo)[None].astype(np.float32) - np.eye(SEQ))
    pool = np.stack(pool).astype(np.float32).reshape(4, 2, P, SEQ).transpose(2, 0, 1, 3)
    le = (t_[:, None] <= t_[None]).astype(np.float32)
    sums = np.stack([le, le.T]).reshape(2, 2, P, SEQ).transpose(2, 0, 1, 3)
    whole = np.zeros((P, P))
    tri = np.stack([np.concatenate([np.where(p[:, None] <= p[None], 0.0, FAR), whole], axis=1),
                    np.concatenate([whole, np.where(p[:, None] >= p[None], 0.0, FAR)], axis=1)])
    tri = tri.astype(np.float32).transpose(1, 0, 2)
    f = np.float32
    return {
        "identity": np.eye(P, dtype=f),
        "rope1": np.concatenate([rot1, np.cos(ang1).astype(f), np.sin(ang1).astype(f)], axis=1),
        "rope2": np.concatenate([rot2, np.cos(ang2).astype(f), np.sin(ang2).astype(f)], axis=1),
        "na_mask": na_mask,
        "ev_const": np.concatenate([ev_mask.reshape(P, -1), pool.reshape(P, -1)], axis=1),
        "od_const": np.concatenate([sums.reshape(P, -1), tri.reshape(P, -1)], axis=1),
    }


def kernel(**inputs):
    import concourse.bacc as bacc
    from concourse.bass_utils import run_bass_kernel_spmd

    v = {k: np.asarray(a) for k, a in inputs.items()}
    f = np.float32
    cat = np.concatenate
    hd = np.arange(HD)
    q_cols = cat([h * HD + hd for h in EV_HEADS])
    ev_in, ev_out = v["ev_w_in_2"][0], v["ev_w_out_2"][0]
    od_in = v["od_w_in_2"][0]
    glu = cat([od_in[:, c * 512 + n * P:c * 512 + (n + 1) * P] for n in range(4) for c in range(2)], axis=1)
    layers = [(0, 0), (0, 1), (1, 0), (1, 1)]
    ada = v["ada_w"]
    arrays = {
        "tokens": np.ascontiguousarray(cat([v["x"][0], v["ctx"][0]]).T.reshape(KT, P, BOTH).transpose(1, 0, 2)),
        "w_ada": cat([chunks_of(ada[0]), chunks_of(ada[1])]),
        "w_ffn_in": cat([ffn_in_chunks(v["ffn_w_in"][a, b][:, :DFF], v["ffn_w_in"][a, b][:, DFF:]) for a, b in layers]
                        + [ffn_in_chunks(v["ffn_w_gate_2"][a, b], v["ffn_w_up_2"][a, b]) for a, b in layers]),
        "w_ffn_out": cat([ffn_out_chunks(v["ffn_w_out"][a, b]) for a, b in layers]
                         + [ffn_out_chunks(v["ffn_w_down_2"][a, b]) for a, b in layers]),
        "w_mix": cat([chunks_of(w) for w in (
            v["da_w_in"][0], v["da_w_out"][0], v["na_w_in"][0], v["na_w_out"][0],
            ev_in[:, :256], ev_in[:, 1280:1536], ev_in[:, 256:1024][:, q_cols], ev_in[:, 1024:1280],
            cat([ev_out[:256], ev_out[256:][q_cols]]),
            glu, od_in[:, 3072:4096], od_in[:, 2048:3072], od_in[:, 1024:2048])]),
        "w_dt": chunks_of(od_in[:, 4096:4128], 2 * SSM_H),
        "w_od_out": chunks_of(v["od_w_out_2"][0], P),
        "na_bias": toeplitz_bias(v["na_rpb"][0]),
        "pool_w": np.ascontiguousarray(v["ev_pool_w_2"][0].reshape(2, P, HD).transpose(1, 0, 2).reshape(P, 2 * HD)),
    }
    parts = {
        "silu_in": np.stack([col(v["c"][0]), col(v["c_ctx"])], axis=2).reshape(P, -1),
        "gain": twice(col(v["norm_g"])),
        "gain2": col(v["norm_w_2"]),
        "ada_b": twice(col(v["ada_b"])),
        "lam": rows(v["da_lambda"][0]),
        "subln": col(v["da_subln_g"][0]),
        "sink": rows(v["ev_sink_2"][0][EV_HEADS]),
        "pool_scale": col(v["ev_pool_scale_2"][0]),
        "dw_w": v["cv_dw_w_2"][0].reshape(CONV_K, 4, P).transpose(2, 1, 0).reshape(P, -1),
        "dw_b": col(v["cv_dw_b_2"][0]),
        "ln_g": col(v["cv_ln_g_2"][0]),
        "ln_b": col(v["cv_ln_b_2"][0]),
        "cw": np.roll(v["ssm_conv_w_2"][0].reshape(4, 16, P), 8, axis=1).transpose(2, 1, 0).reshape(P, -1),
        "cb": np.roll(col(v["ssm_conv_b_2"][0]), 8, axis=1),
        "a_log": rows(v["ssm_A_log_2"][0]),
        "dt_bias": rows(v["ssm_dt_bias_2"][0]),
        "skip": np.repeat(v["ssm_D_2"][0].reshape(KT, 2), HD, axis=1).T,
        "ssm_norm": col(v["ssm_norm_w_2"][0]),
    }
    columns, n_columns = param_columns()
    params = np.zeros((P, n_columns), f)
    for name, (o, n) in columns.items():
        params[:, o:o + n] = parts[name]
    arrays["params"] = params
    arrays.update(constants())
    arrays = {name: np.ascontiguousarray(a) for name, a in arrays.items()}

    nc = bacc.Bacc("TRN2", target_bir_lowering=False, num_devices=1, dynamic_dma_scratch_size=1024)
    t = {name: nc.dram_tensor(f"in_{name}", a.shape, mybir.dt.from_np(a.dtype), kind="ExternalInput").ap()
         for name, a in arrays.items()}
    out = nc.dram_tensor("out_x", (P, KT, SEQ), F32, kind="ExternalOutput").ap()
    build_program(nc, t, out)
    r = run_bass_kernel_spmd(nc, [{f"in_{name}": a for name, a in arrays.items()}], core_ids=[0])
    got = r.results[0]["out_x"]
    return got.transpose(2, 1, 0).reshape(1, SEQ, D)
```
